# Optimizing a Trainium2 kernel written in Bass

```python
import math
import jax, jax.numpy as jnp
from jax import lax
import numpy as np

D_MODEL = 2048
BATCH = 1
SEQ = 256
DEPTH = 1
DEC_BATCH = 8
DEC_SEQ = 1
PAST_LEN = 2048
PAGE_SIZE = 128

N_META = 16
S5_WIDTH = D_MODEL // 2
S5_GROUP_CH = 16
S5_GROUPS = S5_WIDTH // S5_GROUP_CH
S5_STATE = 64
HG_WIDTH = D_MODEL - S5_WIDTH
HG_HEAD_DIM = 128
HG_HEADS = HG_WIDTH // HG_HEAD_DIM
HG_CHUNK = 64
IN_WIDTH = S5_WIDTH + 4 * HG_WIDTH
N_EXPERT_GROUPS = 4
EXPERTS_PER_GROUP = 8
N_EXPERTS = N_EXPERT_GROUPS * EXPERTS_PER_GROUP
EXPERT_TOP_K = 2
EXPERT_HIDDEN = D_MODEL // 4
EPS = 1e-6

kernel_name = "hymba_s5_hgrn2_hmoe_step"

def _rmsnorm(x, gain):
    xf = x.astype(jnp.float32)
    y = xf * lax.rsqrt(jnp.mean(xf * xf, axis=-1, keepdims=True) + EPS)
    return (y * gain.astype(jnp.float32)).astype(x.dtype)

def _s5_combine(e1, e2):
    a1r, a1i, b1r, b1i = e1
    a2r, a2i, b2r, b2i = e2
    return (a2r * a1r - a2i * a1i,
            a2r * a1i + a2i * a1r,
            a2r * b1r - a2i * b1i + b2r,
            a2r * b1i + a2i * b1r + b2i)

def _s5(u, h0_re, h0_im, A_re, A_im, log_step, B_re, B_im, C_re, C_im, D_skip):
    b, t, _ = u.shape
    f32 = jnp.float32
    uf = u.astype(f32)
    A_re = A_re.astype(f32); A_im = A_im.astype(f32)
    step = jnp.exp(log_step.astype(f32))[:, None]
    mag = jnp.exp(step * A_re)
    Ab_re = mag * jnp.cos(step * A_im)
    Ab_im = mag * jnp.sin(step * A_im)
    den = A_re * A_re + A_im * A_im
    nr = Ab_re - 1.0
    fr = (nr * A_re + Ab_im * A_im) / den
    fi = (Ab_im * A_re - nr * A_im) / den
    B_re = B_re.astype(f32); B_im = B_im.astype(f32)
    Bb_re = fr[..., None] * B_re - fi[..., None] * B_im
    Bb_im = fr[..., None] * B_im + fi[..., None] * B_re
    ug = uf.reshape(b, t, S5_GROUPS, S5_GROUP_CH)
    bu_re = jnp.einsum('gpc,btgc->btgp', Bb_re, ug)
    bu_im = jnp.einsum('gpc,btgc->btgp', Bb_im, ug)
    h0_re = h0_re.astype(f32); h0_im = h0_im.astype(f32)
    bu_re = bu_re.at[:, 0].add(Ab_re * h0_re - Ab_im * h0_im)
    bu_im = bu_im.at[:, 0].add(Ab_re * h0_im + Ab_im * h0_re)
    a_re = jnp.broadcast_to(Ab_re, bu_re.shape)
    a_im = jnp.broadcast_to(Ab_im, bu_im.shape)
    _, _, h_re, h_im = lax.associative_scan(_s5_combine, (a_re, a_im, bu_re, bu_im), axis=1)
    y = (jnp.einsum('gcp,btgp->btgc', C_re.astype(f32), h_re)
         - jnp.einsum('gcp,btgp->btgc', C_im.astype(f32), h_im))
    y = y.reshape(b, t, S5_WIDTH) + D_skip.astype(f32) * uf
    return y, h_re[:, -1], h_im[:, -1]

def _hgrn_scan(q, k, v, logf, S0, chunk):
    b, h, t, _ = q.shape
    dv = v.shape[-1]
    n = t // chunk

    def blocks(a):
        return jnp.moveaxis(a.reshape(b, h, n, chunk, a.shape[-1]), 2, 0)

    causal = jnp.tril(jnp.ones((chunk, chunk), dtype=bool))[:, :, None]

    def step(S, blk):
        qc, kc, vc, gc = blk
        G = jnp.cumsum(gc, axis=2)
        diff = G[:, :, :, None, :] - G[:, :, None, :, :]
        decay = jnp.exp(jnp.where(causal, diff, -jnp.inf))
        att = jnp.einsum('bhtk,bhtsk,bhsk->bhts', qc, decay, kc)
        G_last = G[:, :, -1:, :]
        o = (jnp.einsum('bhts,bhsv->bhtv', att, vc)
             + jnp.einsum('bhtk,bhkv->bhtv', qc * jnp.exp(G), S))
        S_new = (jnp.exp(G_last[:, :, 0, :])[..., None] * S
                 + jnp.einsum('bhsk,bhsv->bhkv', kc * jnp.exp(G_last - G), vc))
        return S_new, o

    S_fin, o = lax.scan(step, S0, (blocks(q), blocks(k), blocks(v), blocks(logf)))
    o = jnp.moveaxis(o, 0, 2).reshape(b, h, t, dv)
    return o, S_fin

def _hgrn2(q, f_raw, i_in, g, lb, S0, out_gain, segments):
    b, t, _ = q.shape
    f32 = jnp.float32
    f = lb + (1.0 - lb) * jax.nn.sigmoid(f_raw.astype(f32))
    logf = jnp.log(f)
    k = 1.0 - f

    def heads(a):
        return a.reshape(b, t, HG_HEADS, -1).transpose(0, 2, 1, 3)

    qh = heads(q.astype(f32) * (HG_HEAD_DIM ** -0.5))
    kh = heads(k); vh = heads(i_in.astype(f32)); gh = heads(logf)
    S = S0.astype(f32)
    outs = []
    start = 0
    for length, chunk in segments:
        sl = slice(start, start + length)
        o, S = _hgrn_scan(qh[:, :, sl], kh[:, :, sl], vh[:, :, sl], gh[:, :, sl], S, chunk)
        outs.append(o)
        start += length
    o = jnp.concatenate(outs, axis=2).transpose(0, 2, 1, 3)
    o = o * lax.rsqrt(jnp.mean(o * o, axis=-1, keepdims=True) + EPS)
    o = o * out_gain.astype(f32).reshape(HG_HEADS, HG_HEAD_DIM)
    o = o.reshape(b, t, HG_WIDTH) * jax.nn.silu(g.astype(f32))
    return o.astype(q.dtype), S

def _hier_moe(x, w_coarse, b_coarse, w_fine, b_fine, w_gate, w_up, w_down):
    b, t, d = x.shape
    n = b * t
    xs = x.reshape(n, d)
    f32 = jnp.float32
    p_grp = jax.nn.softmax((xs @ w_coarse + b_coarse).astype(f32), axis=-1)
    pg, grp = lax.top_k(p_grp, 1)
    fl = (xs @ w_fine + b_fine).astype(f32).reshape(n, N_EXPERT_GROUPS, EXPERTS_PER_GROUP)
    fl_sel = jnp.take_along_axis(fl, grp[:, :, None], axis=1)[:, 0]
    wt, idx = lax.top_k(jax.nn.softmax(fl_sel, axis=-1), EXPERT_TOP_K)
    wt = wt / jnp.sum(wt, axis=-1, keepdims=True) * pg
    eidx = grp * EXPERTS_PER_GROUP + idx
    gate = jnp.zeros((n, N_EXPERTS), f32).at[jnp.arange(n)[:, None], eidx].add(wt)
    hg = jnp.einsum('nd,edf->nef', xs, w_gate)
    hu = jnp.einsum('nd,edf->nef', xs, w_up)
    act = jax.nn.silu(hg) * hu * gate.astype(x.dtype)[:, :, None]
    out = jnp.einsum('nef,efd->nd', act, w_down)
    return out.reshape(b, t, d).astype(x.dtype)

def _layer(x, s5_h_re, s5_h_im, hg_S, lb, p, segments):
    xn = _rmsnorm(x, p['norm_mix'])
    z = xn @ p['w_in']
    o1 = S5_WIDTH
    u = z[..., :o1]
    q = z[..., o1:o1 + HG_WIDTH]
    f_raw = z[..., o1 + HG_WIDTH:o1 + 2 * HG_WIDTH]
    i_in = z[..., o1 + 2 * HG_WIDTH:o1 + 3 * HG_WIDTH]
    g = z[..., o1 + 3 * HG_WIDTH:]
    y_s5, s5_re, s5_im = _s5(u, s5_h_re, s5_h_im, p['A_re'], p['A_im'], p['log_step'],
                             p['B_re'], p['B_im'], p['C_re'], p['C_im'], p['D'])
    y_s5 = jax.nn.gelu(y_s5)
    y_s5 = y_s5 * jax.nn.sigmoid(y_s5 @ p['w_glu'].astype(jnp.float32) + p['b_glu'].astype(jnp.float32))
    y_s5 = _rmsnorm(y_s5.astype(x.dtype), p['s5_gain'])
    y_hg, S_new = _hgrn2(q, f_raw, i_in, g, lb, hg_S, p['hg_gain'], segments)
    x = x + jnp.concatenate([y_s5, y_hg], axis=-1) @ p['w_out']
    x = x + _hier_moe(_rmsnorm(x, p['norm_ffn']), p['w_coarse'], p['b_coarse'], p['w_fine'],
                      p['b_fine'], p['w_gate'], p['w_up'], p['w_down'])
    return x, s5_re, s5_im, S_new

def setup_inputs(seed: int = 0) -> dict:
    key = jax.random.key(seed)
    ks = jax.random.split(key, 32)
    f32 = jnp.float32
    nrm = lambda k, s, sc: jax.random.normal(k, s, f32) * sc
    L, G, P, C = DEPTH, S5_GROUPS, S5_STATE, S5_GROUP_CH
    A_im0 = jnp.arange(P, dtype=f32) * math.pi
    return {
        "x_prompt": nrm(ks[0], (BATCH, SEQ, D_MODEL), 1.0),
        "x_sample": nrm(ks[1], (DEC_BATCH, DEC_SEQ, D_MODEL), 1.0),
        "state_s5_re": nrm(ks[2], (L, DEC_BATCH, G, P), 0.1),
        "state_s5_im": nrm(ks[3], (L, DEC_BATCH, G, P), 0.1),
        "state_hgrn": nrm(ks[4], (L, DEC_BATCH, HG_HEADS, HG_HEAD_DIM, HG_HEAD_DIM), 0.3),
        "meta_tokens": nrm(ks[5], (N_META, D_MODEL), 1.0),
        "norm_mix": 1.0 + nrm(ks[6], (L, D_MODEL), 0.02),
        "w_in": nrm(ks[7], (L, D_MODEL, IN_WIDTH), D_MODEL ** -0.5),
        "s5_A_re": -0.5 + nrm(ks[8], (L, G, P), 0.01),
        "s5_A_im": A_im0 + nrm(ks[9], (L, G, P), 0.01),
        "s5_log_step": jax.random.uniform(ks[10], (L, G), f32, math.log(1e-3), math.log(1e-1)),
        "s5_B_re": nrm(ks[11], (L, G, P, C), (2 * C) ** -0.5),
        "s5_B_im": nrm(ks[12], (L, G, P, C), (2 * C) ** -0.5),
        "s5_C_re": nrm(ks[13], (L, G, C, P), (2 * P) ** -0.5),
        "s5_C_im": nrm(ks[14], (L, G, C, P), (2 * P) ** -0.5),
        "s5_D": nrm(ks[15], (L, S5_WIDTH), 1.0),
        "s5_w_glu": nrm(ks[16], (L, S5_WIDTH, S5_WIDTH), S5_WIDTH ** -0.5),
        "s5_b_glu": nrm(ks[17], (L, S5_WIDTH), 0.01),
        "s5_out_gain": 1.0 + nrm(ks[18], (L, S5_WIDTH), 0.02),
        "hg_lb_logits": nrm(ks[19], (L + 1, HG_WIDTH), 0.1),
        "hg_out_gain": 1.0 + nrm(ks[20], (L, HG_WIDTH), 0.02),
        "w_out": nrm(ks[21], (L, D_MODEL, D_MODEL), D_MODEL ** -0.5),
        "norm_ffn": 1.0 + nrm(ks[22], (L, D_MODEL), 0.02),
        "w_coarse": nrm(ks[23], (L, D_MODEL, N_EXPERT_GROUPS), D_MODEL ** -0.5),
        "b_coarse": nrm(ks[24], (L, N_EXPERT_GROUPS), 0.01),
        "w_fine": nrm(ks[25], (L, D_MODEL, N_EXPERTS), D_MODEL ** -0.5),
        "b_fine": nrm(ks[26], (L, N_EXPERTS), 0.01),
        "w_gate": nrm(ks[27], (L, N_EXPERTS, D_MODEL, EXPERT_HIDDEN), D_MODEL ** -0.5),
        "w_up": nrm(ks[28], (L, N_EXPERTS, D_MODEL, EXPERT_HIDDEN), D_MODEL ** -0.5),
        "w_down": nrm(ks[29], (L, N_EXPERTS, EXPERT_HIDDEN, D_MODEL), EXPERT_HIDDEN ** -0.5),
        "norm_final": 1.0 + nrm(ks[30], (D_MODEL,), 0.02),
    }

def reference(x_prompt, x_sample, state_s5_re, state_s5_im, state_hgrn, meta_tokens,
              norm_mix, w_in, s5_A_re, s5_A_im, s5_log_step, s5_B_re, s5_B_im, s5_C_re,
              s5_C_im, s5_D, s5_w_glu, s5_b_glu, s5_out_gain, hg_lb_logits, hg_out_gain,
              w_out, norm_ffn, w_coarse, b_coarse, w_fine, b_fine, w_gate, w_up, w_down,
              norm_final):
    b = x_prompt.shape[0]
    seq = x_prompt.shape[1]
    dec_seq = x_sample.shape[1]
    hp = jnp.concatenate([jnp.broadcast_to(meta_tokens.astype(x_prompt.dtype)[None],
                                           (b, N_META, D_MODEL)), x_prompt], axis=1)
    hs = x_sample
    lbs = jnp.cumsum(jax.nn.softmax(hg_lb_logits.astype(jnp.float32), axis=0), axis=0)
    seg_prompt = ((N_META, N_META), (seq, HG_CHUNK))
    seg_sample = ((dec_seq, dec_seq),)
    z_s5 = jnp.zeros((b, S5_GROUPS, S5_STATE), jnp.float32)
    z_hg = jnp.zeros((b, HG_HEADS, HG_HEAD_DIM, HG_HEAD_DIM), jnp.float32)
    p_re, p_im, p_hg, s_re, s_im, s_hg = [], [], [], [], [], []
    for l in range(DEPTH):
        p = dict(norm_mix=norm_mix[l], w_in=w_in[l], A_re=s5_A_re[l], A_im=s5_A_im[l],
                 log_step=s5_log_step[l], B_re=s5_B_re[l], B_im=s5_B_im[l], C_re=s5_C_re[l],
                 C_im=s5_C_im[l], D=s5_D[l], w_glu=s5_w_glu[l], b_glu=s5_b_glu[l],
                 s5_gain=s5_out_gain[l], hg_gain=hg_out_gain[l], w_out=w_out[l],
                 norm_ffn=norm_ffn[l], w_coarse=w_coarse[l], b_coarse=b_coarse[l],
                 w_fine=w_fine[l], b_fine=b_fine[l], w_gate=w_gate[l], w_up=w_up[l],
                 w_down=w_down[l])
        hp, r1, i1, g1 = _layer(hp, z_s5, z_s5, z_hg, lbs[l], p, seg_prompt)
        hs, r2, i2, g2 = _layer(hs, state_s5_re[l], state_s5_im[l], state_hgrn[l], lbs[l], p, seg_sample)
        p_re.append(r1); p_im.append(i1); p_hg.append(g1)
        s_re.append(r2); s_im.append(i2); s_hg.append(g2)
    y_prompt = _rmsnorm(hp, norm_final)[:, N_META:]
    y_sample = _rmsnorm(hs, norm_final)
    pdt = x_prompt.dtype
    sdt = state_s5_re.dtype
    s5_re_prompt = jnp.stack(p_re).astype(pdt)
    s5_im_prompt = jnp.stack(p_im).astype(pdt)
    hgrn_prompt = jnp.stack(p_hg).astype(pdt)
    s5_re_sample = jnp.stack(s_re).astype(sdt)
    s5_im_sample = jnp.stack(s_im).astype(sdt)
    hgrn_sample = jnp.stack(s_hg).astype(state_hgrn.dtype)
    return (y_prompt, y_sample, s5_re_prompt, s5_im_prompt, hgrn_prompt, s5_re_sample, s5_im_sample, hgrn_sample)


_drawn_inputs = setup_inputs


def setup_inputs(seed=0):
    import zlib

    import numpy as np

    out = dict(_drawn_inputs(seed))
    spreads = {}
    factors = {'s5_A_re': 15.696,
     's5_b_glu': 7.968,
     's5_out_gain': 10.613,
     'hg_out_gain': 14.936,
     'b_coarse': 32.84,
     'b_fine': 14.367,
     'norm_final': 7.571,
     'norm_ffn': 5.286}
    for name, (base, spread) in spreads.items():
        noise = np.random.default_rng([zlib.crc32(name.encode()), seed]).standard_normal(out[name].shape)
        drawn = base * np.exp(spread * noise) if base else spread * noise
        out[name] = __import__('jax').numpy.asarray(drawn.astype(out[name].dtype))
    for name, factor in factors.items():
        out[name] = (out[name] * factor).astype(out[name].dtype)
    return out
```

```python
import math
from contextlib import ExitStack

import concourse.bass as bass
from concourse import mybir

F32 = mybir.dt.float32
I32 = mybir.dt.int32
U32 = mybir.dt.uint32
U8 = mybir.dt.uint8
ALU = mybir.AluOpType
ACT = mybir.ActivationFunctionType
AX = mybir.AxisListType

P = 128
EPS = 1e-6
MAGIC = 1.5 * 2.0 ** 23
TWO_PI_HI = 6.28125
TWO_PI_LO = 2 * math.pi - TWO_PI_HI
PI_BELOW = 3.1415925
BIG = 1024.0
LOWEST = -3.0e38


class Chain:

    def __init__(self, eng, sem):
        self.eng, self.sem, self.n = eng, sem, 0

    def add(self, ins):
        ins.then_inc(self.sem, 1)
        self.n += 1

    def settle(self):
        self.eng.wait_ge(self.sem, self.n)

    def link(self, ins):
        self.add(ins)
        self.settle()


def hymba_step(nc, t):
    SEQ, D = t["x_prompt"].shape[1:]
    NS = t["x_sample"].shape[0]
    NM = t["meta_tokens"].shape[0]
    TP = NM + SEQ
    T = TP + NS
    TT = [P, P, T - 2 * P]
    KD = D // P
    G5, P5, C5 = t["s5_B_re"].shape[1:]
    W5 = G5 * C5
    N5 = W5 // P
    NJ = G5 * P5 // P
    HG = t["hg_out_gain"].shape[1]
    NH = HG // P
    NE, _, FH = t["w_gate"].shape[1:]
    NG = t["w_coarse"].shape[2]
    EG = NE // NG
    KF = FH // P
    CB = 256
    CAP = 64
    ROUNDS = -(-T // CAP)
    LAST = TP - 2 * P
    assert D == 2 * W5 == 2 * HG and NE % 2 == 0 and T <= 3 * P and NS == NH and TT[2] == LAST + NS

    ctx = ExitStack()
    with ctx:
        def sb(name, shape, dt=F32):
            return ctx.enter_context(nc.sbuf_tensor(name, shape, dt))

        def sem(name):
            return ctx.enter_context(nc.semaphore(name))

        SLOT = KD * CB
        ring = sb("ring", [P, 6, SLOT])
        AR_N = 5 * N5 * T + KD * T + 2 * 33 * NJ + 8536
        arena = sb("arena", [P, AR_N])
        ident = sb("ident", [P, P])
        ones = sb("ones", [P, P])
        upper = sb("upper", [P, P])
        vecs = sb("vecs", [P, 80])
        sc5 = sb("sc5", [P, 6, NJ])
        masks = sb("masks", [P, 8, P], U8)
        eps_col = sb("eps_col", [P, 1])
        token_stats = sb("token_stats", [P, 8])
        lb, one_minus_lb, lb_tmp = sb("lb", [P, NH]), sb("one_minus_lb", [P, NH]), sb("lb_tmp", [P, 3, NH])
        parity = sb("parity", [P, 3])
        fs, ks, qs = (sb(n, [P, NH, NS]) for n in ("f_samples", "k_samples", "q_samples"))
        chunk_decay = [sb(f"chunk_decay{i}", [P, 2]) for i in range(2)]

        class Carver:
            def __init__(self, base, at):
                self.base, self.at = base, at

            def __call__(self, *shape):
                n = math.prod(shape)
                v = self.base[:, self.at:self.at + n]
                self.at += n
                if len(shape) > 1:
                    names = "abcd"[:len(shape)]
                    v = v.rearrange(f"p ({' '.join(names)}) -> p {' '.join(names)}",
                                    **{n_: s for n_, s in zip(names, shape)})
                return v

        upair = ring[:, 4:6, :].rearrange("p a n -> p (a n)")

        c = Carver(arena, 0)
        uT, gT = c(N5, T), c(NH, T)
        gT_at, x1_at = N5 * T, c.at
        qT, GT, kT = c(NH, T), c(NH, T), c(NH, T)
        xnT_at = c.at
        xnT = c(KD, T)
        tab_at = c.at
        turn_table = c(2, NJ, 33)
        rest_at = c.at
        c = Carver(arena, rest_at)
        turn = [c(2, TP), c(2, TP)]
        turn_tmp = [c(2, TP), c(2, TP)]
        M1, M2, Wt, Gs = c(2, TP), c(2, TP), c(2, TP), c(2, TP)
        Hst = [c(2, T), c(2, T)]
        assert c.at <= rest_at + 7168
        c = Carver(arena, rest_at)
        Braw, BP = [c(NJ, C5), c(NJ, C5)], [c(N5, P), c(N5, P)]
        Craw, CP = [c(N5, P5), c(N5, P5)], [c(N5, 2, P5), c(N5, 2, P5)]
        Btmp = [c(NJ, C5), c(NJ, C5)]
        assert c.at == rest_at + 7168
        Zs, fin = c(2, NS, NJ), c(2, 1 + NS, NJ)
        rms5 = c(T)
        assert c.at <= AR_N
        LV = [64, 32, 16, 8, 4, 2, 1]
        LW = [TP if b <= 8 else 2 * P for b in LV]
        LO = [sum(LW[:i]) for i in range(len(LV))]
        c = Carver(arena, rest_at)
        QK = [c(sum(LW)), c(sum(LW))]
        att, qG, kG = ([c(TP), c(TP)] for _ in range(3))
        kGt, Sst = ([c(3, P), c(3, P)] for _ in range(2))
        assert c.at <= rest_at + 7168
        c = Carver(arena, xnT_at)
        S0 = [c(NH, P) for _ in range(3)]
        vk = c(NH, P)
        fin_rows = Carver(arena, tab_at)(2, 3, P)
        c = Carver(arena, gT_at)
        vrow, h0row, r5 = c(P), c(2, 2, P), c(12, P)
        assert c.at <= x1_at
        xraw = Carver(arena, x1_at)(3, D)
        c = Carver(upair, 0)
        v_tok = c(3, HG)
        mat_at = c.at
        BT, CT = [c(N5, P), c(N5, P)], [c(N5, P), c(N5, P)]
        sgT = Carver(upair, mat_at)(N5, T)
        c = Carver(upair, 0)
        xsq = c(D)
        ang_r, ang_n, ang_cos, ang_sin = (c(NJ, 33) for _ in range(4))
        z_tmp = [c(NS, NJ), c(NS, NJ)]
        assert c.at <= 2 * SLOT
        c = Carver(arena, tab_at)
        iI, iJ, iX, iota_i = (c(P).bitcast(I32) for _ in range(4))
        mX, mG, mL = c(P), c(P), c(P)
        c = Carver(arena, x1_at)
        x1, wr = c(3, D), c(KD, NG + NE)
        assert c.at <= xnT_at
        xn2T = Carver(arena, xnT_at)(KD, T)
        oh = Carver(arena, xnT_at)(3, CAP)
        c = Carver(arena, tab_at)
        xn_rows = c(3, D)
        c = Carver(arena, tab_at)
        _, xg0, xg1 = c(D), c(D), c(D)
        xg = [xg0, xg1]
        yout = [c(D), c(D)]
        assert c.at <= AR_N
        c = Carver(arena, 0)
        xgT = [c(KD, CAP), c(KD, CAP)]
        sg, up, hh = c(FH), c(FH), c(FH)
        hT = c(KF, CAP)
        lg, c8, e8, pick, f8 = c(3, NG + NE), c(3, 8), c(3, NG), c(3, NG, EG), c(3, EG)
        OH0, OH1, Mr = c(3, NE), c(3, NE), c(3, NE)
        assert c.at <= x1_at
        gfin = Carver(arena, tab_at)(D)
        yrow = [Carver(arena, tab_at + D * (1 + i))(D) for i in range(4)]
        junk = Carver(arena, xnT_at)(D)
        route = sb("route", [P, 608])
        c = Carver(route, 0)
        bias36 = c(NG + NE)
        tid, valid, pgi, dv, w0, w1, grp, e0, e1 = (c(3) for _ in range(9))
        ohg = c(3, NG)
        iota32, slotid = c(NE), c(CAP)
        rankm = c(3, NE + 1)
        PL = c(3, NE + 1, 3)
        maxn, ext, mvals = c(1), c(ROUNDS - 1), c(33)
        assert c.at <= 608
        gmax, fmax = sb("gmax", [P, 3, 8]), sb("fmax", [P, 3, 8])
        gidx, fidx = sb("gidx", [P, 3, 8], U32), sb("fidx", [P, 3, 8], U32)
        extra_i = sb("extra_i", [P, 1], I32)
        idx_tok = [sb(f"idx_tok{i}", [CAP, 1], U32) for i in range(2)]
        idx_dst = [sb(f"idx_dst{i}", [CAP, 1], U32) for i in range(2)]
        gcol = [sb(f"gcol{i}", [CAP, 1]) for i in range(2)]

        PB = [ctx.enter_context(nc.psum_tensor(f"bank{i}", [P, 512], F32)) for i in range(8)]
        xn_dram = nc.dram_tensor("xn_rows", [T, D], F32, kind="Internal").ap()
        y_dram = nc.dram_tensor("expert_rows", [2 * T, D], F32, kind="Internal").ap()

        V_MIX, V_FFN, V_D, V_BGLU, V_G5, V_LB0, V_LB1, V_GH = 0, KD, 32, 40, 48, 56, 64, 72

        def sems(names):
            return [sem(n) for n in names.split()]

        x_loaded, vec_loaded, s5_loaded, wr_loaded = sems("x_loaded vec_loaded s5_loaded wr_loaded")
        slot_loaded = [sem(f"slot_loaded{i}") for i in range(6)]
        pool_consts, dve_consts, act_step, dve_step, pool_step = sems("pool_consts dve_consts act_step dve_step pool_step")
        x_rms, xn_made, xt_done, xt_copied, vec_t, vec_copied = sems("x_rms xn_made xt_done xt_copied vec_t vec_copied")
        lb_in, lb_exp = sems("lb_in lb_exp")
        s5_exp_in, s5_exp, s5_sin_in, s5_sin, s5r_ready = sems("s5_exp_in s5_exp s5_sin_in s5_sin s5r_ready")
        par_t, par_copied, ang_ready, table_ready = sems("par_t par_copied ang_ready table_ready")
        mat_ready, mat_t, mat_copied = sems("mat_ready mat_t mat_copied")
        proj_done, proj_read = sems("proj_done proj_read")
        bu_done, bu_read, turn_ready, turn_used = sems("bu_done bu_read turn_ready turn_used")
        h_ready, h_used, y_done, y5_ready, fin_copied = sems("h_ready h_used y_done y5_ready fin_copied")
        gelu_done, k_ready, lnf_done, G_ready = sems("gelu_done k_ready lnf_done G_ready")
        diff_ready, exp_ready, qk_ready, att_done, att_read = sems("diff_ready exp_ready qk_ready att_done att_read")
        kgt_done, kgt_copied, st_done, st_ready, o_done, o_copied = sems("kgt_done kgt_copied st_done st_ready o_done o_copied")
        S0_loaded = [sem(f"S0_loaded{i}") for i in range(3)]
        S0_stored = [sem(f"S0_stored{i}") for i in range(3)]
        st_stored = [sem(f"st_stored{i}") for i in range(2)]
        S0_decayed, vb_done, S1_ready, os_done, samp_copied = sems("S0_decayed vb_done S1_ready os_done samp_copied")
        glu_done, glu_read, y5g_ready, sq_ready, ss_done, rt_ready, yT_ready = sems(
            "glu_done glu_read y5g_ready sq_ready ss_done rt_ready yT_ready")
        fin_t, fin_read, fin_stored = sems("fin_t fin_read fin_stored")
        x_again, out_done, x1_ready = sems("x_again out_done x1_ready")
        r_rms, r_rstd, xn2_ready, xn2_stored, xt2_done, xt2_copied = sems(
            "r_rms r_rstd xn2_ready xn2_stored xt2_done xt2_copied")
        logit_done, sm_in, sm_exp, route_ready, rank_done, lists_ready = sems(
            "logit_done sm_in sm_exp route_ready rank_done lists_ready")
        oh_ready, list_done, idx_ready, tr_done, xgT_ready, wait_carried = sems(
            "oh_ready list_done idx_ready tr_done xgT_ready wait_carried")
        gathered, scattered = ([sem(f"{n}{i}") for i in range(2)] for n in ("gathered", "scattered"))
        gate_up_done, act_ready, h_made, hT_done, hT_ready, down_done, rows_ready, rows_free = sems(
            "gate_up_done act_ready h_made hT_done hT_ready down_done rows_ready rows_free")
        moe_done, gfin_loaded, ysum_done, f_rms, out_ready, out_stored = sems(
            "moe_done gfin_loaded ysum_done f_rms out_ready out_stored")
        yrow_loaded = [sem(f"yrow_loaded{i}") for i in range(2)]

        PART_AT = {"u": 0, "q": W5, "f": W5 + HG, "v": W5 + 2 * HG, "g": W5 + 3 * HG}
        NB = W5 // CB
        STEPS = [(part, m) for part in "ufqvg" for m in range(NB)]
        NW, NGLU, NO = len(STEPS), 2, D // CB
        NPRE = NW + NGLU + NO
        PRE_SLOTS = 4
        FILLS = [len(range(s, NPRE, PRE_SLOTS)) for s in range(4)] + [0, 0]
        MOE_SLOT = (2, 3, 0, 1)
        S5_TILES = {n: [2 * (n - NB), 2 * (n - NB) + 1] for n in range(NB, NW)}
        CHUNKS = ((0, P), (P, P), (2 * P, LAST))

        def token_rows(tile):
            meta, prompt, sample = t["meta_tokens"], t["x_prompt"][0], t["x_sample"][:, 0]
            if tile == 0:
                return [(0, meta), (NM, prompt[0:P - NM])]
            if tile == 1:
                return [(0, prompt[P - NM:2 * P - NM])]
            return [(0, prompt[2 * P - NM:SEQ]), (LAST, sample)]

        def slot(s, k):
            return ring[:, s, :].rearrange("p (k n) -> p k n", k=k)

        def run_rounds(eng, one_round):
            one_round(0)
            eng.wait_ge(lists_ready, 1)
            extra = eng.value_load(extra_i[0:1, 0:1], min_val=0, max_val=ROUNDS - 1)
            with eng.If(extra > 0):
                with eng.Fori(0, extra) as r:
                    one_round(r + 1)

        def is_first(R):
            return isinstance(R, int)

        block = ctx.enter_context(nc.Block())

        @block.sync
        def _(sp):
            def load_gate_up(e, q):
                w = t["w_gate"] if q % 2 == 0 else t["w_up"]
                half = D // 2
                src = w[0][bass.ds(e, 1), (q // 2) * half:(q // 2 + 1) * half, :]
                sp.dma_start(slot(MOE_SLOT[q], KD // 2), src.rearrange("a (k p) n -> p (a k) n", p=P)) \
                    .then_inc(slot_loaded[MOE_SLOT[q]], 16)

            def load_down(e, s):
                half = FH // 2
                src = t["w_down"][0][bass.ds(e, 1), (s - 4) * half:(s - 3) * half, :]
                sp.dma_start(slot(s, KF // 2), src.rearrange("a (k p) n -> p (a k) n", p=P)) \
                    .then_inc(slot_loaded[s], 16)

            def pre_load(n):
                last = n - PRE_SLOTS
                if last >= NW + NGLU:
                    sp.wait_ge(out_done, 2 * (last - NW - NGLU + 1))
                elif last >= NW:
                    sp.wait_ge(glu_done, N5 // 2 * (last - NW + 1))
                elif last >= 0:
                    sp.wait_ge(proj_done, 2 * (last + 1))
                if n < NW:
                    part, m = STEPS[n]
                    c0 = PART_AT[part] + m * CB
                    src = t["w_in"][0, :, c0:c0 + CB]
                elif n < NW + NGLU:
                    src = t["s5_w_glu"][0, :, (n - NW) * 2 * CB:(n - NW + 1) * 2 * CB]
                else:
                    o = n - NW - NGLU
                    src = t["w_out"][0, :, o * CB:(o + 1) * CB]
                sp.dma_start(slot(n % PRE_SLOTS, src.shape[0] // P), src.rearrange("(k p) n -> p k n", p=P)) \
                    .then_inc(slot_loaded[n % PRE_SLOTS], 16)

            for tile in range(3):
                for at, rows in token_rows(tile):
                    sp.dma_start(xraw[at:at + rows.shape[0], tile, :], rows).then_inc(x_loaded, 16)
            for n in range(NW + PRE_SLOTS):
                pre_load(n)

            def load_S0(b):
                if b >= 3:
                    sp.wait_ge(os_done, b - 2)
                    sp.wait_ge(S0_stored[b % 3], 16 * (b // 3))
                else:
                    sp.wait_ge(proj_done, 2 * NW)
                sp.dma_start(S0[b % 3], t["state_hgrn"][0, b].rearrange("h k v -> k h v")).then_inc(S0_loaded[b % 3], 16)

            for b in range(3):
                load_S0(b)
            for b in range(NS):
                sp.wait_ge(S1_ready, b + 1)
                sp.dma_start(t["hgrn_sample"][0, b].rearrange("h k v -> k h v"), S0[b % 3]).then_inc(S0_stored[b % 3], 16)
                sp.wait_ge(st_ready, 3 * (b + 1))
                sp.dma_start(t["hgrn_prompt"][0, 0, b], Sst[b % 2][:, 2, :]).then_inc(st_stored[b % 2], 16)
                if b + 3 < NS:
                    load_S0(b + 3)

            sp.wait_ge(yT_ready, 2)
            for tile in range(3):
                for at, rows in token_rows(tile):
                    sp.dma_start(x1[at:at + rows.shape[0], tile, :], rows).then_inc(x_again, 16)
            sp.dma_start(wr[:, :, 0:NG], t["w_coarse"][0].rearrange("(k p) n -> p k n", p=P)).then_inc(wr_loaded, 16)
            sp.dma_start(wr[:, :, NG:NG + NE], t["w_fine"][0].rearrange("(k p) n -> p k n", p=P)).then_inc(wr_loaded, 16)
            for n in range(NW + PRE_SLOTS, NPRE):
                pre_load(n)
            for s in (4, 5):
                load_down(0, s)
            for q in range(4):
                sp.wait_ge(out_done, 2 * (NO - 3 + q))
                load_gate_up(0, q)

            def round_loads(R):
                with sp.Fori(1 if is_first(R) else 0, NE) as e:
                    x = e + R * NE
                    for q in range(4):
                        sp.wait_ge(gate_up_done, x * 2 + (q // 2 - 1))
                        load_gate_up(e, q)
                    for s in (4, 5):
                        sp.wait_ge(down_done, x * 2 + (s - 5))
                        load_down(e, s)

            run_rounds(sp, round_loads)

            sp.wait_ge(moe_done, 1)
            sp.dma_start(gfin, t["norm_final"].rearrange("(a n) -> a n", a=1).broadcast_to([P, D])).then_inc(gfin_loaded, 16)
            for tile in range(3):
                if tile == 2:
                    sp.wait_ge(ysum_done, 1)
                for j in range(2):
                    r0 = j * T + tile * P
                    sp.dma_start(yrow[2 * (tile % 2) + j][0:TT[tile], :], y_dram[r0:r0 + TT[tile], :]) \
                        .then_inc(yrow_loaded[tile % 2], 16)
            y = t["y_prompt"][0]
            for tile in range(3):
                sp.wait_ge(out_ready, tile + 1)
                if tile == 0:
                    sp.dma_start(y[0:P - NM, :], x1[NM:P, 0, :]).then_inc(out_stored, 16)
                elif tile == 1:
                    sp.dma_start(y[P - NM:2 * P - NM, :], x1[:, 1, :]).then_inc(out_stored, 16)
                else:
                    sp.dma_start(y[2 * P - NM:SEQ, :], x1[0:LAST, 2, :]).then_inc(out_stored, 16)
                    sp.dma_start(t["y_sample"][:, 0, :], x1[LAST:LAST + NS, 2, :]).then_inc(out_stored, 16)
            sp.wait_ge(out_stored, 64)
            for b in range(3):
                sp.wait_ge(S0_stored[b], 16 * len(range(b, NS, 3)))
            for b in range(2):
                sp.wait_ge(st_stored[b], 16 * NH // 2)

        @block.scalar
        def _(act):
            for name, at in (("norm_mix", V_MIX), ("norm_ffn", V_FFN), ("s5_D", V_D), ("s5_b_glu", V_BGLU),
                             ("s5_out_gain", V_G5), ("hg_lb_logits", V_LB0), ("hg_out_gain", V_GH)):
                rows = t[name].rearrange("a (k p) -> (a k) p", p=P)
                act.dma_start(vrow[at:at + rows.shape[0], :], rows).then_inc(vec_loaded, 16)
            act.dma_start(r5[0:NJ, 0, :], t["s5_A_re"].rearrange("a (j g) p -> (a j) (g p)", g=2)).then_inc(s5_loaded, 16)
            act.dma_start(r5[0:NJ, 1, :], t["s5_A_im"].rearrange("a (j g) p -> (a j) (g p)", g=2)).then_inc(s5_loaded, 16)
            act.dma_start(r5[0:NJ, 2, 0:2], t["s5_log_step"].rearrange("a (j g) -> (a j) g", g=2)).then_inc(s5_loaded, 16)
            for z, name in enumerate(("state_s5_re", "state_s5_im")):
                src = t[name][0].rearrange("(h b) (j g) p -> h b j (g p)", g=2, h=2)
                for half in range(2):
                    act.dma_start(h0row[:, z, half, :], src[half].rearrange("b j n -> (b j) n")).then_inc(s5_loaded, 16)
            for z, (bn, cn) in enumerate((("s5_B_re", "s5_C_re"), ("s5_B_im", "s5_C_im"))):
                act.dma_start(Braw[z], t[bn][0].rearrange("(j g) p c -> (g p) j c", g=2)).then_inc(s5_loaded, 16)
                act.dma_start(Craw[z], t[cn][0].rearrange("(i g) c p -> (g c) i p", g=8)).then_inc(s5_loaded, 16)
            act.dma_start(bias36[:, 0:NG], t["b_coarse"].broadcast_to([P, NG])).then_inc(wr_loaded, 16)
            act.dma_start(bias36[:, NG:NG + NE], t["b_fine"].broadcast_to([P, NE])).then_inc(wr_loaded, 16)

            step = Chain(act, act_step)

            def token_rms(src, scratch, signal):
                for tile in range(3):
                    n = TT[tile]
                    step.link(nc.scalar.activation(scratch[0:n, :], src[0:n, tile, :], ACT.Square,
                                                   accum_out=token_stats[0:n, tile:tile + 1]))
                for tile in range(3):
                    n = TT[tile]
                    s = token_stats[0:n, tile:tile + 1]
                    nc.scalar.activation(s, s, ACT.Sqrt, bias=eps_col[0:n, :], scale=1.0 / D).then_inc(signal, 1)

            act.wait_ge(x_loaded, 16 * 5)
            act.wait_ge(dve_consts, 1)
            token_rms(xraw, xsq, x_rms)
            act.wait_ge(s5_loaded, 16 * 11)
            nc.scalar.activation(r5[0:NJ, 2, 2:4], r5[0:NJ, 2, 0:2], ACT.Exp).then_inc(s5_exp, 1)
            act.wait_ge(s5_exp_in, 1)
            nc.scalar.activation(r5[0:NJ, 3, :], r5[0:NJ, 10, :], ACT.Exp).then_inc(s5_exp, 1)
            act.wait_ge(lb_in, 1)
            nc.scalar.activation(lb_tmp[:, 0:2, :], lb_tmp[:, 0:2, :], ACT.Exp).then_inc(lb_exp, 1)
            act.wait_ge(s5_sin_in, 1)
            nc.scalar.activation(r5[0:NJ, 6, :], r5[0:NJ, 4, :], ACT.Sin).then_inc(s5_sin, 1)
            nc.scalar.activation(r5[0:NJ, 7, :], r5[0:NJ, 5, :], ACT.Sin).then_inc(s5_sin, 1)
            for z, ang in ((1, ang_sin), (0, ang_cos)):
                act.wait_ge(ang_ready, 2 - z)
                nc.scalar.activation(turn_table[:, z], ang, ACT.Sin, scale=6.283185).then_inc(table_ready, 1)

            def evac(n):
                part, m = STEPS[n]
                for b in range(2):
                    unit = 2 * n + b
                    act.wait_ge(proj_done, unit + 1)
                    bank, i = PB[unit % 4], 2 * m + b
                    if part == "u":
                        ins = nc.scalar.activation(uT[:, i, :], bank[:, 0:T], ACT.Copy)
                    elif part == "f":
                        ins = nc.scalar.activation(GT[:, i, :], bank[:, 0:T], ACT.Sigmoid)
                    elif part == "q":
                        ins = nc.scalar.activation(qT[:, i, :], bank[:, 0:T], ACT.Copy, scale=float(P) ** -0.5)
                    elif part == "g":
                        ins = nc.scalar.activation(gT[:, i, :], bank[:, 0:T], ACT.Silu)
                    elif b == 0:
                        ins = nc.scalar.activation(v_tok[:, 0:2, m * CB:(m + 1) * CB],
                                                   bank[:, 0:2 * CB].rearrange("p (a n) -> p a n", a=2), ACT.Copy)
                    else:
                        ins = nc.scalar.activation(v_tok[0:TT[2], 2, m * CB:(m + 1) * CB], bank[0:TT[2], 0:CB], ACT.Copy)
                    ins.then_inc(proj_read, 1)

            def keep_last(j):
                act.wait_ge(h_ready, j + 1)
                nc.scalar.activation(fin[:, :, :, j], Hst[j % 2][:, :, TP - 1:T], ACT.Copy).then_inc(fin_copied, 1)

            for n in range(NW):
                if STEPS[n] == ("f", 0):
                    act.wait_ge(xt_done, 12)
                if STEPS[n] == ("v", 0):
                    act.wait_ge(mat_copied, 8)
                evac(n)
                for j in S5_TILES.get(n, []):
                    if j >= 1:
                        keep_last(j - 1)
            keep_last(NJ - 1)
            act.wait_ge(y5_ready, N5)
            nc.scalar.activation(uT, uT, ACT.Gelu_apprx_tanh).then_inc(gelu_done, 1)
            act.wait_ge(k_ready, NH)
            nc.scalar.activation(GT, GT, ACT.Ln).then_inc(lnf_done, 1)

            for h in range(NH):
                b = h % 2
                act.wait_ge(G_ready, h + 1)
                act.wait_ge(diff_ready, h + 1)
                nc.scalar.activation(QK[b], QK[b], ACT.Exp)
                if h >= 2:
                    act.wait_ge(o_done, h - 1)
                    act.wait_ge(st_ready, 3 * (h - 1))
                nc.scalar.activation(qG[b], GT[:, h, 0:TP], ACT.Exp)
                nc.scalar.activation(chunk_decay[b][:, :], GT[:, h, 2 * P - 1:TP:LAST], ACT.Exp)
                for c0, n in CHUNKS:
                    ins = nc.scalar.activation(kG[b][:, c0:c0 + n], GT[:, h, c0:c0 + n], ACT.Exp,
                                               bias=GT[:, h, c0 + n - 1:c0 + n], scale=-1.0)
                ins.then_inc(exp_ready, 1)
                act.wait_ge(kgt_done, h + 1)
                nc.scalar.activation(kGt[b][:, 0:2, :], PB[7][:, 0:2 * P].rearrange("p (a n) -> p a n", a=2), ACT.Copy)
                nc.scalar.activation(kGt[b][0:LAST, 2, :], PB[7][0:LAST, 2 * P:3 * P], ACT.Copy).then_inc(kgt_copied, 1)
                act.wait_ge(glu_done, h + 1)
                nc.scalar.activation(sgT[:, h, :], PB[2][:, 0:T], ACT.Sigmoid,
                                     bias=vecs[:, V_BGLU + h:V_BGLU + h + 1]).then_inc(glu_read, 1)
                act.wait_ge(o_done, h + 1)
                nc.scalar.activation(kT[:, h, 0:TP], PB[6][:, 0:TP], ACT.Copy).then_inc(o_copied, 1)
            act.wait_ge(y5g_ready, 1)
            nc.scalar.activation(sgT, uT, ACT.Square).then_inc(sq_ready, 1)
            act.wait_ge(samp_copied, 1)
            act.wait_ge(o_copied, NH)
            nc.scalar.activation(qT, kT, ACT.Square).then_inc(sq_ready, 1)
            act.wait_ge(ss_done, 1)
            nc.scalar.activation(rms5, PB[3][:, 0:T], ACT.Sqrt, bias=eps_col[:, :], scale=1.0 / W5).then_inc(rt_ready, 1)
            for h in range(NH):
                act.wait_ge(ss_done, h + 2)
                nc.scalar.activation(GT[:, h, :], PB[4 + h % 2][:, 0:T], ACT.Sqrt, bias=eps_col[:, :],
                                     scale=1.0 / P).then_inc(rt_ready, 1)
            for z in range(2):
                act.wait_ge(fin_t, z + 1)
                nc.scalar.activation(fin_rows[0:3 * NJ, z, :, :], PB[z][0:3 * NJ, 0:3 * P].rearrange("p (a n) -> p a n", a=3),
                                     ACT.Copy).then_inc(fin_read, 1)
            act.wait_ge(fin_read, 2)
            for z, (pn, sn) in enumerate((("s5_re_prompt", "s5_re_sample"), ("s5_im_prompt", "s5_im_sample"))):
                act.dma_start(t[pn][0, 0].rearrange("(j g) p -> j (g p)", g=2), fin_rows[0:NJ, z, 0, :]).then_inc(fin_stored, 16)
                rows = t[sn][0].rearrange("b (j g) p -> (b j) (g p)", g=2)
                act.dma_start(rows[0:2 * NJ], fin_rows[NJ:3 * NJ, z, 0, :]).then_inc(fin_stored, 16)
                act.dma_start(rows[2 * NJ:5 * NJ], fin_rows[0:3 * NJ, z, 1, :]).then_inc(fin_stored, 16)
                act.dma_start(rows[5 * NJ:8 * NJ], fin_rows[0:3 * NJ, z, 2, :]).then_inc(fin_stored, 16)
            act.wait_ge(fin_stored, 16 * 8)
            act.wait_ge(x1_ready, 2 * NO)
            token_rms(x1, yout[0], r_rms)
            act.wait_ge(r_rstd, 1)
            for tile in range(3):
                n = TT[tile]
                nc.scalar.activation(xn_rows[0:n, tile, :], x1[0:n, tile, :], ACT.Copy,
                                     scale=token_stats[0:n, 3 + tile:4 + tile]).then_inc(xn2_ready, 1)
                act.wait_ge(xn2_ready, tile + 1)
                act.dma_start(xn_dram[tile * P:tile * P + n, :], xn_rows[0:n, tile, :]).then_inc(xn2_stored, 16)
            act.wait_ge(sm_in, 1)
            nc.scalar.activation(e8, e8, ACT.Exp).then_inc(sm_exp, 1)
            act.wait_ge(sm_in, 2)
            nc.scalar.activation(dv, dv, ACT.Exp).then_inc(sm_exp, 1)
            nc.scalar.activation(chunk_decay[0][:, :], chunk_decay[0][:, :], ACT.Copy).then_inc(rows_ready, 1)

            def round_act(R):
                with act.Fori(0, NE // 2) as i:
                    for b in range(2):
                        x = i * 2 + (R * NE + b)
                        act.wait_ge(gate_up_done, x * 2 + 2)
                        act.wait_ge(h_made, x + 1)
                        nc.scalar.activation(sg[0:CAP, :], PB[b][0:CAP, :], ACT.Silu)
                        nc.scalar.activation(up[0:CAP, :], PB[b][CAP:P, :], ACT.Copy).then_inc(act_ready, 1)
                        act.wait_ge(down_done, x * 2 + 2)
                        act.wait_ge(rows_free, x + 1)
                        for cc in range(4):
                            ins = nc.scalar.activation(yout[b][0:CAP, cc * 512:(cc + 1) * 512],
                                                       PB[2 + cc // 2][(cc % 2) * CAP:(cc % 2 + 1) * CAP, :], ACT.Copy)
                        ins.then_inc(rows_ready, 1)

            run_rounds(act, round_act)
            for tile in range(3):
                n = TT[tile]
                act.wait_ge(ysum_done, tile + 1)
                s = token_stats[0:n, tile:tile + 1]
                step.link(nc.scalar.activation(junk[0:n, :], x1[0:n, tile, :], ACT.Square, accum_out=s))
                nc.scalar.activation(s, s, ACT.Sqrt, bias=eps_col[0:n, :], scale=1.0 / D).then_inc(f_rms, 1)

        @block.gpsimd
        def _(pool):
            def made(ins):
                ins.then_inc(pool_consts, 1)

            made(pool.memset(ident[:, :], 0.0))
            made(pool.memset(upper[:, :], 0.0))
            pool.wait_ge(pool_consts, 2)
            made(pool.affine_select(out=ident[:, :], in_=ident[:, :], compare_op=ALU.not_equal, fill=1.0, base=0,
                                    pattern=[[-1, P]], channel_multiplier=1))
            made(pool.affine_select(out=upper[:, :], in_=upper[:, :], compare_op=ALU.is_ge, fill=1.0, base=0,
                                    pattern=[[-1, P]], channel_multiplier=1))
            made(pool.iota(iI, pattern=[[1, P]], base=0, channel_multiplier=0))
            made(pool.iota(iJ, pattern=[[0, P]], base=0, channel_multiplier=1))
            made(pool.iota(iota_i[:, 0:64], pattern=[[1, 64]], base=0, channel_multiplier=0))
            made(pool.iota(iota_i[:, 64:81], pattern=[[16, 17]], base=0, channel_multiplier=0))
            made(pool.iota(iota_i[:, 81:84], pattern=[[P, 3]], base=0, channel_multiplier=1))

            step = Chain(pool, pool_step)
            pool.wait_ge(table_ready, 2)
            pool.wait_ge(mat_t, 8)
            for j in range(NJ):
                b = j % 2
                if j >= 2:
                    pool.wait_ge(turn_used, j - 1)
                A = [turn_table[:, z, j, 16:33].unsqueeze(2).broadcast_to([P, 17, 16]) for z in range(2)]
                B = [turn_table[:, z, j, 0:16].unsqueeze(1).broadcast_to([P, 17, 16]) for z in range(2)]

                def out(x, z):
                    return x[:, z].rearrange("p (a b) -> p a b", b=16)

                t1, t2 = turn_tmp
                step.add(pool.tensor_tensor(out(t1, 0), A[0], B[0], ALU.mult))
                step.add(pool.tensor_tensor(out(t1, 1), A[1], B[0], ALU.mult))
                step.add(pool.tensor_tensor(out(t2, 0), A[1], B[1], ALU.mult))
                step.add(pool.tensor_tensor(out(t2, 1), A[0], B[1], ALU.mult))
                step.settle()
                step.add(pool.tensor_tensor(turn[b][:, 0], t1[:, 0], t2[:, 0], ALU.subtract))
                step.add(pool.tensor_tensor(turn[b][:, 1], t1[:, 1], t2[:, 1], ALU.add))
                step.settle()
                pool.engine_nop().then_inc(turn_ready, 1)
            pool.wait_ge(y5_ready, N5)
            for h in range(NH):
                b = h % 2
                pool.wait_ge(G_ready, h + 1)
                if h >= 2:
                    pool.wait_ge(att_done, 8 * (h - 1))
                for l, B in enumerate(LV):
                    g = GT[:, h, 0:LW[l]].rearrange("p (n two b) -> p n two b", two=2, b=B)
                    o = QK[b][:, LO[l]:LO[l] + LW[l]].rearrange("p (n two b) -> p n two b", two=2, b=B)
                    mid = g[:, :, 0, B - 1:B].broadcast_to([P, LW[l] // (2 * B), B])
                    pool.tensor_tensor(o[:, :, 0, :], mid, g[:, :, 0, :], ALU.subtract)
                    ins = pool.tensor_tensor(o[:, :, 1, :], g[:, :, 1, :], mid, ALU.subtract)
                ins.then_inc(diff_ready, 1)
                pool.wait_ge(S0_loaded[h % 3], 16 * (h // 3 + 1))
                pool.tensor_tensor(S0[h % 3], S0[h % 3], fs[:, :, h:h + 1].broadcast_to([P, NH, P]), ALU.mult) \
                    .then_inc(S0_decayed, 1)
            pool.engine_nop().then_inc(rows_free, 1)
            pool.engine_nop().then_inc(rows_free, 1)
            pool.wait_ge(xn2_stored, 48)
            last_token, last_row = pool.to_reg(T - 1), pool.to_reg(2 * T - 1)

            def gather(g, p):
                pool.wait_ge(idx_ready, g + 1)
                pool.sem_inc(wait_carried, 1)
                pool.indirect_dma_start(out=xg[p][0:CAP, :], out_offset=None, in_=xn_dram,
                                        in_offset=bass.IndirectOffsetOnAxis(ap=idx_tok[p][:, 0:1], axis=0),
                                        bounds_check=last_token, oob_is_err=False).then_inc(gathered[p], 16)

            def round_rows(R):
                if is_first(R):
                    pool.wait_ge(xt2_done, 12)
                else:
                    pool.wait_ge(tr_done, R * (NE + 1) + 1)
                gather(R * (NE + 1), 0)
                with pool.Fori(0, NE // 2) as i:
                    for b in range(2):
                        x = i * 2 + (R * NE + b)
                        g = i * 2 + (R * (NE + 1) + b + 1)
                        pool.wait_ge(tr_done, g)
                        gather(g, 1 - b)
                        pool.wait_ge(rows_ready, x + 2)
                        pool.sem_inc(wait_carried, 1)
                        pool.indirect_dma_start(out=y_dram, out_offset=bass.IndirectOffsetOnAxis(ap=idx_dst[b][:, 0:1], axis=0),
                                                in_=yout[b][0:CAP, :], in_offset=None, bounds_check=last_row,
                                                oob_is_err=False).then_inc(scattered[b], 16)
                        pool.wait_ge(scattered[b], i * 16 + (R * (NE // 2) + 1) * 16)
                        pool.sem_inc(rows_free, 1)

            run_rounds(pool, round_rows)
            pool.engine_nop().then_inc(moe_done, 1)

        @block.tensor
        def _(pe):
            pe.wait_ge(pool_consts, 4)
            pe.wait_ge(vec_loaded, 16 * 7)
            pe.transpose(PB[7][:, 0:80], vrow[0:80, :], ident[0:80, 0:80]).then_inc(vec_t, 1)

            def transpose_tokens(src, ready, done, copied):
                for tile in range(3):
                    n = TT[tile]
                    pe.wait_ge(ready, tile + 1)
                    for q in range(KD // 4):
                        unit = tile * (KD // 4) + q
                        if unit >= 4:
                            pe.wait_ge(copied, unit - 3)
                        for a in range(4):
                            k = 4 * q + a
                            ins = pe.transpose(PB[unit % 4][:, a * P:a * P + n], src[0:n, tile, k * P:(k + 1) * P],
                                               ident[0:n, 0:n])
                        ins.then_inc(done, 1)

            transpose_tokens(xraw, xn_made, xt_done, xt_copied)

            def project(n, half_work):
                part, _ = STEPS[n]
                s = n % PRE_SLOTS
                w = slot(s, KD)
                pe.wait_ge(slot_loaded[s], 16 * (n // PRE_SLOTS + 1))
                if n == 0:
                    pe.wait_ge(xt_copied, 12)
                for b in range(2):
                    unit = 2 * n + b
                    if unit >= 4:
                        pe.wait_ge(proj_read, unit - 3)
                    bank = PB[unit % 4]
                    if part == "v":
                        for tile in ((0, 1) if b == 0 else (2,)):
                            at = (tile % 2) * CB
                            for k in range(KD):
                                ins = pe.matmul(bank[0:TT[tile], at:at + CB], xnT[:, k, tile * P:tile * P + TT[tile]],
                                                w[:, k, :], start=(k == 0), stop=(k == KD - 1))
                    else:
                        for k in range(KD):
                            ins = pe.matmul(bank[:, 0:T], w[:, k, b * P:(b + 1) * P], xnT[:, k, :],
                                            start=(k == 0), stop=(k == KD - 1))
                    ins.then_inc(proj_done, 1)
                    half_work(b)

            def bu(j):
                i, a = j // 4, j % 4
                rows = slice(32 * a, 32 * a + 32)
                if j % 4 == 0:
                    pe.wait_ge(proj_read, i + 1)
                if j >= 1:
                    pe.wait_ge(bu_read, j)
                else:
                    pe.wait_ge(mat_copied, 8)
                for z in range(2):
                    ins = pe.matmul(PB[4 + z][:, 0:T], BT[z][rows, i, :], uT[rows, i, :], start=True, stop=True)
                ins.then_inc(bu_done, 1)

            def y_of(j):
                i, a = j // 4, j % 4
                pe.wait_ge(h_ready, j + 1)
                if a == 0 and i >= 1:
                    pe.wait_ge(y5_ready, i)
                for z in range(2):
                    ins = pe.matmul(PB[6][32 * a:32 * a + 32, 0:T], CT[z][:, i, 32 * a:32 * a + 32], Hst[j % 2][:, z, :],
                                    start=(z == 0), stop=(z == 1))
                ins.then_inc(h_used, 1)

            def parameters(n):
                if n == 0:
                    pe.wait_ge(s5r_ready, 1)
                    pe.wait_ge(vec_copied, 1)
                    for q, row in enumerate((3, 5, 8, 9, 6, 7)):
                        ins = pe.transpose(PB[7][:, P + q * NJ:P + (q + 1) * NJ], r5[0:NJ, row, :], ident[0:NJ, 0:NJ])
                    ins.then_inc(par_t, 1)
                    for z in range(2):
                        for half in range(2):
                            at = z * 2 * P + half * P
                            ins = pe.transpose(PB[6][:, at:at + P], h0row[:, z, half, :], ident[:, :])
                    ins.then_inc(par_t, 1)
                else:
                    pe.wait_ge(mat_ready, n)
                    pe.wait_ge(par_copied, 2)
                    for z in range(2):
                        for q in range(2):
                            bank = PB[4 + 2 * z + q]
                            if n == 2:
                                pe.wait_ge(mat_copied, 2 * z + q + 1)
                            for a in range(4):
                                i = 4 * q + a
                                src = BP[z][:, i, :] if n == 1 else CP[z][:, i].rearrange("p a b -> p (a b)")
                                ins = pe.transpose(bank[:, a * P:(a + 1) * P], src, ident[:, :])
                            ins.then_inc(mat_t, 1)

            for n in range(NW):
                tiles = S5_TILES.get(n)

                def between(b):
                    if tiles:
                        j = tiles[b]
                        bu(j)
                        if j >= 1:
                            y_of(j - 1)
                    elif b == 1 and 1 <= n <= 3:
                        parameters(n - 1)

                project(n, between)
            y_of(NJ - 1)

            pe.wait_ge(y5_ready, N5)
            pe.wait_ge(proj_read, 2 * NW)
            for h in range(NH):
                b = h % 2
                cols = slice(h * P, (h + 1) * P)
                if h >= 1:
                    pe.wait_ge(S1_ready, h)
                for z in range(2):
                    ins = pe.matmul(PB[z][:, :], ident[0:TT[2], LAST + h:LAST + h + 1].broadcast_to([TT[2], P]),
                                    v_tok[0:TT[2], 2, z * 512:(z + 1) * 512], start=True, stop=True)
                ins.then_inc(vb_done, 1)
                if h == 0:
                    pe.wait_ge(gelu_done, 1)
                else:
                    pe.wait_ge(glu_read, h)
                n = NW + h // 4
                s = n % PRE_SLOTS
                pe.wait_ge(slot_loaded[s], 16 * (n // PRE_SLOTS + 1))
                for k in range(N5):
                    ins = pe.matmul(PB[2][:, 0:T], slot(s, N5)[:, k, (h % 4) * P:(h % 4 + 1) * P], uT[:, k, :],
                                    start=(k == 0), stop=(k == N5 - 1))
                ins.then_inc(glu_done, 1)
                pe.wait_ge(qk_ready, h + 1)
                if h >= 1:
                    pe.wait_ge(kgt_copied, h)
                for q, (c0, n_) in enumerate(CHUNKS):
                    ins = pe.transpose(PB[7][0:n_, q * P:(q + 1) * P], kG[b][:, c0:c0 + n_], ident[:, :])
                ins.then_inc(kgt_done, 1)
                for l in range(8):
                    u = 8 * h + l
                    if u >= 2:
                        pe.wait_ge(att_read, u - 1)
                    bank = PB[4 + l % 2]
                    for c0, n_ in (CHUNKS if l >= 3 else CHUNKS[:2]):
                        if l < 7:
                            k_ = q_ = QK[b][:, LO[l] + c0:LO[l] + c0 + n_]
                        else:
                            k_, q_ = kT[:, h, c0:c0 + n_], qT[:, h, c0:c0 + n_]
                        ins = pe.matmul(bank[0:n_, c0:c0 + n_], k_, q_, start=True, stop=True)
                    ins.then_inc(att_done, 1)
                pe.wait_ge(kgt_copied, h + 1)
                if h >= 1:
                    pe.wait_ge(st_ready, 3 * h)
                for q, (c0, n_) in enumerate(CHUNKS):
                    ins = pe.matmul(PB[3][:, q * P:(q + 1) * P], kGt[b][0:n_, q, :], v_tok[0:n_, q, cols], start=True, stop=True)
                ins.then_inc(st_done, 1)
                pe.wait_ge(att_read, 8 * (h + 1))
                pe.wait_ge(st_ready, 3 * h + 2)
                if h >= 1:
                    pe.wait_ge(o_copied, h)
                for q, (c0, n_) in enumerate(CHUNKS):
                    if q:
                        pe.matmul(PB[6][:, c0:c0 + n_], Sst[b][:, q - 1, :], qG[b][:, c0:c0 + n_], start=True, stop=False)
                    ins = pe.matmul(PB[6][:, c0:c0 + n_], v_tok[0:n_, q, cols], att[b][0:n_, c0:c0 + n_],
                                    start=(q == 0), stop=True)
                ins.then_inc(o_done, 1)
                pe.wait_ge(S1_ready, h + 1)
                for hd in range(NH):
                    at = 3 * P + hd * NS + h
                    ins = pe.matmul(PB[7][:, at:at + 1], S0[h % 3][:, hd, :], qs[:, hd, h:h + 1], start=True, stop=True)
                ins.then_inc(os_done, 1)

            for z in range(2):
                flat = fin[:, z].rearrange("p a b -> p (a b)")
                for a in range(3):
                    ins = pe.transpose(PB[z][0:3 * NJ, a * P:(a + 1) * P], flat[:, a * 3 * NJ:(a + 1) * 3 * NJ], ident[:, :])
                ins.then_inc(fin_t, 1)
            pe.wait_ge(sq_ready, 1)
            for i in range(N5):
                ins = pe.matmul(PB[3][:, 0:T], ones[:, :], sgT[:, i, :], start=(i == 0), stop=(i == N5 - 1))
            ins.then_inc(ss_done, 1)
            pe.wait_ge(sq_ready, 2)
            for h in range(NH):
                if h >= 2:
                    pe.wait_ge(rt_ready, h)
                pe.matmul(PB[4 + h % 2][:, 0:T], ones[:, :], qT[:, h, :], start=True, stop=True).then_inc(ss_done, 1)

            yT = [uT[:, k] for k in range(N5)] + [gT[:, k] for k in range(NH)]
            pe.wait_ge(yT_ready, 2)
            pe.wait_ge(fin_read, 2)
            for o in range(NO):
                n = NW + NGLU + o
                s = n % PRE_SLOTS
                pe.wait_ge(slot_loaded[s], 16 * (n // PRE_SLOTS + 1))
                for b in range(2):
                    unit = 2 * o + b
                    if unit >= 4:
                        pe.wait_ge(x1_ready, unit - 3)
                    for tile in ((0, 1) if b == 0 else (2,)):
                        at = (tile % 2) * CB
                        for k in range(KD):
                            ins = pe.matmul(PB[unit % 4][0:TT[tile], at:at + CB], yT[k][:, tile * P:tile * P + TT[tile]],
                                            slot(s, KD)[:, k, :], start=(k == 0), stop=(k == KD - 1))
                    ins.then_inc(out_done, 1)

            pe.wait_ge(x1_ready, 2 * NO)
            transpose_tokens(xn_rows, xn2_ready, xt2_done, xt2_copied)
            pe.wait_ge(xt2_copied, 12)
            pe.wait_ge(wr_loaded, 64)
            for tile in range(3):
                for k in range(KD):
                    at = tile * (NG + NE)
                    ins = pe.matmul(PB[6][0:TT[tile], at:at + NG + NE], xn2T[:, k, tile * P:tile * P + TT[tile]], wr[:, k, :],
                                    start=(k == 0), stop=(k == KD - 1))
            ins.then_inc(logit_done, 1)
            pe.wait_ge(route_ready, 1)
            for q in range(4):
                for tile in range(min(q + 1, 3)):
                    last = tile == min(q, 2)
                    ins = pe.matmul(PB[7][:, q * NE:(q + 1) * NE], (upper if tile == q else ones)[:, :], Mr[:, tile, :],
                                    start=(tile == 0), stop=last)
            ins.then_inc(rank_done, 1)
            pe.nop().then_inc(tr_done, 1)

            def list_of(g, e):
                pe.wait_ge(oh_ready, g + 1)
                for tile in range(3):
                    ins = pe.matmul(PB[7][0:CAP, 0:3], oh[:, tile, :], PL[:, tile, bass.ds(e, 1), :].rearrange("p a b -> p (a b)"),
                                    start=(tile == 0), stop=(tile == 2))
                ins.then_inc(list_done, 1)

            def turn_64(out, rows, waits):
                eye = ident[0:CAP, 0:CAP]
                return pe.matmul(out, rows, eye, start=True, stop=True) if waits else pe.transpose(out, rows, eye)

            def transpose_rows(p):
                for k in range(KD):
                    ins = turn_64(PB[4 + k // 8][:, (k % 8) * CAP:(k % 8 + 1) * CAP], xg[p][0:CAP, k * P:(k + 1) * P], k == 0)
                ins.then_inc(tr_done, 1)

            def round_pe(R):
                if is_first(R):
                    pe.wait_ge(lists_ready, 1)
                else:
                    pe.wait_ge(idx_ready, R * (NE + 1))
                    pe.wait_ge(xgT_ready, R * (NE + 1))
                list_of(R * (NE + 1), 0)
                pe.wait_ge(gathered[0], R * (16 * 17) + 16)
                transpose_rows(0)
                with pe.Fori(0, NE // 2) as i:
                    for b in range(2):
                        x = i * 2 + (R * NE + b)
                        g = i * 2 + (R * (NE + 1) + b + 1)
                        pe.wait_ge(idx_ready, g)
                        list_of(g, i * 2 + (b + 1))
                        pe.wait_ge(xgT_ready, g)
                        for half in range(2):
                            sg_, su_ = MOE_SLOT[2 * half], MOE_SLOT[2 * half + 1]
                            pe.wait_ge(slot_loaded[sg_], x * 16 + 16 * (FILLS[sg_] + 1))
                            pe.wait_ge(slot_loaded[su_], x * 16 + 16 * (FILLS[su_] + 1))
                            for k in range(KD // 2):
                                kk = half * (KD // 2) + k
                                for at, s in ((0, sg_), (CAP, su_)):
                                    ins = pe.matmul(PB[b][at:at + CAP, :], xgT[b][:, kk, :], slot(s, KD // 2)[:, k, :],
                                                    start=(kk == 0), stop=(kk == KD - 1))
                            ins.then_inc(gate_up_done, 1)
                        if b == 0:
                            pe.wait_ge(gathered[1], i * 16 + (R * 16 + 1) * 16)
                        else:
                            pe.wait_ge(gathered[0], i * 16 + (R * 17 + 2) * 16)
                        transpose_rows(1 - b)
                        pe.wait_ge(h_made, x + 2)
                        for f in range(KF):
                            ins = turn_64(PB[6][:, f * CAP:(f + 1) * CAP], hh[0:CAP, f * P:(f + 1) * P], f == 0)
                        ins.then_inc(hT_done, 1)
                        pe.wait_ge(hT_ready, x + 1)
                        pe.wait_ge(rows_ready, x + 1)
                        for half in range(2):
                            pe.wait_ge(slot_loaded[4 + half], x * 16 + 16)
                            for k in range(KF // 2):
                                f = half * (KF // 2) + k
                                for cc in range(4):
                                    at = (cc % 2) * CAP
                                    ins = pe.matmul(PB[2 + cc // 2][at:at + CAP, :], hT[:, f, :],
                                                    slot(4 + half, KF // 2)[:, k, cc * 512:(cc + 1) * 512],
                                                    start=(f == 0), stop=(f == KF - 1))
                            ins.then_inc(down_done, 1)

            run_rounds(pe, round_pe)

        @block.vector
        def _(dve):
            step = Chain(dve, dve_step)
            TS, TTo, STT = nc.vector.tensor_scalar, nc.vector.tensor_tensor, nc.vector.scalar_tensor_tensor
            nc.vector.memset(ones[:, :], 1.0)
            nc.vector.memset(eps_col[:, :], EPS).then_inc(dve_consts, 1)

            def token_rstd(rms, count, dst=3):
                dve.wait_ge(rms, count)
                step.add(nc.vector.reciprocal(token_stats[:, dst:dst + 2], token_stats[:, 0:2]))
                step.link(nc.vector.reciprocal(token_stats[0:TT[2], dst + 2:dst + 3], token_stats[0:TT[2], 2:3]))

            token_rstd(x_rms, 3)
            for tile in range(3):
                n = TT[tile]
                TS(xraw[0:n, tile, :], xraw[0:n, tile, :], token_stats[0:n, 3 + tile:4 + tile], None, ALU.mult) \
                    .then_inc(xn_made, 1)
            dve.wait_ge(vec_t, 1)
            nc.vector.tensor_copy(vecs[:, :], PB[7][:, 0:80]).then_inc(vec_copied, 1)
            dve.wait_ge(vec_copied, 1)

            def copy_transposed(dst, gain, done, copied):
                for tile in range(3):
                    n = TT[tile]
                    for q in range(KD // 4):
                        unit = tile * (KD // 4) + q
                        dve.wait_ge(done, unit + 1)
                        TTo(dst[:, 4 * q:4 * q + 4, tile * P:tile * P + n],
                            PB[unit % 4][:, :].rearrange("p (a n) -> p a n", a=4)[:, :, 0:n],
                            vecs[:, gain + 4 * q:gain + 4 * q + 4].unsqueeze(2).broadcast_to([P, 4, n]), ALU.mult) \
                            .then_inc(copied, 1)

            copy_transposed(xnT, V_MIX, xt_done, xt_copied)

            step.link(TTo(lb_tmp[:, 2, :], vecs[:, V_LB0:V_LB0 + 8], vecs[:, V_LB1:V_LB1 + 8], ALU.max))
            TTo(lb_tmp[:, 0, :], vecs[:, V_LB0:V_LB0 + 8], lb_tmp[:, 2, :], ALU.subtract)
            TTo(lb_tmp[:, 1, :], vecs[:, V_LB1:V_LB1 + 8], lb_tmp[:, 2, :], ALU.subtract).then_inc(lb_in, 1)

            R = [r5[0:NJ, q, :] for q in range(12)]
            two = [r.rearrange("p (a b) -> p a b", a=2) for r in R]
            stepc = R[2][:, 2:4].unsqueeze(2).broadcast_to([NJ, 2, P5])
            dve.wait_ge(s5_loaded, 16 * 11)
            dve.wait_ge(s5_exp, 1)
            TTo(two[10], two[0], stepc, ALU.mult).then_inc(s5_exp_in, 1)
            step.link(TTo(two[11], two[1], stepc, ALU.mult))
            step.link(TS(R[4], R[11], 1 / (2 * math.pi), MAGIC, ALU.mult, ALU.add))
            step.link(TS(R[4], R[4], MAGIC, None, ALU.subtract))
            step.link(STT(R[11], R[4], -TWO_PI_HI, R[11], ALU.mult, ALU.add))
            step.link(STT(R[4], R[4], -TWO_PI_LO, R[11], ALU.mult, ALU.add))
            step.link(TS(R[4], R[4], PI_BELOW, -PI_BELOW, ALU.min, ALU.max))
            step.link(TS(R[5], R[4], math.pi / 2, None, ALU.add))
            step.link(TS(R[11], R[5], PI_BELOW, -2 * math.pi, ALU.is_gt, ALU.mult))
            step.link(TTo(R[5], R[5], R[11], ALU.add))
            TS(R[5], R[5], PI_BELOW, -PI_BELOW, ALU.min, ALU.max).then_inc(s5_sin_in, 1)
            dve.wait_ge(lb_exp, 1)
            step.link(TTo(lb_tmp[:, 1, :], lb_tmp[:, 0, :], lb_tmp[:, 1, :], ALU.add))
            step.link(nc.vector.reciprocal(lb_tmp[:, 1, :], lb_tmp[:, 1, :]))
            step.link(TTo(lb[:, :], lb_tmp[:, 0, :], lb_tmp[:, 1, :], ALU.mult))
            step.link(TS(one_minus_lb[:, :], lb[:, :], -1.0, 1.0, ALU.mult, ALU.add))
            dve.wait_ge(s5_exp, 2)
            dve.wait_ge(s5_sin, 2)
            step.add(TS(R[5], R[4], 1 / (2 * math.pi), None, ALU.mult))
            step.add(TTo(R[8], R[3], R[7], ALU.mult))
            step.add(TTo(R[9], R[3], R[6], ALU.mult))
            step.add(TTo(R[10], R[0], R[0], ALU.mult))
            step.add(TTo(R[11], R[1], R[1], ALU.mult))
            step.settle()
            step.link(TTo(R[10], R[10], R[11], ALU.add))
            step.add(nc.vector.reciprocal(R[10], R[10]))
            step.link(TS(R[11], R[8], -1.0, None, ALU.add))
            step.add(TTo(R[6], R[11], R[0], ALU.mult))
            step.link(TTo(R[7], R[9], R[1], ALU.mult))
            step.link(TTo(R[6], R[6], R[7], ALU.add))
            step.add(TTo(R[6], R[6], R[10], ALU.mult))
            step.add(TTo(R[7], R[9], R[0], ALU.mult))
            step.link(TTo(R[11], R[11], R[1], ALU.mult))
            step.link(TTo(R[7], R[7], R[11], ALU.subtract))
            TTo(R[7], R[7], R[10], ALU.mult).then_inc(s5r_ready, 1)

            dve.wait_ge(pool_consts, 9)
            nc.vector.tensor_copy(mvals[:, 0:16], iota_i[:, 0:16])
            nc.vector.tensor_copy(mvals[:, 16:33], iota_i[:, 64:81])
            nc.vector.tensor_copy(iota32, iota_i[:, 0:NE])
            nc.vector.tensor_copy(slotid, iota_i[:, 0:CAP])
            nc.vector.tensor_copy(tid, iota_i[:, 81:84])
            step.add(TTo(iX, iI, iJ, ALU.bitwise_xor))
            step.add(TTo(mG, iI, iJ, ALU.is_gt))
            step.add(TTo(masks[:, 7, :], iI, iJ, ALU.is_equal))
            step.link(TS(parity[:, 2:3].bitcast(I32), iJ[:, 0:1], 16, None, ALU.bitwise_and))
            step.link(nc.vector.tensor_copy(mX, iX))
            step.link(STT(mX, mX, 1.0, mG, ALU.add, ALU.mult))
            step.add(TS(mX, mX, -1.0, None, ALU.add))
            step.link(nc.vector.tensor_copy(parity[:, 1:2], parity[:, 2:3].bitcast(I32)))
            step.link(TS(parity[:, 1:2], parity[:, 1:2], 1.0 / 16, None, ALU.mult))
            step.link(TS(parity[:, 0:1], parity[:, 1:2], -1.0, 1.0, ALU.mult, ALU.add))
            for l, B in enumerate(LV):
                step.link(TS(mL, mX, 2.0 * B, None, ALU.is_lt))
                step.link(STT(masks[:, l, :], mX, float(B), mL, ALU.is_ge, ALU.mult))

            for z in range(2):
                for half in range(2):
                    TS(CP[z][:, :, half, :], Craw[z], parity[:, half:half + 1], 1.0 if z == 0 else -1.0, ALU.mult, ALU.mult)
            for z in range(2):
                step.add(nc.vector.memset(BP[z], 0.0))

            dve.wait_ge(par_t, 2)
            step.link(nc.vector.tensor_copy(sc5[:, :, :], PB[7][:, P:P + 6 * NJ].rearrange("p (a n) -> p a n", a=6)))
            dec = [sc5[:, q, :].unsqueeze(1).broadcast_to([P, NS, NJ]) for q in (2, 3)]
            h0 = [PB[6][:, z * 2 * P:(z + 1) * 2 * P].rearrange("p (a n) -> p a n", a=NS) for z in range(2)]
            step.add(TTo(Zs[:, 0], h0[0], dec[0], ALU.mult))
            step.add(TTo(z_tmp[0], h0[1], dec[1], ALU.mult))
            step.add(TTo(Zs[:, 1], h0[1], dec[0], ALU.mult))
            step.add(TTo(z_tmp[1], h0[0], dec[1], ALU.mult))
            step.link(TTo(ang_r, sc5[:, 1, :].unsqueeze(2).broadcast_to([P, NJ, 33]),
                          mvals.unsqueeze(1).broadcast_to([P, NJ, 33]), ALU.mult))
            nc.vector.tensor_copy(parity[:, 2:3], parity[:, 1:2]).then_inc(par_copied, 2)
            step.add(TTo(Zs[:, 0], Zs[:, 0], z_tmp[0], ALU.subtract))
            step.add(TTo(Zs[:, 1], Zs[:, 1], z_tmp[1], ALU.add))
            step.link(TS(ang_n, ang_r, MAGIC, MAGIC, ALU.add, ALU.subtract))
            step.link(TTo(ang_sin, ang_r, ang_n, ALU.subtract))
            TS(ang_sin, ang_sin, 0.5, -0.5, ALU.min, ALU.max).then_inc(ang_ready, 1)
            step.link(TS(ang_r, ang_r, 0.25, None, ALU.add))
            step.link(TS(ang_n, ang_r, MAGIC, MAGIC, ALU.add, ALU.subtract))
            step.link(TTo(ang_cos, ang_r, ang_n, ALU.subtract))
            TS(ang_cos, ang_cos, 0.5, -0.5, ALU.min, ALU.max).then_inc(ang_ready, 1)
            fr, fi = (sc5[:, q, :].unsqueeze(2).broadcast_to([P, NJ, C5]) for q in (4, 5))
            for z in range(2):
                step.add(TTo(Btmp[0], fr, Braw[z], ALU.mult))
                step.link(TTo(Btmp[1], fi, Braw[1 - z], ALU.mult))
                op = ALU.subtract if z == 0 else ALU.add
                pad = BP[z].rearrange("p i (a g c) -> p (i a) g c", a=4, g=2)
                for g in range(2):
                    rows = slice(64 * g, 64 * g + 64)
                    ins = TTo(pad[rows, :, g, :], Btmp[0][rows], Btmp[1][rows], op)
                    if z == 1 and g == 1:
                        ins.then_inc(mat_ready, 1)
                    else:
                        step.add(ins)
                step.settle()
            nc.vector.tensor_copy(parity[:, 2:3], parity[:, 1:2]).then_inc(mat_ready, 1)
            dve.wait_ge(table_ready, 2)
            for n in range(2):
                for z in range(2):
                    for q in range(2):
                        dve.wait_ge(mat_t, 4 * n + 2 * z + q + 1)
                        nc.vector.tensor_copy((BT, CT)[n][z][:, 4 * q:4 * q + 4, :],
                                              PB[4 + 2 * z + q][:, :].rearrange("p (a n) -> p a n", a=4)).then_inc(mat_copied, 1)

            for j in range(NJ):
                b = j % 2
                re, im = PB[4], PB[5]
                cos, sin = turn[b][:, 0], turn[b][:, 1]
                dve.wait_ge(bu_done, j + 1)
                dve.wait_ge(turn_ready, j + 1)
                if j >= 2:
                    dve.wait_ge(h_used, j - 1)
                    dve.wait_ge(fin_copied, j - 1)
                if j >= 1:
                    dve.wait_ge(h_ready, j)
                step.add(TTo(M1[:, 0], re[:, 0:TP], cos, ALU.mult))
                step.add(TTo(M1[:, 1], im[:, 0:TP], cos, ALU.mult))
                step.add(TTo(M2[:, 0], im[:, 0:TP], sin, ALU.mult))
                step.add(TTo(M2[:, 1], re[:, 0:TP], sin, ALU.mult))
                step.add(TTo(Hst[b][:, 0, TP:T], re[:, TP:T], Zs[:, 0, :, j], ALU.add))
                TTo(Hst[b][:, 1, TP:T], im[:, TP:T], Zs[:, 1, :, j], ALU.add).then_inc(bu_read, 1)
                step.settle()
                step.add(TTo(Wt[:, 0], M1[:, 0], M2[:, 0], ALU.add))
                step.link(TTo(Wt[:, 1], M1[:, 1], M2[:, 1], ALU.subtract))
                for z in range(2):
                    step.add(nc.vector.tensor_tensor_scan(Gs[:, z], sc5[:, 0, j:j + 1].broadcast_to([P, TP]), Wt[:, z], 0.0,
                                                          ALU.mult, ALU.add))
                step.settle()
                step.add(TTo(M1[:, 0], Gs[:, 0], cos, ALU.mult))
                step.add(TTo(M1[:, 1], Gs[:, 1], cos, ALU.mult))
                step.add(TTo(M2[:, 0], Gs[:, 1], sin, ALU.mult))
                step.add(TTo(M2[:, 1], Gs[:, 0], sin, ALU.mult))
                step.settle()
                TTo(Hst[b][:, 0, 0:TP], M1[:, 0], M2[:, 0], ALU.subtract).then_inc(turn_used, 1)
                TTo(Hst[b][:, 1, 0:TP], M1[:, 1], M2[:, 1], ALU.add).then_inc(h_ready, 1)
                if j % 4 == 3:
                    i = j // 4
                    dve.wait_ge(h_used, j + 1)
                    STT(uT[:, i, :], uT[:, i, :], vecs[:, V_D + i:V_D + i + 1], PB[6][:, 0:T], ALU.mult, ALU.add) \
                        .then_inc(y5_ready, 1)

            dve.wait_ge(proj_read, 2 * NW)
            for h in range(NH):
                step.add(TS(GT[:, h, :], GT[:, h, :], one_minus_lb[:, h:h + 1], lb[:, h:h + 1], ALU.mult, ALU.add))
            step.settle()
            step.add(nc.vector.tensor_copy(fs[:, :, :], GT[:, :, TP:T]))
            for h in range(NH):
                TS(kT[:, h, :], GT[:, h, :], -1.0, 1.0, ALU.mult, ALU.add).then_inc(k_ready, 1)
            dve.wait_ge(k_ready, NH)
            step.add(nc.vector.tensor_copy(ks[:, :, :], kT[:, :, TP:T]))
            step.add(nc.vector.tensor_copy(qs[:, :, :], qT[:, :, TP:T]))
            dve.wait_ge(fin_copied, NJ)
            for b in range(2):
                step.add(nc.vector.memset(att[b], 0.0))
            step.settle()
            dve.wait_ge(lnf_done, 1)
            for h in range(NH):
                for c0, n in CHUNKS:
                    ins = nc.vector.tensor_tensor_scan(GT[:, h, c0:c0 + n], ones[:, 0:1].broadcast_to([P, n]),
                                                       GT[:, h, c0:c0 + n], 0.0, ALU.mult, ALU.add)
                ins.then_inc(G_ready, 1)
            for h in range(NH):
                b = h % 2
                dve.wait_ge(exp_ready, h + 1)
                for l, B in enumerate(LV):
                    o = QK[b][:, LO[l]:LO[l] + LW[l]].rearrange("p (n two b) -> p n two b", two=2, b=B)
                    for side, src in ((0, kT), (1, qT)):
                        s = src[:, h, 0:LW[l]].rearrange("p (n two b) -> p n two b", two=2, b=B)
                        TTo(o[:, :, side, :], o[:, :, side, :], s[:, :, side, :], ALU.mult)
                TTo(qG[b], qG[b], qT[:, h, 0:TP], ALU.mult)
                TTo(kG[b], kG[b], kT[:, h, 0:TP], ALU.mult).then_inc(qk_ready, 1)
                dve.wait_ge(vb_done, h + 1)
                if h >= 1:
                    dve.wait_ge(S1_ready, h)
                for z in range(2):
                    step.add(TTo(vk[:, 4 * z:4 * z + 4, :], PB[z][:, :].rearrange("p (a n) -> p a n", a=4),
                                 ks[:, 4 * z:4 * z + 4, h:h + 1].broadcast_to([P, 4, P]), ALU.mult))
                step.settle()
                dve.wait_ge(S0_decayed, h + 1)
                TTo(S0[h % 3], S0[h % 3], vk, ALU.add).then_inc(S1_ready, 1)
                for l in range(8):
                    u = 8 * h + l
                    dve.wait_ge(att_done, u + 1)
                    if u:
                        dve.wait_ge(att_read, u)
                    bank = PB[4 + l % 2]
                    ins = nc.vector.copy_predicated(att[b][:, 0:2 * P].rearrange("p (a n) -> p a n", a=2),
                                                    masks[:, l, :].unsqueeze(1).broadcast_to([P, 2, P]),
                                                    bank[:, 0:2 * P].rearrange("p (a n) -> p a n", a=2))
                    if l >= 3:
                        ins = nc.vector.copy_predicated(att[b][0:LAST, 2 * P:TP], masks[0:LAST, l, 0:LAST],
                                                        bank[0:LAST, 2 * P:TP])
                    ins.then_inc(att_read, 1)
                dve.wait_ge(st_done, h + 1)
                if h >= 2:
                    dve.wait_ge(st_stored[b], 16 * (h // 2))
                for q in range(3):
                    part = PB[3][:, q * P:(q + 1) * P]
                    if q == 0:
                        ins = nc.vector.tensor_copy(Sst[b][:, 0, :], part)
                    else:
                        dve.wait_ge(st_ready, 3 * h + q)
                        ins = STT(Sst[b][:, q, :], Sst[b][:, q - 1, :], chunk_decay[b][:, q - 1:q], part, ALU.mult, ALU.add)
                    ins.then_inc(st_ready, 1)

            dve.wait_ge(glu_read, NH)
            TTo(uT, uT, sgT, ALU.mult).then_inc(y5g_ready, 1)
            dve.wait_ge(os_done, NS)
            nc.vector.tensor_copy(kT[:, :, TP:T], PB[7][:, 3 * P:3 * P + NH * NS].rearrange("p (h b) -> p h b", h=NH)) \
                .then_inc(samp_copied, 1)
            dve.wait_ge(rt_ready, 1)
            step.link(nc.vector.reciprocal(rms5, rms5))
            for i in range(N5):
                ins = STT(uT[:, i, :], uT[:, i, :], vecs[:, V_G5 + i:V_G5 + i + 1], rms5, ALU.mult, ALU.mult)
            ins.then_inc(yT_ready, 1)
            dve.wait_ge(rt_ready, 1 + NH)
            step.link(nc.vector.reciprocal(GT, GT))
            for h in range(NH):
                step.add(STT(kT[:, h, :], kT[:, h, :], vecs[:, V_GH + h:V_GH + h + 1], GT[:, h, :], ALU.mult, ALU.mult))
            step.settle()
            TTo(gT, gT, kT, ALU.mult).then_inc(yT_ready, 1)

            dve.wait_ge(x_again, 16 * 5)
            for o in range(NO):
                for b in range(2):
                    unit = 2 * o + b
                    dve.wait_ge(out_done, unit + 1)
                    cols = slice(o * CB, (o + 1) * CB)
                    if b == 0:
                        x_, p_ = x1[:, 0:2, cols], PB[unit % 4][:, 0:2 * CB].rearrange("p (a n) -> p a n", a=2)
                    else:
                        x_, p_ = x1[0:TT[2], 2, cols], PB[unit % 4][0:TT[2], 0:CB]
                    TTo(x_, x_, p_, ALU.add).then_inc(x1_ready, 1)

            dve.wait_ge(r_rms, 3)
            step.add(nc.vector.reciprocal(token_stats[:, 3:5], token_stats[:, 0:2]))
            nc.vector.reciprocal(token_stats[0:TT[2], 5:6], token_stats[0:TT[2], 2:3]).then_inc(r_rstd, 1)
            for b in range(3):
                dve.wait_ge(S0_stored[b], 16 * len(range(b, NS, 3)))
            copy_transposed(xn2T, V_FFN, xt2_done, xt2_copied)

            step.add(nc.vector.memset(lg, 0.0))
            step.add(nc.vector.memset(c8, LOWEST))
            dve.wait_ge(wr_loaded, 64)
            dve.wait_ge(logit_done, 1)
            step.settle()
            NL = NG + NE
            step.add(TTo(lg[:, 0:2, :], PB[6][:, 0:2 * NL].rearrange("p (a n) -> p a n", a=2),
                         bias36.unsqueeze(1).broadcast_to([P, 2, NL]), ALU.add))
            step.link(TTo(lg[0:TT[2], 2, :], PB[6][0:TT[2], 2 * NL:3 * NL], bias36[0:TT[2], :], ALU.add))
            step.link(nc.vector.tensor_copy(c8[:, :, 0:NG], lg[:, :, 0:NG]))
            for tile in range(3):
                step.add(nc.vector.max(out=gmax[:, tile, :], in_=c8[:, tile, :]))
            step.settle()
            for tile in range(3):
                step.add(nc.vector.max_index(out=gidx[:, tile, :], in_max=gmax[:, tile, :], in_values=c8[:, tile, :]))
            TTo(e8, lg[:, :, 0:NG], gmax[:, :, 0:1].broadcast_to([P, 3, NG]), ALU.subtract).then_inc(sm_in, 1)
            step.settle()
            step.link(nc.vector.tensor_copy(grp, gidx[:, :, 0]))
            step.link(TTo(ohg, iota32[:, 0:NG].unsqueeze(1).broadcast_to([P, 3, NG]),
                          grp.unsqueeze(2).broadcast_to([P, 3, NG]), ALU.is_equal))
            for tile in range(3):
                step.add(TTo(pick[:, tile], lg[:, tile, NG:NL].rearrange("p (g j) -> p g j", g=NG),
                             ohg[:, tile, :].unsqueeze(2).broadcast_to([P, NG, EG]), ALU.mult))
            step.settle()
            for tile in range(3):
                step.add(nc.vector.tensor_reduce(f8[:, tile, :], pick[:, tile].rearrange("p g j -> p j g"), AX.X, ALU.add))
            step.settle()
            for tile in range(3):
                step.add(nc.vector.max(out=fmax[:, tile, :], in_=f8[:, tile, :]))
            step.settle()
            for tile in range(3):
                step.add(nc.vector.max_index(out=fidx[:, tile, :], in_max=fmax[:, tile, :], in_values=f8[:, tile, :]))
            step.settle()
            TTo(dv, fmax[:, :, 1], fmax[:, :, 0], ALU.subtract).then_inc(sm_in, 1)
            step.add(nc.vector.tensor_copy(e0, fidx[:, :, 0]))
            step.link(nc.vector.tensor_copy(e1, fidx[:, :, 1]))
            step.add(STT(e0, grp, float(EG), e0, ALU.mult, ALU.add))
            step.add(STT(e1, grp, float(EG), e1, ALU.mult, ALU.add))
            step.link(TS(valid, tid, float(T), None, ALU.is_lt))
            for o_, e_ in ((OH0, e0), (OH1, e1)):
                step.add(TTo(o_, iota32.unsqueeze(1).broadcast_to([P, 3, NE]), e_.unsqueeze(2).broadcast_to([P, 3, NE]), ALU.is_equal))
            step.settle()
            for o_ in (OH0, OH1):
                step.add(TTo(o_, o_, valid.unsqueeze(2).broadcast_to([P, 3, NE]), ALU.mult))
            step.settle()
            TTo(Mr, OH0, OH1, ALU.add).then_inc(route_ready, 1)
            dve.wait_ge(sm_exp, 2)
            step.add(nc.vector.tensor_reduce(pgi, e8, AX.X, ALU.add))
            step.link(TS(w0, dv, 1.0, None, ALU.add))
            step.link(TTo(w0, w0, pgi, ALU.mult))
            step.link(nc.vector.reciprocal(w0, w0))
            step.link(TTo(w1, w0, dv, ALU.mult))
            step.add(nc.vector.memset(PL, 0.0))
            step.add(nc.vector.memset(rankm, -1.0))
            step.settle()
            tidb = tid.unsqueeze(2).broadcast_to([P, 3, NE])
            step.add(TTo(pick.rearrange("p a g j -> p a (g j)"), OH0, w0.unsqueeze(2).broadcast_to([P, 3, NE]), ALU.mult))
            step.add(TTo(PL[:, :, 0:NE, 2], OH1, w1.unsqueeze(2).broadcast_to([P, 3, NE]), ALU.mult))
            step.add(TS(PL[:, :, 0:NE, 0], tidb, -BIG, None, ALU.add))
            step.link(STT(PL[:, :, 0:NE, 1], OH1, float(T), tidb, ALU.mult, ALU.add))
            step.add(TTo(PL[:, :, 0:NE, 2], PL[:, :, 0:NE, 2], pick.rearrange("p a g j -> p a (g j)"), ALU.add))
            step.link(TS(PL[:, :, 0:NE, 1], PL[:, :, 0:NE, 1], -BIG, None, ALU.add))
            dve.wait_ge(rank_done, 1)
            step.add(TTo(rankm[:, :, 0:NE], PB[7][:, 0:3 * NE].rearrange("p (a n) -> p a n", a=3), Mr, ALU.mult))
            step.link(nc.vector.tensor_reduce(maxn, PB[7][:, 3 * NE:4 * NE], AX.X, ALU.max))
            step.add(TTo(rankm[:, :, 0:NE], rankm[:, :, 0:NE], Mr, ALU.add))
            for r in range(1, ROUNDS):
                step.add(TS(ext[:, r - 1:r], maxn, float(CAP * r), None, ALU.is_gt))
            step.settle()
            step.add(TS(rankm[:, :, 0:NE], rankm[:, :, 0:NE], -1.0, None, ALU.add))
            step.link(nc.vector.tensor_reduce(maxn, ext, AX.X, ALU.add))
            nc.vector.tensor_copy(extra_i[:, :], maxn).then_inc(lists_ready, 1)
            nc.vector.engine_nop().then_inc(h_made, 1)
            dve.wait_ge(lists_ready, 1)

            def places(e):
                TTo(oh[:, :, :], rankm[:, :, bass.ds(e, 1)].broadcast_to([P, 3, CAP]),
                    slotid.unsqueeze(1).broadcast_to([P, 3, CAP]), ALU.is_equal).then_inc(oh_ready, 1)

            def indices(g, p):
                dve.wait_ge(list_done, g + 1)
                TS(idx_tok[p][:, :], PB[7][0:CAP, 0:1], BIG, None, ALU.add)
                TS(idx_dst[p][:, :], PB[7][0:CAP, 1:2], BIG, None, ALU.add)
                nc.vector.tensor_copy(gcol[p][:, :], PB[7][0:CAP, 2:3]).then_inc(idx_ready, 1)

            def rows_in(g, p):
                dve.wait_ge(tr_done, g + 2)
                for q in range(2):
                    ins = TTo(xgT[p][:, 8 * q:8 * q + 8, :], PB[4 + q][:, :].rearrange("p (a n) -> p a n", a=8),
                              vecs[:, V_FFN + 8 * q:V_FFN + 8 * q + 8].unsqueeze(2).broadcast_to([P, 8, CAP]), ALU.mult)
                ins.then_inc(xgT_ready, 1)

            def round_dve(R):
                g0 = R * (NE + 1)
                if not is_first(R):
                    dve.wait_ge(list_done, g0)
                    TS(rankm, rankm, -float(CAP), None, ALU.add).then_inc(lists_ready, 1)
                    dve.wait_ge(lists_ready, R + 1)
                    dve.wait_ge(rows_free, R * NE + 2)
                places(0)
                indices(g0, 0)
                rows_in(g0, 0)
                with dve.Fori(0, NE // 2) as i:
                    for b in range(2):
                        x = i * 2 + (R * NE + b)
                        g = i * 2 + (R * (NE + 1) + b + 1)
                        dve.wait_ge(list_done, g)
                        places(i * 2 + (b + 1))
                        dve.wait_ge(rows_free, x + 2)
                        indices(g, 1 - b)
                        dve.wait_ge(act_ready, x + 1)
                        STT(hh[0:CAP, :], sg[0:CAP, :], gcol[b][:, 0:1], up[0:CAP, :], ALU.mult, ALU.mult).then_inc(h_made, 1)
                        dve.wait_ge(hT_done, x + 1)
                        nc.vector.tensor_copy(hT, PB[6][:, 0:KF * CAP].rearrange("p (a n) -> p a n", a=KF)).then_inc(hT_ready, 1)
                        rows_in(g, 1 - b)

            run_rounds(dve, round_dve)
            dve.wait_ge(moe_done, 1)
            dve.wait_ge(gfin_loaded, 16)
            for tile in range(3):
                n = TT[tile]
                dve.wait_ge(yrow_loaded[tile % 2], 32 * (tile // 2 + 1))
                y0, y1 = yrow[2 * (tile % 2)], yrow[2 * (tile % 2) + 1]
                xt = x1[0:n, tile, :]
                step.link(TTo(xt, xt, y0[0:n, :], ALU.add))
                TTo(xt, xt, y1[0:n, :], ALU.add).then_inc(ysum_done, 1)
                dve.wait_ge(f_rms, tile + 1)
                r = token_stats[0:n, 3 + tile:4 + tile]
                step.link(nc.vector.reciprocal(r, token_stats[0:n, tile:tile + 1]))
                STT(xt, xt, r, gfin[0:n, :], ALU.mult, ALU.mult).then_inc(out_ready, 1)


_INS = ['x_prompt', 'x_sample', 'state_s5_re', 'state_s5_im', 'state_hgrn', 'meta_tokens', 'norm_mix', 'w_in',
        's5_A_re', 's5_A_im', 's5_log_step', 's5_B_re', 's5_B_im', 's5_C_re', 's5_C_im', 's5_D', 's5_w_glu',
        's5_b_glu', 's5_out_gain', 'hg_lb_logits', 'hg_out_gain', 'w_out', 'norm_ffn', 'w_coarse', 'b_coarse',
        'w_fine', 'b_fine', 'w_gate', 'w_up', 'w_down', 'norm_final']
_OUTS = ['y_prompt', 'y_sample', 's5_re_prompt', 's5_im_prompt', 'hgrn_prompt', 's5_re_sample', 's5_im_sample',
         'hgrn_sample']


def kernel(**inputs):
    import numpy as _np
    import concourse.bacc as _bacc
    from concourse import mybir as _mybir
    from concourse.bass_utils import run_bass_kernel_spmd as _run

    nc = _bacc.Bacc("TRN2", target_bir_lowering=False, num_devices=1)
    arrays, args = {}, {}
    for name in _INS:
        a = _np.ascontiguousarray(inputs[name])
        arrays[f"in_{name}_dram"] = a
        args[name] = nc.dram_tensor(f"in_{name}_dram", a.shape, _mybir.dt.from_np(a.dtype), kind="ExternalInput").ap()
    g5, p5 = inputs["s5_A_re"].shape[1:]
    nh, dk, dv = inputs["state_hgrn"].shape[2:]
    ns = inputs["x_sample"].shape[0]
    shapes = [inputs["x_prompt"].shape, inputs["x_sample"].shape, (1, 1, g5, p5), (1, 1, g5, p5),
              (1, 1, nh, dk, dv), (1, ns, g5, p5), (1, ns, g5, p5), (1, ns, nh, dk, dv)]
    for name, shape in zip(_OUTS, shapes):
        args[name] = nc.dram_tensor(f"out_{name}_dram", shape, _mybir.dt.float32, kind="ExternalOutput").ap()
    hymba_step(nc, args)
    r = _run(nc, [arrays], core_ids=[0])
    return tuple(r.results[0][f"out_{name}_dram"] for name in _OUTS)
```

```python
import math
from contextlib import ExitStack

import concourse.bass as bass
from concourse import mybir

F32 = mybir.dt.float32
I32 = mybir.dt.int32
U32 = mybir.dt.uint32
U8 = mybir.dt.uint8
ALU = mybir.AluOpType
ACT = mybir.ActivationFunctionType
AX = mybir.AxisListType

P = 128
EPS = 1e-6
MAGIC = 1.5 * 2.0 ** 23
TWO_PI_HI = 6.28125
TWO_PI_LO = 2 * math.pi - TWO_PI_HI
PI_BELOW = 3.1415925
BIG = 1024.0
LOWEST = -3.0e38


class Chain:

    def __init__(self, eng, sem):
        self.eng, self.sem, self.n = eng, sem, 0

    def add(self, ins):
        ins.then_inc(self.sem, 1)
        self.n += 1

    def settle(self):
        self.eng.wait_ge(self.sem, self.n)

    def link(self, ins):
        self.add(ins)
        self.settle()


def hymba_step(nc, t):
    SEQ, D = t["x_prompt"].shape[1:]
    NS = t["x_sample"].shape[0]
    NM = t["meta_tokens"].shape[0]
    TP = NM + SEQ
    T = TP + NS
    TT = [P, P, T - 2 * P]
    KD = D // P
    G5, P5, C5 = t["s5_B_re"].shape[1:]
    W5 = G5 * C5
    N5 = W5 // P
    NJ = G5 * P5 // P
    HG = t["hg_out_gain"].shape[1]
    NH = HG // P
    NE, _, FH = t["w_gate"].shape[1:]
    NG = t["w_coarse"].shape[2]
    EG = NE // NG
    KF = FH // P
    CB = 256
    CAP = 64
    ROUNDS = -(-T // CAP)
    LAST = TP - 2 * P
    assert D == 2 * W5 == 2 * HG and NE % 2 == 0 and T <= 3 * P and NS == NH and TT[2] == LAST + NS

    ctx = ExitStack()
    with ctx:
        def sb(name, shape, dt=F32):
            return ctx.enter_context(nc.sbuf_tensor(name, shape, dt))

        def sem(name):
            return ctx.enter_context(nc.semaphore(name))

        SLOT = KD * CB
        ring = sb("ring", [P, 6, SLOT])
        AR_N = 5 * N5 * T + KD * T + 2 * 33 * NJ + 8536
        arena = sb("arena", [P, AR_N])
        ident = sb("ident", [P, P])
        ones = sb("ones", [P, P])
        upper = sb("upper", [P, P])
        vecs = sb("vecs", [P, 80])
        sc5 = sb("sc5", [P, 6, NJ])
        masks = sb("masks", [P, 8, P], U8)
        eps_col = sb("eps_col", [P, 1])
        token_stats = sb("token_stats", [P, 8])
        lb, one_minus_lb, lb_tmp = sb("lb", [P, NH]), sb("one_minus_lb", [P, NH]), sb("lb_tmp", [P, 3, NH])
        parity = sb("parity", [P, 3])
        fs, ks = (sb(n, [P, NH, NS]) for n in ("f_samples", "k_samples"))
        chunk_decay = [sb(f"chunk_decay{i}", [P, 2]) for i in range(2)]

        class Carver:
            def __init__(self, base, at):
                self.base, self.at = base, at

            def __call__(self, *shape):
                n = math.prod(shape)
                v = self.base[:, self.at:self.at + n]
                self.at += n
                if len(shape) > 1:
                    names = "abcd"[:len(shape)]
                    v = v.rearrange(f"p ({' '.join(names)}) -> p {' '.join(names)}",
                                    **{n_: s for n_, s in zip(names, shape)})
                return v

        upair = ring[:, 4:6, :].rearrange("p a n -> p (a n)")

        c = Carver(arena, 0)
        uT, gT = c(N5, T), c(NH, T)
        gT_at, x1_at = N5 * T, c.at
        qT, GT, kT = c(NH, T), c(NH, T), c(NH, T)
        xnT_at = c.at
        xnT = c(KD, T)
        tab_at = c.at
        turn_table = c(2, NJ, 33)
        rest_at = c.at
        c = Carver(arena, rest_at)
        turn = [c(2, TP), c(2, TP)]
        turn_tmp = [c(2, TP), c(2, TP)]
        M1, M2, Wt, Gs = c(2, TP), c(2, TP), c(2, TP), c(2, TP)
        NHST = 3
        Hst = [c(2, T) for _ in range(NHST)]
        assert c.at <= rest_at + 7168
        c = Carver(arena, rest_at)
        Braw, BP = [c(NJ, C5), c(NJ, C5)], [c(N5, P), c(N5, P)]
        Craw, CP = [c(N5, P5), c(N5, P5)], [c(N5, 2, P5), c(N5, 2, P5)]
        Btmp = [c(NJ, C5), c(NJ, C5)]
        assert c.at == rest_at + 7168
        Zs, fin = c(2, NS, NJ), c(2, 1 + NS, NJ)
        rms5 = c(T)
        assert c.at <= AR_N
        LV = [64, 32, 16, 8, 4, 2, 1]
        LW = [TP if b <= 8 else 2 * P for b in LV]
        LO = [sum(LW[:i]) for i in range(len(LV))]
        c = Carver(arena, rest_at)
        QK = [c(sum(LW)), c(sum(LW))]
        att, qG, kG = ([c(TP), c(TP)] for _ in range(3))
        kGt, Sst = ([c(3, P), c(3, P)] for _ in range(2))
        assert c.at <= rest_at + 7168
        c = Carver(arena, tab_at)
        S0_last, vk = c(NH, P), c(NH, P)
        assert c.at <= rest_at
        c = Carver(arena, xnT_at)
        fin_rows, o_rows = c(2, 3, P), c(2, P)
        c = Carver(arena, gT_at)
        vrow, h0row, r5 = c(P), c(2, 2, P), c(12, P)
        assert c.at <= x1_at
        xraw = Carver(arena, x1_at)(3, D)
        c = Carver(upair, 0)
        v_tok = c(3, HG)
        mat_at = c.at
        BT, CT = [c(N5, P), c(N5, P)], [c(N5, P), c(N5, P)]
        v_part = c(4, CB)
        assert c.at <= 2 * SLOT
        c = Carver(upair, mat_at)
        sgT = c(N5, T)
        S0 = [c(NH, P), c(NH, P), S0_last]
        q_own = c(NH, NS, NS)
        assert c.at <= 2 * SLOT
        c = Carver(upair, 0)
        xsq = c(D)
        ang_r, ang_n, ang_cos, ang_sin = (c(NJ, 33) for _ in range(4))
        z_tmp = [c(NS, NJ), c(NS, NJ)]
        assert c.at <= 2 * SLOT
        c = Carver(arena, tab_at)
        iI, iJ, iX, iota_i = (c(P).bitcast(I32) for _ in range(4))
        mX, mG, mL = c(P), c(P), c(P)
        c = Carver(arena, x1_at)
        x1, wr = c(3, D), c(KD, NG + NE)
        assert c.at <= xnT_at
        xn2T = Carver(arena, xnT_at)(KD, T)
        oh = Carver(arena, xnT_at)(3, CAP)
        c = Carver(arena, tab_at)
        xn_rows = c(3, D)
        c = Carver(arena, tab_at)
        _, xg0, xg1 = c(D), c(D), c(D)
        xg = [xg0, xg1]
        yout = [c(D), c(D)]
        assert c.at <= AR_N
        c = Carver(arena, 0)
        xgT = [c(KD, CAP), c(KD, CAP)]
        sg, up, hh = c(FH), c(FH), c(FH)
        hT = c(KF, CAP)
        lg, c8, e8, pick, f8 = c(3, NG + NE), c(3, 8), c(3, NG), c(3, NG, EG), c(3, EG)
        OH0, OH1, Mr = c(3, NE), c(3, NE), c(3, NE)
        assert c.at <= x1_at
        gfin = Carver(arena, tab_at)(D)
        yrow = [Carver(arena, tab_at + D * (1 + i))(D) for i in range(4)]
        junk = Carver(arena, xnT_at)(D)
        route = sb("route", [P, 608])
        c = Carver(route, 0)
        bias36 = c(NG + NE)
        tid, valid, pgi, dv, w0, w1, grp, e0, e1 = (c(3) for _ in range(9))
        ohg = c(3, NG)
        iota32, slotid = c(NE), c(CAP)
        rankm = c(3, NE + 1)
        PL = c(3, NE + 1, 3)
        maxn, ext, mvals = c(1), c(ROUNDS - 1), c(33)
        assert c.at <= 608
        gmax, fmax = sb("gmax", [P, 3, 8]), sb("fmax", [P, 3, 8])
        gidx, fidx = sb("gidx", [P, 3, 8], U32), sb("fidx", [P, 3, 8], U32)
        extra_i = sb("extra_i", [P, 1], I32)
        idx_tok = [sb(f"idx_tok{i}", [CAP, 1], U32) for i in range(2)]
        idx_dst = [sb(f"idx_dst{i}", [CAP, 1], U32) for i in range(2)]
        gcol = [sb(f"gcol{i}", [CAP, 1]) for i in range(2)]

        PB = [ctx.enter_context(nc.psum_tensor(f"bank{i}", [P, 512], F32)) for i in range(8)]
        xn_dram = nc.dram_tensor("xn_rows", [T, D], F32, kind="Internal").ap()
        v_dram = nc.dram_tensor("v_samples", [NS, HG], F32, kind="Internal").ap()
        y_dram = nc.dram_tensor("expert_rows", [2 * T, D], F32, kind="Internal").ap()

        V_MIX, V_FFN, V_D, V_BGLU, V_G5, V_LB0, V_LB1, V_GH = 0, KD, 32, 40, 48, 56, 64, 72

        def sems(names):
            return [sem(n) for n in names.split()]

        x_loaded, vec_loaded, s5_loaded, wr_loaded = sems("x_loaded vec_loaded s5_loaded wr_loaded")
        slot_loaded = [sem(f"slot_loaded{i}") for i in range(6)]
        pool_consts, dve_consts, act_step, dve_step, pool_step = sems("pool_consts dve_consts act_step dve_step pool_step")
        x_rms, xn_made, xt_done, xt_copied, vec_t, vec_copied = sems("x_rms xn_made xt_done xt_copied vec_t vec_copied")
        lb_in, lb_exp = sems("lb_in lb_exp")
        s5_exp_in, s5_exp, s5_sin_in, s5_sin, s5r_ready = sems("s5_exp_in s5_exp s5_sin_in s5_sin s5r_ready")
        par_t, par_copied, ang_ready, table_ready = sems("par_t par_copied ang_ready table_ready")
        mat_ready, mat_t, mat_copied = sems("mat_ready mat_t mat_copied")
        proj_done, proj_read, v_summed, g_done, g_read, silu_done = sems(
            "proj_done proj_read v_summed g_done g_read silu_done")
        bu_done, bu_read, turn_ready, turn_used = sems("bu_done bu_read turn_ready turn_used")
        h_ready, h_used, y_done, y5_ready, fin_copied = sems("h_ready h_used y_done y5_ready fin_copied")
        gelu_done, k_ready, lnf_done, G_ready = sems("gelu_done k_ready lnf_done G_ready")
        diff_ready, exp_ready, qk_ready, att_done, att_read = sems("diff_ready exp_ready qk_ready att_done att_read")
        kgt_done, kgt_copied, st_done, st_ready, o_done, o_copied = sems("kgt_done kgt_copied st_done st_ready o_done o_copied")
        S0_loaded = [sem(f"S0_loaded{i}") for i in range(3)]
        S0_stored = [sem(f"S0_stored{i}") for i in range(3)]
        st_stored = [sem(f"st_stored{i}") for i in range(2)]
        S0_decayed, v_stored, v_spread, S1_ready, os_done = sems("S0_decayed v_stored v_spread S1_ready os_done")
        os_copied, os_turned, samp_copied = sems("os_copied os_turned samp_copied")
        glu_done, glu_read, y5g_ready, sq_ready, ss_done, rt_ready, yT_ready = sems(
            "glu_done glu_read y5g_ready sq_ready ss_done rt_ready yT_ready")
        fin_t, fin_read, fin_stored = sems("fin_t fin_read fin_stored")
        x_again, out_done, x1_ready = sems("x_again out_done x1_ready")
        r_rms, r_rstd, xn2_ready, xn2_stored, xt2_done, xt2_copied = sems(
            "r_rms r_rstd xn2_ready xn2_stored xt2_done xt2_copied")
        logit_done, sm_in, sm_exp, route_ready, rank_done, lists_ready = sems(
            "logit_done sm_in sm_exp route_ready rank_done lists_ready")
        oh_ready, list_done, idx_ready, tr_done, xgT_ready, wait_carried = sems(
            "oh_ready list_done idx_ready tr_done xgT_ready wait_carried")
        gathered, scattered = ([sem(f"{n}{i}") for i in range(2)] for n in ("gathered", "scattered"))
        gate_up_done, act_ready, h_made, hT_done, hT_ready, down_done, rows_ready, rows_free = sems(
            "gate_up_done act_ready h_made hT_done hT_ready down_done rows_ready rows_free")
        moe_done, gfin_loaded, ysum_done, f_rms, out_ready, out_stored = sems(
            "moe_done gfin_loaded ysum_done f_rms out_ready out_stored")
        yrow_loaded = [sem(f"yrow_loaded{i}") for i in range(2)]

        PART_AT = {"u": 0, "q": W5, "f": W5 + HG, "v": W5 + 2 * HG, "g": W5 + 3 * HG}
        NB = W5 // CB
        STEPS = [(part, m) for part in "ufqv" for m in range(NB)]
        NW, NO = len(STEPS), D // CB
        PRE_SLOTS = 4
        HEAD_BLOCKS = [("g", 0, 2), ("glu", 0, 4), ("g", 1, 4), ("g", 2, 6), ("glu", 1, 8), ("g", 3, 8)]
        G_BLOCK = [NW + i for i, blk in enumerate(HEAD_BLOCKS) if blk[0] == "g"]
        GLU_BLOCK = [NW + i for i, blk in enumerate(HEAD_BLOCKS) if blk[0] == "glu"]
        OUT_AT = NW + len(HEAD_BLOCKS)
        NPRE = OUT_AT + NO
        FILLS = [len(range(s, NPRE, PRE_SLOTS)) for s in range(4)] + [0, 0]
        MOE_SLOT = (2, 3, 0, 1)
        EIGHTHS = 8
        S5_TILES = {}
        for j in range(NJ):
            at = EIGHTHS * NB + j * EIGHTHS * (NW - NB) // NJ
            S5_TILES[divmod(at, EIGHTHS)] = j
        STEP_OF = {j: n for (n, _), j in S5_TILES.items()}
        assert len(S5_TILES) == NJ
        PARAMETERS_AT = [(NB - 2, 0), (NB - 1, 0), (NB - 1, 4)]

        def half_tiles(n, b):
            per_half = EIGHTHS if STEPS[n][0] == "v" else EIGHTHS // 2
            return [S5_TILES[n, q] for q in range(b * per_half, min((b + 1) * per_half, EIGHTHS)) if (n, q) in S5_TILES]
        CHUNKS = ((0, P), (P, P), (2 * P, LAST))
        F_TILE = min(j for j in range(NJ) if STEPS[STEP_OF[j]][0] == "q") + 1
        LN_STEP = STEP_OF[F_TILE + NH - 1] + 1
        G_TILE = NJ - NH
        assert STEP_OF[G_TILE] > LN_STEP

        def token_rows(tile):
            meta, prompt, sample = t["meta_tokens"], t["x_prompt"][0], t["x_sample"][:, 0]
            if tile == 0:
                return [(0, meta), (NM, prompt[0:P - NM])]
            if tile == 1:
                return [(0, prompt[P - NM:2 * P - NM])]
            return [(0, prompt[2 * P - NM:SEQ]), (LAST, sample)]

        def slot(s, k):
            return ring[:, s, :].rearrange("p (k n) -> p k n", k=k)

        def run_rounds(eng, one_round):
            one_round(0)
            eng.wait_ge(lists_ready, 1)
            extra = eng.value_load(extra_i[0:1, 0:1], min_val=0, max_val=ROUNDS - 1)
            with eng.If(extra > 0):
                with eng.Fori(0, extra) as r:
                    one_round(r + 1)

        def is_first(R):
            return isinstance(R, int)

        block = ctx.enter_context(nc.Block())

        @block.sync
        def _(sp):
            def load_gate_up(e, q):
                w = t["w_gate"] if q % 2 == 0 else t["w_up"]
                half = D // 2
                src = w[0][bass.ds(e, 1), (q // 2) * half:(q // 2 + 1) * half, :]
                sp.dma_start(slot(MOE_SLOT[q], KD // 2), src.rearrange("a (k p) n -> p (a k) n", p=P)) \
                    .then_inc(slot_loaded[MOE_SLOT[q]], 16)

            def load_down(e, s):
                half = FH // 2
                src = t["w_down"][0][bass.ds(e, 1), (s - 4) * half:(s - 3) * half, :]
                sp.dma_start(slot(s, KF // 2), src.rearrange("a (k p) n -> p (a k) n", p=P)) \
                    .then_inc(slot_loaded[s], 16)

            def pre_load(n):
                last = n - PRE_SLOTS
                if last >= OUT_AT:
                    sp.wait_ge(out_done, 2 * (last - OUT_AT + 1))
                elif last >= NW:
                    kind, _, used = HEAD_BLOCKS[last - NW]
                    sp.wait_ge(g_done if kind == "g" else glu_done, used)
                elif last >= 0:
                    sp.wait_ge(proj_done, 2 * (last + 1))
                if n < OUT_AT:
                    part, m = STEPS[n] if n < NW else HEAD_BLOCKS[n - NW][:2]
                    if part == "glu":
                        src = t["s5_w_glu"][0, :, m * 2 * CB:(m + 1) * 2 * CB]
                    else:
                        c0 = PART_AT[part] + m * CB
                        src = t["w_in"][0, :, c0:c0 + CB]
                else:
                    o = n - OUT_AT
                    src = t["w_out"][0, :, o * CB:(o + 1) * CB]
                sp.dma_start(slot(n % PRE_SLOTS, src.shape[0] // P), src.rearrange("(k p) n -> p k n", p=P)) \
                    .then_inc(slot_loaded[n % PRE_SLOTS], 16)

            for tile in range(3):
                for at, rows in token_rows(tile):
                    sp.dma_start(xraw[at:at + rows.shape[0], tile, :], rows).then_inc(x_loaded, 16)
            for n in range(NW + PRE_SLOTS):
                pre_load(n)

            def load_S0(b):
                if b >= 3:
                    sp.wait_ge(os_done, b - 2)
                    sp.wait_ge(S0_stored[b % 3], 16 * (b // 3))
                else:
                    sp.wait_ge(y5_ready, N5)
                    sp.wait_ge(v_summed, NB)
                sp.dma_start(S0[b % 3], t["state_hgrn"][0, b].rearrange("h k v -> k h v")).then_inc(S0_loaded[b % 3], 16)

            def spread_v(b):
                if b:
                    sp.wait_ge(S1_ready, b)
                sp.dma_start(vk, v_dram[b:b + 1, :].broadcast_to([P, HG])).then_inc(v_spread, 16)

            sp.wait_ge(v_summed, NB)
            sp.dma_start(v_dram, v_tok[LAST:TT[2], 2, :]).then_inc(v_stored, 16)
            load_S0(0)
            sp.wait_ge(v_stored, 16)
            spread_v(0)
            load_S0(1)
            load_S0(2)
            for b in range(NS):
                sp.wait_ge(S1_ready, b + 1)
                if b + 1 < NS:
                    spread_v(b + 1)
                sp.dma_start(t["hgrn_sample"][0, b].rearrange("h k v -> k h v"), S0[b % 3]).then_inc(S0_stored[b % 3], 16)
                sp.wait_ge(st_ready, 3 * (b + 1))
                sp.dma_start(t["hgrn_prompt"][0, 0, b], Sst[b % 2][:, 2, :]).then_inc(st_stored[b % 2], 16)
                if b + 3 < NS:
                    load_S0(b + 3)
                for n in {0: (20,), 2: (22,), 3: (21,), 4: (23,)}.get(b, ()):
                    pre_load(n)

            sp.wait_ge(yT_ready, 2)
            for tile in range(3):
                for at, rows in token_rows(tile):
                    sp.dma_start(x1[at:at + rows.shape[0], tile, :], rows).then_inc(x_again, 16)
            sp.dma_start(wr[:, :, 0:NG], t["w_coarse"][0].rearrange("(k p) n -> p k n", p=P)).then_inc(wr_loaded, 16)
            sp.dma_start(wr[:, :, NG:NG + NE], t["w_fine"][0].rearrange("(k p) n -> p k n", p=P)).then_inc(wr_loaded, 16)
            for n in range(OUT_AT + 2, NPRE):
                pre_load(n)
            for b in range(2):
                sp.wait_ge(S0_stored[b], 16 * len(range(b, NS, 3)))
            for s in (4, 5):
                load_down(0, s)
            for q in range(4):
                sp.wait_ge(out_done, 2 * (NO - 3 + q))
                load_gate_up(0, q)

            def round_loads(R):
                with sp.Fori(1 if is_first(R) else 0, NE) as e:
                    x = e + R * NE
                    for q in range(4):
                        sp.wait_ge(gate_up_done, x * 2 + (q // 2 - 1))
                        load_gate_up(e, q)
                    for s in (4, 5):
                        sp.wait_ge(down_done, x * 2 + (s - 5))
                        load_down(e, s)

            run_rounds(sp, round_loads)

            sp.wait_ge(moe_done, 1)
            sp.dma_start(gfin, t["norm_final"].rearrange("(a n) -> a n", a=1).broadcast_to([P, D])).then_inc(gfin_loaded, 16)
            for tile in range(3):
                if tile == 2:
                    sp.wait_ge(ysum_done, 1)
                for j in range(2):
                    r0 = j * T + tile * P
                    sp.dma_start(yrow[2 * (tile % 2) + j][0:TT[tile], :], y_dram[r0:r0 + TT[tile], :]) \
                        .then_inc(yrow_loaded[tile % 2], 16)
            y = t["y_prompt"][0]
            for tile in range(3):
                sp.wait_ge(out_ready, tile + 1)
                if tile == 0:
                    sp.dma_start(y[0:P - NM, :], x1[NM:P, 0, :]).then_inc(out_stored, 16)
                elif tile == 1:
                    sp.dma_start(y[P - NM:2 * P - NM, :], x1[:, 1, :]).then_inc(out_stored, 16)
                else:
                    sp.dma_start(y[2 * P - NM:SEQ, :], x1[0:LAST, 2, :]).then_inc(out_stored, 16)
                    sp.dma_start(t["y_sample"][:, 0, :], x1[LAST:LAST + NS, 2, :]).then_inc(out_stored, 16)
            sp.wait_ge(out_stored, 64)
            for b in range(3):
                sp.wait_ge(S0_stored[b], 16 * len(range(b, NS, 3)))
            for b in range(2):
                sp.wait_ge(st_stored[b], 16 * NH // 2)

        @block.scalar
        def _(act):
            for name, at in (("norm_mix", V_MIX), ("norm_ffn", V_FFN), ("s5_D", V_D), ("s5_b_glu", V_BGLU),
                             ("s5_out_gain", V_G5), ("hg_lb_logits", V_LB0), ("hg_out_gain", V_GH)):
                rows = t[name].rearrange("a (k p) -> (a k) p", p=P)
                act.dma_start(vrow[at:at + rows.shape[0], :], rows).then_inc(vec_loaded, 16)
            act.dma_start(r5[0:NJ, 0, :], t["s5_A_re"].rearrange("a (j g) p -> (a j) (g p)", g=2)).then_inc(s5_loaded, 16)
            act.dma_start(r5[0:NJ, 1, :], t["s5_A_im"].rearrange("a (j g) p -> (a j) (g p)", g=2)).then_inc(s5_loaded, 16)
            act.dma_start(r5[0:NJ, 2, 0:2], t["s5_log_step"].rearrange("a (j g) -> (a j) g", g=2)).then_inc(s5_loaded, 16)
            for z, name in enumerate(("state_s5_re", "state_s5_im")):
                src = t[name][0].rearrange("(h b) (j g) p -> h b j (g p)", g=2, h=2)
                for half in range(2):
                    act.dma_start(h0row[:, z, half, :], src[half].rearrange("b j n -> (b j) n")).then_inc(s5_loaded, 16)
            for z, (bn, cn) in enumerate((("s5_B_re", "s5_C_re"), ("s5_B_im", "s5_C_im"))):
                act.dma_start(Braw[z], t[bn][0].rearrange("(j g) p c -> (g p) j c", g=2)).then_inc(s5_loaded, 16)
                act.dma_start(Craw[z], t[cn][0].rearrange("(i g) c p -> (g c) i p", g=8)).then_inc(s5_loaded, 16)
            act.dma_start(bias36[:, 0:NG], t["b_coarse"].broadcast_to([P, NG])).then_inc(wr_loaded, 16)
            act.dma_start(bias36[:, NG:NG + NE], t["b_fine"].broadcast_to([P, NE])).then_inc(wr_loaded, 16)

            step = Chain(act, act_step)

            def token_rms(src, scratch, signal):
                for tile in range(3):
                    n = TT[tile]
                    step.link(nc.scalar.activation(scratch[0:n, :], src[0:n, tile, :], ACT.Square,
                                                   accum_out=token_stats[0:n, tile:tile + 1]))
                for tile in range(3):
                    n = TT[tile]
                    s = token_stats[0:n, tile:tile + 1]
                    nc.scalar.activation(s, s, ACT.Sqrt, bias=eps_col[0:n, :], scale=1.0 / D).then_inc(signal, 1)

            act.wait_ge(x_loaded, 16 * 5)
            act.wait_ge(dve_consts, 1)
            token_rms(xraw, xsq, x_rms)
            act.wait_ge(s5_loaded, 16 * 11)
            nc.scalar.activation(r5[0:NJ, 2, 2:4], r5[0:NJ, 2, 0:2], ACT.Exp).then_inc(s5_exp, 1)
            act.wait_ge(s5_exp_in, 1)
            nc.scalar.activation(r5[0:NJ, 3, :], r5[0:NJ, 10, :], ACT.Exp).then_inc(s5_exp, 1)
            act.wait_ge(lb_in, 1)
            nc.scalar.activation(lb_tmp[:, 0:2, :], lb_tmp[:, 0:2, :], ACT.Exp).then_inc(lb_exp, 1)
            act.wait_ge(s5_sin_in, 1)
            nc.scalar.activation(r5[0:NJ, 6, :], r5[0:NJ, 4, :], ACT.Sin).then_inc(s5_sin, 1)
            nc.scalar.activation(r5[0:NJ, 7, :], r5[0:NJ, 5, :], ACT.Sin).then_inc(s5_sin, 1)
            def evac(n, b):
                part, m = STEPS[n]
                unit = 2 * n + b
                act.wait_ge(proj_done, unit + 1)
                bank, i = PB[unit % 4], 2 * m + b
                if part == "u":
                    ins = nc.scalar.activation(uT[:, i, :], bank[:, 0:T], ACT.Copy)
                elif part == "f":
                    ins = nc.scalar.activation(GT[:, i, :], bank[:, 0:T], ACT.Sigmoid)
                elif part == "q":
                    ins = nc.scalar.activation(qT[:, i, :], bank[:, 0:T], ACT.Copy, scale=float(P) ** -0.5)
                elif b == 0:
                    ins = nc.scalar.activation(v_tok[:, 0:2, m * CB:(m + 1) * CB],
                                               bank[:, 0:2 * CB].rearrange("p (a n) -> p a n", a=2), ACT.Copy)
                else:
                    if m:
                        act.wait_ge(v_summed, m)
                    for a in range(4):
                        ins = nc.scalar.activation(v_part[0:TT[2], a, :], bank[32 * a:32 * a + TT[2], 0:CB], ACT.Copy)
                ins.then_inc(proj_read, 1)

            def keep_last(j):
                act.wait_ge(h_ready, j + 1)
                nc.scalar.activation(fin[:, :, :, j], Hst[j % NHST][:, :, TP - 1:T], ACT.Copy).then_inc(fin_copied, 1)

            for n in range(NW):
                if n == PARAMETERS_AT[0][0]:
                    for z, ang in ((1, ang_sin), (0, ang_cos)):
                        act.wait_ge(ang_ready, 2 - z)
                        nc.scalar.activation(turn_table[:, z], ang, ACT.Sin, scale=6.283185).then_inc(table_ready, 1)
                if STEPS[n] == ("f", 0):
                    act.wait_ge(xt_done, 12)
                if STEPS[n] == ("v", 0):
                    act.wait_ge(mat_copied, 8)
                for b in range(2):
                    evac(n, b)
                    for j in half_tiles(n, b):
                        if j >= 1:
                            keep_last(j - 1)
                if n == LN_STEP:
                    act.wait_ge(k_ready, NH)
                    nc.scalar.activation(GT, GT, ACT.Ln).then_inc(lnf_done, 1)
            keep_last(NJ - 1)
            act.wait_ge(y5_ready, N5)
            nc.scalar.activation(uT, uT, ACT.Gelu_apprx_tanh).then_inc(gelu_done, 1)

            def keep_g(i):
                act.wait_ge(g_done, i + 1)
                nc.scalar.activation(gT[:, i, :], PB[2][:, 0:T], ACT.Copy).then_inc(g_read, 1)

            def exponents(h):
                b = h % 2
                act.wait_ge(G_ready, h + 1)
                act.wait_ge(diff_ready, h + 1)
                nc.scalar.activation(QK[b], QK[b], ACT.Exp)
                if h >= 2:
                    act.wait_ge(o_done, h - 1)
                    act.wait_ge(st_ready, 3 * (h - 1))
                nc.scalar.activation(qG[b], GT[:, h, 0:TP], ACT.Exp)
                nc.scalar.activation(chunk_decay[b][:, :], GT[:, h, 2 * P - 1:TP:LAST], ACT.Exp)
                for c0, n in CHUNKS:
                    ins = nc.scalar.activation(kG[b][:, c0:c0 + n], GT[:, h, c0:c0 + n], ACT.Exp,
                                               bias=GT[:, h, c0 + n - 1:c0 + n], scale=-1.0)
                ins.then_inc(exp_ready, 1)

            keep_g(0)
            act.wait_ge(fin_copied, NJ)
            exponents(0)
            for h in range(NH):
                b = h % 2
                act.wait_ge(glu_done, h + 1)
                nc.scalar.activation(sgT[:, h, :], PB[2][:, 0:T], ACT.Sigmoid,
                                     bias=vecs[:, V_BGLU + h:V_BGLU + h + 1]).then_inc(glu_read, 1)
                act.wait_ge(kgt_done, h + 1)
                nc.scalar.activation(kGt[b][:, 0:2, :], PB[7][:, 0:2 * P].rearrange("p (a n) -> p a n", a=2), ACT.Copy)
                nc.scalar.activation(kGt[b][0:LAST, 2, :], PB[7][0:LAST, 2 * P:3 * P], ACT.Copy).then_inc(kgt_copied, 1)
                if h + 1 < NH:
                    exponents(h + 1)
                    keep_g(h + 1)
                act.wait_ge(o_done, h + 1)
                nc.scalar.activation(kT[:, h, 0:TP], PB[6][:, 0:TP], ACT.Copy).then_inc(o_copied, 1)
            act.wait_ge(g_read, NH)
            nc.scalar.activation(gT, gT, ACT.Silu).then_inc(silu_done, 1)
            act.wait_ge(y5g_ready, 1)
            nc.scalar.activation(sgT, uT, ACT.Square).then_inc(sq_ready, 1)
            act.wait_ge(samp_copied, 4)
            act.wait_ge(o_copied, NH)
            nc.scalar.activation(qT, kT, ACT.Square).then_inc(sq_ready, 1)
            act.wait_ge(ss_done, 1)
            nc.scalar.activation(rms5, PB[3][:, 0:T], ACT.Sqrt, bias=eps_col[:, :], scale=1.0 / W5).then_inc(rt_ready, 1)
            for h in range(NH):
                act.wait_ge(ss_done, h + 2)
                nc.scalar.activation(GT[:, h, :], PB[4 + h % 2][:, 0:T], ACT.Sqrt, bias=eps_col[:, :],
                                     scale=1.0 / P).then_inc(rt_ready, 1)
            for z in range(2):
                act.wait_ge(fin_t, z + 1)
                nc.scalar.activation(fin_rows[0:3 * NJ, z, :, :], PB[z][0:3 * NJ, 0:3 * P].rearrange("p (a n) -> p a n", a=3),
                                     ACT.Copy).then_inc(fin_read, 1)
            act.wait_ge(fin_read, 2)
            for z, (pn, sn) in enumerate((("s5_re_prompt", "s5_re_sample"), ("s5_im_prompt", "s5_im_sample"))):
                act.dma_start(t[pn][0, 0].rearrange("(j g) p -> j (g p)", g=2), fin_rows[0:NJ, z, 0, :]).then_inc(fin_stored, 16)
                rows = t[sn][0].rearrange("b (j g) p -> (b j) (g p)", g=2)
                act.dma_start(rows[0:2 * NJ], fin_rows[NJ:3 * NJ, z, 0, :]).then_inc(fin_stored, 16)
                act.dma_start(rows[2 * NJ:5 * NJ], fin_rows[0:3 * NJ, z, 1, :]).then_inc(fin_stored, 16)
                act.dma_start(rows[5 * NJ:8 * NJ], fin_rows[0:3 * NJ, z, 2, :]).then_inc(fin_stored, 16)
            act.wait_ge(fin_stored, 16 * 8)
            act.wait_ge(x1_ready, 2 * NO)
            act.wait_ge(S0_stored[2], 16 * len(range(2, NS, 3)))
            token_rms(x1, yout[0], r_rms)
            act.wait_ge(r_rstd, 1)
            for tile in range(3):
                n = TT[tile]
                nc.scalar.activation(xn_rows[0:n, tile, :], x1[0:n, tile, :], ACT.Copy,
                                     scale=token_stats[0:n, 3 + tile:4 + tile]).then_inc(xn2_ready, 1)
                act.wait_ge(xn2_ready, tile + 1)
                act.dma_start(xn_dram[tile * P:tile * P + n, :], xn_rows[0:n, tile, :]).then_inc(xn2_stored, 16)
            act.wait_ge(sm_in, 1)
            nc.scalar.activation(e8, e8, ACT.Exp).then_inc(sm_exp, 1)
            act.wait_ge(sm_in, 2)
            nc.scalar.activation(dv, dv, ACT.Exp).then_inc(sm_exp, 1)
            nc.scalar.activation(chunk_decay[0][:, :], chunk_decay[0][:, :], ACT.Copy).then_inc(rows_ready, 1)

            def round_act(R):
                with act.Fori(0, NE // 2) as i:
                    for b in range(2):
                        x = i * 2 + (R * NE + b)
                        act.wait_ge(gate_up_done, x * 2 + 2)
                        act.wait_ge(h_made, x + 1)
                        nc.scalar.activation(sg[0:CAP, :], PB[b][0:CAP, :], ACT.Silu)
                        nc.scalar.activation(up[0:CAP, :], PB[b][CAP:P, :], ACT.Copy).then_inc(act_ready, 1)
                        act.wait_ge(down_done, x * 2 + 2)
                        act.wait_ge(rows_free, x + 1)
                        for cc in range(4):
                            ins = nc.scalar.activation(yout[b][0:CAP, cc * 512:(cc + 1) * 512],
                                                       PB[2 + cc // 2][(cc % 2) * CAP:(cc % 2 + 1) * CAP, :], ACT.Copy)
                        ins.then_inc(rows_ready, 1)

            run_rounds(act, round_act)
            for tile in range(3):
                n = TT[tile]
                act.wait_ge(ysum_done, tile + 1)
                s = token_stats[0:n, tile:tile + 1]
                step.link(nc.scalar.activation(junk[0:n, :], x1[0:n, tile, :], ACT.Square, accum_out=s))
                nc.scalar.activation(s, s, ACT.Sqrt, bias=eps_col[0:n, :], scale=1.0 / D).then_inc(f_rms, 1)

        @block.gpsimd
        def _(pool):
            def made(ins):
                ins.then_inc(pool_consts, 1)

            made(pool.memset(ident[:, :], 0.0))
            made(pool.memset(upper[:, :], 0.0))
            pool.wait_ge(pool_consts, 2)
            made(pool.affine_select(out=ident[:, :], in_=ident[:, :], compare_op=ALU.not_equal, fill=1.0, base=0,
                                    pattern=[[-1, P]], channel_multiplier=1))
            made(pool.affine_select(out=upper[:, :], in_=upper[:, :], compare_op=ALU.is_ge, fill=1.0, base=0,
                                    pattern=[[-1, P]], channel_multiplier=1))
            made(pool.iota(iI, pattern=[[1, P]], base=0, channel_multiplier=0))
            made(pool.iota(iJ, pattern=[[0, P]], base=0, channel_multiplier=1))
            made(pool.iota(iota_i[:, 0:64], pattern=[[1, 64]], base=0, channel_multiplier=0))
            made(pool.iota(iota_i[:, 64:81], pattern=[[16, 17]], base=0, channel_multiplier=0))
            made(pool.iota(iota_i[:, 81:84], pattern=[[P, 3]], base=0, channel_multiplier=1))

            step = Chain(pool, pool_step)
            pool.wait_ge(table_ready, 2)
            pool.wait_ge(mat_t, 8)
            for j in range(NJ):
                b = j % 2
                if j >= 2:
                    pool.wait_ge(turn_used, j - 1)
                A = [turn_table[:, z, j, 16:33].unsqueeze(2).broadcast_to([P, 17, 16]) for z in range(2)]
                B = [turn_table[:, z, j, 0:16].unsqueeze(1).broadcast_to([P, 17, 16]) for z in range(2)]

                def out(x, z):
                    return x[:, z].rearrange("p (a b) -> p a b", b=16)

                t1, t2 = turn_tmp
                step.add(pool.tensor_tensor(out(t1, 0), A[0], B[0], ALU.mult))
                step.add(pool.tensor_tensor(out(t1, 1), A[1], B[0], ALU.mult))
                step.add(pool.tensor_tensor(out(t2, 0), A[1], B[1], ALU.mult))
                step.add(pool.tensor_tensor(out(t2, 1), A[0], B[1], ALU.mult))
                step.settle()
                step.add(pool.tensor_tensor(turn[b][:, 0], t1[:, 0], t2[:, 0], ALU.subtract))
                step.add(pool.tensor_tensor(turn[b][:, 1], t1[:, 1], t2[:, 1], ALU.add))
                step.settle()
                pool.engine_nop().then_inc(turn_ready, 1)
            pool.wait_ge(y5_ready, N5)
            for h in range(NH):
                b = h % 2
                pool.wait_ge(G_ready, h + 1)
                if h >= 2:
                    pool.wait_ge(att_done, 8 * (h - 1))
                for l, B in enumerate(LV):
                    g = GT[:, h, 0:LW[l]].rearrange("p (n two b) -> p n two b", two=2, b=B)
                    o = QK[b][:, LO[l]:LO[l] + LW[l]].rearrange("p (n two b) -> p n two b", two=2, b=B)
                    mid = g[:, :, 0, B - 1:B].broadcast_to([P, LW[l] // (2 * B), B])
                    pool.tensor_tensor(o[:, :, 0, :], mid, g[:, :, 0, :], ALU.subtract)
                    ins = pool.tensor_tensor(o[:, :, 1, :], g[:, :, 1, :], mid, ALU.subtract)
                ins.then_inc(diff_ready, 1)
                pool.wait_ge(S0_loaded[h % 3], 16 * (h // 3 + 1))
                pool.tensor_tensor(S0[h % 3], S0[h % 3], fs[:, :, h:h + 1].broadcast_to([P, NH, P]), ALU.mult) \
                    .then_inc(S0_decayed, 1)
            pool.engine_nop().then_inc(rows_free, 1)
            pool.engine_nop().then_inc(rows_free, 1)
            pool.wait_ge(xn2_stored, 48)
            last_token, last_row = pool.to_reg(T - 1), pool.to_reg(2 * T - 1)

            def gather(g, p):
                pool.wait_ge(idx_ready, g + 1)
                pool.sem_inc(wait_carried, 1)
                pool.indirect_dma_start(out=xg[p][0:CAP, :], out_offset=None, in_=xn_dram,
                                        in_offset=bass.IndirectOffsetOnAxis(ap=idx_tok[p][:, 0:1], axis=0),
                                        bounds_check=last_token, oob_is_err=False).then_inc(gathered[p], 16)

            def round_rows(R):
                if is_first(R):
                    pool.wait_ge(xt2_done, 12)
                else:
                    pool.wait_ge(tr_done, R * (NE + 1) + 1)
                gather(R * (NE + 1), 0)
                with pool.Fori(0, NE // 2) as i:
                    for b in range(2):
                        x = i * 2 + (R * NE + b)
                        g = i * 2 + (R * (NE + 1) + b + 1)
                        pool.wait_ge(tr_done, g)
                        gather(g, 1 - b)
                        pool.wait_ge(rows_ready, x + 2)
                        pool.sem_inc(wait_carried, 1)
                        pool.indirect_dma_start(out=y_dram, out_offset=bass.IndirectOffsetOnAxis(ap=idx_dst[b][:, 0:1], axis=0),
                                                in_=yout[b][0:CAP, :], in_offset=None, bounds_check=last_row,
                                                oob_is_err=False).then_inc(scattered[b], 16)
                        pool.wait_ge(scattered[b], i * 16 + (R * (NE // 2) + 1) * 16)
                        pool.sem_inc(rows_free, 1)

            run_rounds(pool, round_rows)
            pool.engine_nop().then_inc(moe_done, 1)

        @block.tensor
        def _(pe):
            pe.wait_ge(pool_consts, 4)
            pe.wait_ge(vec_loaded, 16 * 7)
            pe.transpose(PB[7][:, 0:80], vrow[0:80, :], ident[0:80, 0:80]).then_inc(vec_t, 1)

            def transpose_tokens(src, ready, done, copied):
                for tile in range(3):
                    n = TT[tile]
                    pe.wait_ge(ready, tile + 1)
                    for q in range(KD // 4):
                        unit = tile * (KD // 4) + q
                        if unit >= 4:
                            pe.wait_ge(copied, unit - 3)
                        for a in range(4):
                            k = 4 * q + a
                            ins = pe.transpose(PB[unit % 4][:, a * P:a * P + n], src[0:n, tile, k * P:(k + 1) * P],
                                               ident[0:n, 0:n])
                        ins.then_inc(done, 1)

            transpose_tokens(xraw, xn_made, xt_done, xt_copied)

            def last_tile(bank, lhs, w):
                for k in range(KD):
                    at = 32 * (k % 4)
                    ins = pe.matmul(bank[at:at + TT[2], 0:CB], lhs[k][:, 2 * P:T], w[:, k, :], start=(k < 4), stop=(k >= KD - 4),
                                    tile_position=(0, at))
                return ins

            def project(n, eighth_work):
                part, _ = STEPS[n]
                s = n % PRE_SLOTS
                w = slot(s, KD)
                pe.wait_ge(slot_loaded[s], 16 * (n // PRE_SLOTS + 1))
                if n == 0:
                    pe.wait_ge(xt_copied, 12)
                for b in range(2):
                    unit = 2 * n + b
                    if unit >= 4:
                        pe.wait_ge(proj_read, unit - 3)
                    bank = PB[unit % 4]
                    if part == "v" and b == 0:
                        for tile in range(2):
                            for k in range(KD):
                                if k % 4 == 0:
                                    eighth_work(tile * 4 + k // 4)
                                ins = pe.matmul(bank[:, tile * CB:(tile + 1) * CB], xnT[:, k, tile * P:(tile + 1) * P],
                                                w[:, k, :], start=(k == 0), stop=(k == KD - 1))
                    elif part == "v":
                        ins = last_tile(bank, [xnT[:, k] for k in range(KD)], w)
                    else:
                        for k in range(KD):
                            if k % 4 == 0:
                                eighth_work(b * 4 + k // 4)
                            ins = pe.matmul(bank[:, 0:T], w[:, k, b * P:(b + 1) * P], xnT[:, k, :],
                                            start=(k == 0), stop=(k == KD - 1))
                    ins.then_inc(proj_done, 1)

            def bu(j):
                i, a = j // 4, j % 4
                rows = slice(32 * a, 32 * a + 32)
                if j % 4 == 0:
                    pe.wait_ge(proj_read, i + 1)
                if j >= 1:
                    pe.wait_ge(bu_read, j)
                else:
                    pe.wait_ge(mat_copied, 8)
                for z in range(2):
                    ins = pe.matmul(PB[4 + z][:, 0:T], BT[z][rows, i, :], uT[rows, i, :], start=True, stop=True)
                ins.then_inc(bu_done, 1)

            def y_of(j):
                i, a = j // 4, j % 4
                pe.wait_ge(h_ready, j + 1)
                if a == 0 and i >= 1:
                    pe.wait_ge(y5_ready, i)
                for z in range(2):
                    ins = pe.matmul(PB[6][32 * a:32 * a + 32, 0:T], CT[z][:, i, 32 * a:32 * a + 32], Hst[j % NHST][:, z, :],
                                    start=(z == 0), stop=(z == 1))
                ins.then_inc(h_used, 1)

            def parameters(n):
                if n == 0:
                    pe.wait_ge(s5r_ready, 1)
                    pe.wait_ge(vec_copied, 1)
                    for q, row in enumerate((3, 5, 8, 9, 6, 7)):
                        ins = pe.transpose(PB[7][:, P + q * NJ:P + (q + 1) * NJ], r5[0:NJ, row, :], ident[0:NJ, 0:NJ])
                    ins.then_inc(par_t, 1)
                    for z in range(2):
                        for half in range(2):
                            at = z * 2 * P + half * P
                            ins = pe.transpose(PB[6][:, at:at + P], h0row[:, z, half, :], ident[:, :])
                    ins.then_inc(par_t, 1)
                else:
                    pe.wait_ge(mat_ready, n)
                    pe.wait_ge(par_copied, 2)
                    for z in range(2):
                        for q in range(2):
                            bank = PB[4 + 2 * z + q]
                            if n == 2:
                                pe.wait_ge(mat_copied, 2 * z + q + 1)
                            for a in range(4):
                                i = 4 * q + a
                                src = BP[z][:, i, :] if n == 1 else CP[z][:, i].rearrange("p a b -> p (a b)")
                                ins = pe.transpose(bank[:, a * P:(a + 1) * P], src, ident[:, :])
                            ins.then_inc(mat_t, 1)

            for n in range(NW):
                def between(q):
                    if (n, q) in PARAMETERS_AT:
                        parameters(PARAMETERS_AT.index((n, q)))
                    if (n, q) in S5_TILES:
                        j = S5_TILES[n, q]
                        bu(j)
                        if j >= 2:
                            y_of(j - 2)

                project(n, between)
            y_of(NJ - 2)

            def project_g(i, ks):
                n = G_BLOCK[i // 2]
                s = n % PRE_SLOTS
                if ks[0] == 0:
                    pe.wait_ge(slot_loaded[s], 16 * (n // PRE_SLOTS + 1))
                    if i >= 1:
                        pe.wait_ge(glu_read, i)
                for k in ks:
                    ins = pe.matmul(PB[2][:, 0:T], slot(s, KD)[:, k, (i % 2) * P:(i % 2 + 1) * P], xnT[:, k, :],
                                    start=(k == 0), stop=(k == KD - 1))
                if ks[-1] == KD - 1:
                    ins.then_inc(g_done, 1)

            pe.wait_ge(proj_read, 2 * NW)
            project_g(0, range(KD))
            y_of(NJ - 1)
            pe.wait_ge(y5_ready, N5)
            pe.wait_ge(v_summed, NB)
            for h in range(NH):
                b = h % 2
                cols = slice(h * P, (h + 1) * P)
                pe.wait_ge(gelu_done, 1)
                pe.wait_ge(g_read, h + 1)
                n = GLU_BLOCK[h // 4]
                s = n % PRE_SLOTS
                pe.wait_ge(slot_loaded[s], 16 * (n // PRE_SLOTS + 1))
                for k in range(N5):
                    ins = pe.matmul(PB[2][:, 0:T], slot(s, N5)[:, k, (h % 4) * P:(h % 4 + 1) * P], uT[:, k, :],
                                    start=(k == 0), stop=(k == N5 - 1))
                ins.then_inc(glu_done, 1)
                pe.wait_ge(qk_ready, h + 1)
                if h >= 1:
                    pe.wait_ge(kgt_copied, h)
                for q, (c0, n_) in enumerate(CHUNKS):
                    ins = pe.transpose(PB[7][0:n_, q * P:(q + 1) * P], kG[b][:, c0:c0 + n_], ident[:, :])
                ins.then_inc(kgt_done, 1)
                for l in range(8):
                    u = 8 * h + l
                    if u >= 2:
                        pe.wait_ge(att_read, u - 1)
                    bank = PB[4 + l % 2]
                    for c0, n_ in (CHUNKS if l >= 3 else CHUNKS[:2]):
                        if l < 7:
                            k_ = q_ = QK[b][:, LO[l] + c0:LO[l] + c0 + n_]
                        else:
                            k_, q_ = kT[:, h, c0:c0 + n_], qT[:, h, c0:c0 + n_]
                        ins = pe.matmul(bank[0:n_, c0:c0 + n_], k_, q_, start=True, stop=True)
                    ins.then_inc(att_done, 1)
                    if h + 1 < NH:
                        project_g(h + 1, (2 * l, 2 * l + 1))
                pe.wait_ge(kgt_copied, h + 1)
                if h >= 1:
                    pe.wait_ge(st_ready, 3 * h)
                for q, (c0, n_) in enumerate(CHUNKS):
                    ins = pe.matmul(PB[3][:, q * P:(q + 1) * P], kGt[b][0:n_, q, :], v_tok[0:n_, q, cols], start=True, stop=True)
                ins.then_inc(st_done, 1)
                pe.wait_ge(att_read, 8 * (h + 1))
                pe.wait_ge(st_ready, 3 * h + 2)
                if h >= 1:
                    pe.wait_ge(o_copied, h)
                for q, (c0, n_) in enumerate(CHUNKS):
                    if q:
                        pe.matmul(PB[6][:, c0:c0 + n_], Sst[b][:, q - 1, :], qG[b][:, c0:c0 + n_], start=True, stop=False)
                    ins = pe.matmul(PB[6][:, c0:c0 + n_], v_tok[0:n_, q, cols], att[b][0:n_, c0:c0 + n_],
                                    start=(q == 0), stop=True)
                ins.then_inc(o_done, 1)
                pe.wait_ge(S1_ready, h + 1)
                for half in range(2):
                    for a in range(4):
                        ins = pe.matmul(PB[half][32 * a:32 * a + NS, 0:P], q_own[:, 4 * half + a, h, :],
                                        S0[h % 3][:, 4 * half + a, :], start=(h == 0), stop=(h == NS - 1),
                                        tile_position=(0, 32 * a))
                ins.then_inc(os_done, 1)

            pe.wait_ge(os_copied, 1)
            pe.wait_ge(o_copied, NH)
            for hd in range(NH):
                half, a = hd // 4, hd % 4
                rows = slice(32 * a, 32 * a + NS)
                ins = pe.transpose(PB[4 + a][:, half * NS:(half + 1) * NS], o_rows[rows, half, :], ident[rows, rows])
            ins.then_inc(os_turned, 1)

            for z in range(2):
                flat = fin[:, z].rearrange("p a b -> p (a b)")
                for a in range(3):
                    ins = pe.transpose(PB[z][0:3 * NJ, a * P:(a + 1) * P], flat[:, a * 3 * NJ:(a + 1) * 3 * NJ], ident[:, :])
                ins.then_inc(fin_t, 1)
            pe.wait_ge(sq_ready, 1)
            for i in range(N5):
                ins = pe.matmul(PB[3][:, 0:T], ones[:, :], sgT[:, i, :], start=(i == 0), stop=(i == N5 - 1))
            ins.then_inc(ss_done, 1)
            pe.wait_ge(sq_ready, 2)
            for h in range(NH):
                if h >= 2:
                    pe.wait_ge(rt_ready, h)
                pe.matmul(PB[4 + h % 2][:, 0:T], ones[:, :], qT[:, h, :], start=True, stop=True).then_inc(ss_done, 1)

            yT = [uT[:, k] for k in range(N5)] + [gT[:, k] for k in range(NH)]
            pe.wait_ge(yT_ready, 1)
            pe.wait_ge(fin_read, 2)
            for o in range(NO):
                n = OUT_AT + o
                s = n % PRE_SLOTS
                pe.wait_ge(slot_loaded[s], 16 * (n // PRE_SLOTS + 1))
                for b in range(2):
                    unit = 2 * o + b
                    if unit >= 4:
                        pe.wait_ge(x1_ready, unit - 3)
                    if b == 0:
                        for tile in range(2):
                            for k in range(KD):
                                if unit == tile == 0 and k == N5:
                                    pe.wait_ge(yT_ready, 2)
                                ins = pe.matmul(PB[unit % 4][:, tile * CB:(tile + 1) * CB], yT[k][:, tile * P:(tile + 1) * P],
                                                slot(s, KD)[:, k, :], start=(k == 0), stop=(k == KD - 1))
                    else:
                        ins = last_tile(PB[unit % 4], yT, slot(s, KD))
                    ins.then_inc(out_done, 1)

            pe.wait_ge(x1_ready, 2 * NO)
            transpose_tokens(xn_rows, xn2_ready, xt2_done, xt2_copied)
            pe.wait_ge(xt2_copied, 12)
            pe.wait_ge(wr_loaded, 64)
            for tile in range(3):
                for k in range(KD):
                    at = tile * (NG + NE)
                    ins = pe.matmul(PB[6][0:TT[tile], at:at + NG + NE], xn2T[:, k, tile * P:tile * P + TT[tile]], wr[:, k, :],
                                    start=(k == 0), stop=(k == KD - 1))
            ins.then_inc(logit_done, 1)
            pe.wait_ge(route_ready, 1)
            for q in range(4):
                for tile in range(min(q + 1, 3)):
                    last = tile == min(q, 2)
                    ins = pe.matmul(PB[7][:, q * NE:(q + 1) * NE], (upper if tile == q else ones)[:, :], Mr[:, tile, :],
                                    start=(tile == 0), stop=last)
            ins.then_inc(rank_done, 1)
            pe.nop().then_inc(tr_done, 1)

            def list_of(g, e):
                pe.wait_ge(oh_ready, g + 1)
                for tile in range(3):
                    ins = pe.matmul(PB[7][0:CAP, 0:3], oh[:, tile, :], PL[:, tile, bass.ds(e, 1), :].rearrange("p a b -> p (a b)"),
                                    start=(tile == 0), stop=(tile == 2))
                ins.then_inc(list_done, 1)

            def turn_64(out, rows, waits):
                eye = ident[0:CAP, 0:CAP]
                return pe.matmul(out, rows, eye, start=True, stop=True) if waits else pe.transpose(out, rows, eye)

            def transpose_rows(p):
                for k in range(KD):
                    ins = turn_64(PB[4 + k // 8][:, (k % 8) * CAP:(k % 8 + 1) * CAP], xg[p][0:CAP, k * P:(k + 1) * P], k == 0)
                ins.then_inc(tr_done, 1)

            def round_pe(R):
                if is_first(R):
                    pe.wait_ge(lists_ready, 1)
                else:
                    pe.wait_ge(idx_ready, R * (NE + 1))
                    pe.wait_ge(xgT_ready, R * (NE + 1))
                list_of(R * (NE + 1), 0)
                pe.wait_ge(gathered[0], R * (16 * 17) + 16)
                transpose_rows(0)
                with pe.Fori(0, NE // 2) as i:
                    for b in range(2):
                        x = i * 2 + (R * NE + b)
                        g = i * 2 + (R * (NE + 1) + b + 1)
                        pe.wait_ge(idx_ready, g)
                        list_of(g, i * 2 + (b + 1))
                        pe.wait_ge(xgT_ready, g)
                        for half in range(2):
                            sg_, su_ = MOE_SLOT[2 * half], MOE_SLOT[2 * half + 1]
                            pe.wait_ge(slot_loaded[sg_], x * 16 + 16 * (FILLS[sg_] + 1))
                            pe.wait_ge(slot_loaded[su_], x * 16 + 16 * (FILLS[su_] + 1))
                            for k in range(KD // 2):
                                kk = half * (KD // 2) + k
                                for at, s in ((0, sg_), (CAP, su_)):
                                    ins = pe.matmul(PB[b][at:at + CAP, :], xgT[b][:, kk, :], slot(s, KD // 2)[:, k, :],
                                                    start=(kk == 0), stop=(kk == KD - 1))
                            ins.then_inc(gate_up_done, 1)
                        if b == 0:
                            pe.wait_ge(gathered[1], i * 16 + (R * 16 + 1) * 16)
                        else:
                            pe.wait_ge(gathered[0], i * 16 + (R * 17 + 2) * 16)
                        transpose_rows(1 - b)
                        pe.wait_ge(h_made, x + 2)
                        for f in range(KF):
                            ins = turn_64(PB[6][:, f * CAP:(f + 1) * CAP], hh[0:CAP, f * P:(f + 1) * P], f == 0)
                        ins.then_inc(hT_done, 1)
                        pe.wait_ge(hT_ready, x + 1)
                        pe.wait_ge(rows_ready, x + 1)
                        for half in range(2):
                            pe.wait_ge(slot_loaded[4 + half], x * 16 + 16)
                            for k in range(KF // 2):
                                f = half * (KF // 2) + k
                                for cc in range(4):
                                    at = (cc % 2) * CAP
                                    ins = pe.matmul(PB[2 + cc // 2][at:at + CAP, :], hT[:, f, :],
                                                    slot(4 + half, KF // 2)[:, k, cc * 512:(cc + 1) * 512],
                                                    start=(f == 0), stop=(f == KF - 1))
                            ins.then_inc(down_done, 1)

            run_rounds(pe, round_pe)

        @block.vector
        def _(dve):
            step = Chain(dve, dve_step)
            TS, TTo, STT = nc.vector.tensor_scalar, nc.vector.tensor_tensor, nc.vector.scalar_tensor_tensor
            nc.vector.memset(ones[:, :], 1.0)
            nc.vector.memset(eps_col[:, :], EPS).then_inc(dve_consts, 1)

            def token_rstd(rms, count, dst=3):
                dve.wait_ge(rms, count)
                step.add(nc.vector.reciprocal(token_stats[:, dst:dst + 2], token_stats[:, 0:2]))
                step.link(nc.vector.reciprocal(token_stats[0:TT[2], dst + 2:dst + 3], token_stats[0:TT[2], 2:3]))

            token_rstd(x_rms, 3)
            for tile in range(3):
                n = TT[tile]
                TS(xraw[0:n, tile, :], xraw[0:n, tile, :], token_stats[0:n, 3 + tile:4 + tile], None, ALU.mult) \
                    .then_inc(xn_made, 1)
            dve.wait_ge(vec_t, 1)
            nc.vector.tensor_copy(vecs[:, :], PB[7][:, 0:80]).then_inc(vec_copied, 1)
            dve.wait_ge(vec_copied, 1)

            def copy_transposed(dst, gain, done, copied):
                for tile in range(3):
                    n = TT[tile]
                    for q in range(KD // 4):
                        unit = tile * (KD // 4) + q
                        dve.wait_ge(done, unit + 1)
                        TTo(dst[:, 4 * q:4 * q + 4, tile * P:tile * P + n],
                            PB[unit % 4][:, :].rearrange("p (a n) -> p a n", a=4)[:, :, 0:n],
                            vecs[:, gain + 4 * q:gain + 4 * q + 4].unsqueeze(2).broadcast_to([P, 4, n]), ALU.mult) \
                            .then_inc(copied, 1)

            copy_transposed(xnT, V_MIX, xt_done, xt_copied)

            step.link(TTo(lb_tmp[:, 2, :], vecs[:, V_LB0:V_LB0 + 8], vecs[:, V_LB1:V_LB1 + 8], ALU.max))
            TTo(lb_tmp[:, 0, :], vecs[:, V_LB0:V_LB0 + 8], lb_tmp[:, 2, :], ALU.subtract)
            TTo(lb_tmp[:, 1, :], vecs[:, V_LB1:V_LB1 + 8], lb_tmp[:, 2, :], ALU.subtract).then_inc(lb_in, 1)

            R = [r5[0:NJ, q, :] for q in range(12)]
            two = [r.rearrange("p (a b) -> p a b", a=2) for r in R]
            stepc = R[2][:, 2:4].unsqueeze(2).broadcast_to([NJ, 2, P5])
            dve.wait_ge(s5_loaded, 16 * 11)
            dve.wait_ge(s5_exp, 1)
            TTo(two[10], two[0], stepc, ALU.mult).then_inc(s5_exp_in, 1)
            step.link(TTo(two[11], two[1], stepc, ALU.mult))
            step.link(TS(R[4], R[11], 1 / (2 * math.pi), MAGIC, ALU.mult, ALU.add))
            step.link(TS(R[4], R[4], MAGIC, None, ALU.subtract))
            step.link(STT(R[11], R[4], -TWO_PI_HI, R[11], ALU.mult, ALU.add))
            step.link(STT(R[4], R[4], -TWO_PI_LO, R[11], ALU.mult, ALU.add))
            step.link(TS(R[4], R[4], PI_BELOW, -PI_BELOW, ALU.min, ALU.max))
            step.link(TS(R[5], R[4], math.pi / 2, None, ALU.add))
            step.link(TS(R[11], R[5], PI_BELOW, -2 * math.pi, ALU.is_gt, ALU.mult))
            step.link(TTo(R[5], R[5], R[11], ALU.add))
            TS(R[5], R[5], PI_BELOW, -PI_BELOW, ALU.min, ALU.max).then_inc(s5_sin_in, 1)
            dve.wait_ge(lb_exp, 1)
            step.link(TTo(lb_tmp[:, 1, :], lb_tmp[:, 0, :], lb_tmp[:, 1, :], ALU.add))
            step.link(nc.vector.reciprocal(lb_tmp[:, 1, :], lb_tmp[:, 1, :]))
            step.link(TTo(lb[:, :], lb_tmp[:, 0, :], lb_tmp[:, 1, :], ALU.mult))
            step.link(TS(one_minus_lb[:, :], lb[:, :], -1.0, 1.0, ALU.mult, ALU.add))
            dve.wait_ge(s5_exp, 2)
            dve.wait_ge(s5_sin, 2)
            step.add(TS(R[5], R[4], 1 / (2 * math.pi), None, ALU.mult))
            step.add(TTo(R[8], R[3], R[7], ALU.mult))
            step.add(TTo(R[9], R[3], R[6], ALU.mult))
            step.add(TTo(R[10], R[0], R[0], ALU.mult))
            step.add(TTo(R[11], R[1], R[1], ALU.mult))
            step.settle()
            step.link(TTo(R[10], R[10], R[11], ALU.add))
            step.add(nc.vector.reciprocal(R[10], R[10]))
            step.link(TS(R[11], R[8], -1.0, None, ALU.add))
            step.add(TTo(R[6], R[11], R[0], ALU.mult))
            step.link(TTo(R[7], R[9], R[1], ALU.mult))
            step.link(TTo(R[6], R[6], R[7], ALU.add))
            step.add(TTo(R[6], R[6], R[10], ALU.mult))
            step.add(TTo(R[7], R[9], R[0], ALU.mult))
            step.link(TTo(R[11], R[11], R[1], ALU.mult))
            step.link(TTo(R[7], R[7], R[11], ALU.subtract))
            TTo(R[7], R[7], R[10], ALU.mult).then_inc(s5r_ready, 1)

            dve.wait_ge(pool_consts, 9)
            nc.vector.tensor_copy(mvals[:, 0:16], iota_i[:, 0:16])
            nc.vector.tensor_copy(mvals[:, 16:33], iota_i[:, 64:81])
            nc.vector.tensor_copy(iota32, iota_i[:, 0:NE])
            nc.vector.tensor_copy(slotid, iota_i[:, 0:CAP])
            nc.vector.tensor_copy(tid, iota_i[:, 81:84])
            step.add(TTo(iX, iI, iJ, ALU.bitwise_xor))
            step.add(TTo(mG, iI, iJ, ALU.is_gt))
            step.add(TTo(masks[:, 7, :], iI, iJ, ALU.is_equal))
            step.link(TS(parity[:, 2:3].bitcast(I32), iJ[:, 0:1], 16, None, ALU.bitwise_and))
            step.link(nc.vector.tensor_copy(mX, iX))
            step.link(STT(mX, mX, 1.0, mG, ALU.add, ALU.mult))
            step.add(TS(mX, mX, -1.0, None, ALU.add))
            step.link(nc.vector.tensor_copy(parity[:, 1:2], parity[:, 2:3].bitcast(I32)))
            step.link(TS(parity[:, 1:2], parity[:, 1:2], 1.0 / 16, None, ALU.mult))
            step.link(TS(parity[:, 0:1], parity[:, 1:2], -1.0, 1.0, ALU.mult, ALU.add))
            for l, B in enumerate(LV):
                step.link(TS(mL, mX, 2.0 * B, None, ALU.is_lt))
                step.link(STT(masks[:, l, :], mX, float(B), mL, ALU.is_ge, ALU.mult))

            for z in range(2):
                for half in range(2):
                    TS(CP[z][:, :, half, :], Craw[z], parity[:, half:half + 1], 1.0 if z == 0 else -1.0, ALU.mult, ALU.mult)
            for z in range(2):
                step.add(nc.vector.memset(BP[z], 0.0))

            dve.wait_ge(par_t, 2)
            step.link(nc.vector.tensor_copy(sc5[:, :, :], PB[7][:, P:P + 6 * NJ].rearrange("p (a n) -> p a n", a=6)))
            dec = [sc5[:, q, :].unsqueeze(1).broadcast_to([P, NS, NJ]) for q in (2, 3)]
            h0 = [PB[6][:, z * 2 * P:(z + 1) * 2 * P].rearrange("p (a n) -> p a n", a=NS) for z in range(2)]
            step.add(TTo(Zs[:, 0], h0[0], dec[0], ALU.mult))
            step.add(TTo(z_tmp[0], h0[1], dec[1], ALU.mult))
            step.add(TTo(Zs[:, 1], h0[1], dec[0], ALU.mult))
            step.add(TTo(z_tmp[1], h0[0], dec[1], ALU.mult))
            step.link(TTo(ang_r, sc5[:, 1, :].unsqueeze(2).broadcast_to([P, NJ, 33]),
                          mvals.unsqueeze(1).broadcast_to([P, NJ, 33]), ALU.mult))
            nc.vector.tensor_copy(parity[:, 2:3], parity[:, 1:2]).then_inc(par_copied, 2)
            step.add(TTo(Zs[:, 0], Zs[:, 0], z_tmp[0], ALU.subtract))
            step.add(TTo(Zs[:, 1], Zs[:, 1], z_tmp[1], ALU.add))
            step.link(TS(ang_n, ang_r, MAGIC, MAGIC, ALU.add, ALU.subtract))
            step.link(TTo(ang_sin, ang_r, ang_n, ALU.subtract))
            TS(ang_sin, ang_sin, 0.5, -0.5, ALU.min, ALU.max).then_inc(ang_ready, 1)
            step.link(TS(ang_r, ang_r, 0.25, None, ALU.add))
            step.link(TS(ang_n, ang_r, MAGIC, MAGIC, ALU.add, ALU.subtract))
            step.link(TTo(ang_cos, ang_r, ang_n, ALU.subtract))
            TS(ang_cos, ang_cos, 0.5, -0.5, ALU.min, ALU.max).then_inc(ang_ready, 1)
            fr, fi = (sc5[:, q, :].unsqueeze(2).broadcast_to([P, NJ, C5]) for q in (4, 5))
            for z in range(2):
                step.add(TTo(Btmp[0], fr, Braw[z], ALU.mult))
                step.link(TTo(Btmp[1], fi, Braw[1 - z], ALU.mult))
                op = ALU.subtract if z == 0 else ALU.add
                pad = BP[z].rearrange("p i (a g c) -> p (i a) g c", a=4, g=2)
                for g in range(2):
                    rows = slice(64 * g, 64 * g + 64)
                    ins = TTo(pad[rows, :, g, :], Btmp[0][rows], Btmp[1][rows], op)
                    if z == 1 and g == 1:
                        ins.then_inc(mat_ready, 1)
                    else:
                        step.add(ins)
                step.settle()
            nc.vector.tensor_copy(parity[:, 2:3], parity[:, 1:2]).then_inc(mat_ready, 1)
            dve.wait_ge(table_ready, 2)
            for n in range(2):
                for z in range(2):
                    for q in range(2):
                        dve.wait_ge(mat_t, 4 * n + 2 * z + q + 1)
                        nc.vector.tensor_copy((BT, CT)[n][z][:, 4 * q:4 * q + 4, :],
                                              PB[4 + 2 * z + q][:, :].rearrange("p (a n) -> p a n", a=4)).then_inc(mat_copied, 1)

            def make_k(h):
                dve.wait_ge(proj_read, 4 * NB)
                step.link(TS(GT[:, h, :], GT[:, h, :], one_minus_lb[:, h:h + 1], lb[:, h:h + 1], ALU.mult, ALU.add))
                step.add(nc.vector.tensor_copy(fs[:, h, :], GT[:, h, TP:T]))
                TS(kT[:, h, :], GT[:, h, :], -1.0, 1.0, ALU.mult, ALU.add).then_inc(k_ready, 1)

            def sum_ln_f(h):
                dve.wait_ge(lnf_done, 1)
                for c0, n in CHUNKS:
                    ins = nc.vector.tensor_tensor_scan(GT[:, h, c0:c0 + n], ones[:, 0:1].broadcast_to([P, n]),
                                                       GT[:, h, c0:c0 + n], 0.0, ALU.mult, ALU.add)
                ins.then_inc(G_ready, 1)

            def add_v_parts(n):
                m = STEPS[n][1]
                dve.wait_ge(proj_read, 2 * n + 2)
                v = v_part[0:TT[2]]
                step.link(TTo(v[:, 0:2, :], v[:, 0:2, :], v[:, 2:4, :], ALU.add))
                TTo(v_tok[0:TT[2], 2, m * CB:(m + 1) * CB], v[:, 0, :], v[:, 1, :], ALU.add).then_inc(v_summed, 1)

            for j in range(NJ):
                b = j % 2
                hst = Hst[j % NHST]
                re, im = PB[4], PB[5]
                cos, sin = turn[b][:, 0], turn[b][:, 1]
                dve.wait_ge(bu_done, j + 1)
                dve.wait_ge(turn_ready, j + 1)
                if j >= NHST:
                    dve.wait_ge(h_used, j - NHST + 1)
                    dve.wait_ge(fin_copied, j - NHST + 1)
                if j >= 1:
                    dve.wait_ge(h_ready, j)
                step.add(TTo(M1[:, 0], re[:, 0:TP], cos, ALU.mult))
                step.add(TTo(M1[:, 1], im[:, 0:TP], cos, ALU.mult))
                step.add(TTo(M2[:, 0], im[:, 0:TP], sin, ALU.mult))
                step.add(TTo(M2[:, 1], re[:, 0:TP], sin, ALU.mult))
                step.add(TTo(hst[:, 0, TP:T], re[:, TP:T], Zs[:, 0, :, j], ALU.add))
                TTo(hst[:, 1, TP:T], im[:, TP:T], Zs[:, 1, :, j], ALU.add).then_inc(bu_read, 1)
                step.settle()
                step.add(TTo(Wt[:, 0], M1[:, 0], M2[:, 0], ALU.add))
                step.link(TTo(Wt[:, 1], M1[:, 1], M2[:, 1], ALU.subtract))
                for z in range(2):
                    step.add(nc.vector.tensor_tensor_scan(Gs[:, z], sc5[:, 0, j:j + 1].broadcast_to([P, TP]), Wt[:, z], 0.0,
                                                          ALU.mult, ALU.add))
                step.settle()
                step.add(TTo(M1[:, 0], Gs[:, 0], cos, ALU.mult))
                step.add(TTo(M1[:, 1], Gs[:, 1], cos, ALU.mult))
                step.add(TTo(M2[:, 0], Gs[:, 1], sin, ALU.mult))
                step.add(TTo(M2[:, 1], Gs[:, 0], sin, ALU.mult))
                step.settle()
                TTo(hst[:, 0, 0:TP], M1[:, 0], M2[:, 0], ALU.subtract).then_inc(turn_used, 1)
                TTo(hst[:, 1, 0:TP], M1[:, 1], M2[:, 1], ALU.add).then_inc(h_ready, 1)
                for i in ((j - 5) // 4,) if j % 4 == 1 and j > 1 else (N5 - 1,) if j == NJ - 1 else ():
                    dve.wait_ge(h_used, 4 * i + 4)
                    STT(uT[:, i, :], uT[:, i, :], vecs[:, V_D + i:V_D + i + 1], PB[6][:, 0:T], ALU.mult, ALU.add) \
                        .then_inc(y5_ready, 1)
                if F_TILE <= j < F_TILE + NH:
                    make_k(j - F_TILE)
                if j >= G_TILE:
                    sum_ln_f(j - G_TILE)
                n = STEP_OF[j] - 1
                if STEPS[n][0] == "v" and STEP_OF[j - 1] == n:
                    add_v_parts(n)
            add_v_parts(NW - 1)

            step.add(nc.vector.tensor_copy(ks[:, :, :], kT[:, :, TP:T]))
            dve.wait_ge(y5_ready, N5)
            dve.wait_ge(v_summed, NB)
            step.link(nc.vector.memset(q_own, 0.0))
            for b in range(NS):
                step.add(nc.vector.tensor_copy(q_own[:, :, b, b:b + 1], qT[:, :, TP + b:TP + b + 1]))
            dve.wait_ge(fin_copied, NJ)
            for b in range(2):
                step.add(nc.vector.memset(att[b], 0.0))
            step.settle()
            for h in range(NH):
                b = h % 2
                dve.wait_ge(exp_ready, h + 1)
                for l, B in enumerate(LV):
                    o = QK[b][:, LO[l]:LO[l] + LW[l]].rearrange("p (n two b) -> p n two b", two=2, b=B)
                    for side, src in ((0, kT), (1, qT)):
                        s = src[:, h, 0:LW[l]].rearrange("p (n two b) -> p n two b", two=2, b=B)
                        TTo(o[:, :, side, :], o[:, :, side, :], s[:, :, side, :], ALU.mult)
                TTo(qG[b], qG[b], qT[:, h, 0:TP], ALU.mult)
                TTo(kG[b], kG[b], kT[:, h, 0:TP], ALU.mult).then_inc(qk_ready, 1)
                dve.wait_ge(v_spread, 16 * (h + 1))
                step.add(TTo(vk, vk, ks[:, :, h:h + 1].broadcast_to([P, NH, P]), ALU.mult))
                step.settle()
                dve.wait_ge(S0_decayed, h + 1)
                TTo(S0[h % 3], S0[h % 3], vk, ALU.add).then_inc(S1_ready, 1)
                for l in range(8):
                    u = 8 * h + l
                    dve.wait_ge(att_done, u + 1)
                    if u:
                        dve.wait_ge(att_read, u)
                    bank = PB[4 + l % 2]
                    ins = nc.vector.copy_predicated(att[b][:, 0:2 * P].rearrange("p (a n) -> p a n", a=2),
                                                    masks[:, l, :].unsqueeze(1).broadcast_to([P, 2, P]),
                                                    bank[:, 0:2 * P].rearrange("p (a n) -> p a n", a=2))
                    if l >= 3:
                        ins = nc.vector.copy_predicated(att[b][0:LAST, 2 * P:TP], masks[0:LAST, l, 0:LAST],
                                                        bank[0:LAST, 2 * P:TP])
                    ins.then_inc(att_read, 1)
                dve.wait_ge(st_done, h + 1)
                if h >= 2:
                    dve.wait_ge(st_stored[b], 16 * (h // 2))
                for q in range(3):
                    part = PB[3][:, q * P:(q + 1) * P]
                    if q == 0:
                        ins = nc.vector.tensor_copy(Sst[b][:, 0, :], part)
                    else:
                        dve.wait_ge(st_ready, 3 * h + q)
                        ins = STT(Sst[b][:, q, :], Sst[b][:, q - 1, :], chunk_decay[b][:, q - 1:q], part, ALU.mult, ALU.add)
                    ins.then_inc(st_ready, 1)

            dve.wait_ge(os_done, NS)
            for half in range(2):
                for a in range(4):
                    rows = slice(32 * a, 32 * a + NS)
                    ins = nc.vector.tensor_copy(o_rows[rows, half, :], PB[half][rows, 0:P])
                    if 4 * half + a == NH - 1:
                        ins.then_inc(os_copied, 1)
                    else:
                        step.add(ins)
            dve.wait_ge(glu_read, NH)
            TTo(uT, uT, sgT, ALU.mult).then_inc(y5g_ready, 1)
            dve.wait_ge(os_turned, 1)
            for a in range(4):
                nc.vector.tensor_copy(kT[:, a::4, TP:T], PB[4 + a][:, 0:2 * NS].rearrange("p (h b) -> p h b", h=2)) \
                    .then_inc(samp_copied, 1)
            dve.wait_ge(rt_ready, 1)
            step.link(nc.vector.reciprocal(rms5, rms5))
            for i in range(N5):
                ins = STT(uT[:, i, :], uT[:, i, :], vecs[:, V_G5 + i:V_G5 + i + 1], rms5, ALU.mult, ALU.mult)
            ins.then_inc(yT_ready, 1)
            dve.wait_ge(rt_ready, 1 + NH)
            step.link(nc.vector.reciprocal(GT, GT))
            for h in range(NH):
                step.add(STT(kT[:, h, :], kT[:, h, :], vecs[:, V_GH + h:V_GH + h + 1], GT[:, h, :], ALU.mult, ALU.mult))
            step.settle()
            dve.wait_ge(silu_done, 1)
            TTo(gT, gT, kT, ALU.mult).then_inc(yT_ready, 1)

            dve.wait_ge(x_again, 16 * 5)
            for o in range(NO):
                for b in range(2):
                    unit = 2 * o + b
                    dve.wait_ge(out_done, unit + 1)
                    cols = slice(o * CB, (o + 1) * CB)
                    if b == 0:
                        x_, p_ = x1[:, 0:2, cols], PB[unit % 4][:, 0:2 * CB].rearrange("p (a n) -> p a n", a=2)
                    else:
                        x_ = x1[0:TT[2], 2, cols]
                        for a in range(3):
                            step.link(TTo(x_, x_, PB[unit % 4][32 * a:32 * a + TT[2], 0:CB], ALU.add))
                        p_ = PB[unit % 4][96:96 + TT[2], 0:CB]
                    TTo(x_, x_, p_, ALU.add).then_inc(x1_ready, 1)

            dve.wait_ge(r_rms, 3)
            step.add(nc.vector.reciprocal(token_stats[:, 3:5], token_stats[:, 0:2]))
            nc.vector.reciprocal(token_stats[0:TT[2], 5:6], token_stats[0:TT[2], 2:3]).then_inc(r_rstd, 1)
            copy_transposed(xn2T, V_FFN, xt2_done, xt2_copied)

            step.add(nc.vector.memset(lg, 0.0))
            step.add(nc.vector.memset(c8, LOWEST))
            dve.wait_ge(wr_loaded, 64)
            dve.wait_ge(logit_done, 1)
            step.settle()
            NL = NG + NE
            step.add(TTo(lg[:, 0:2, :], PB[6][:, 0:2 * NL].rearrange("p (a n) -> p a n", a=2),
                         bias36.unsqueeze(1).broadcast_to([P, 2, NL]), ALU.add))
            step.link(TTo(lg[0:TT[2], 2, :], PB[6][0:TT[2], 2 * NL:3 * NL], bias36[0:TT[2], :], ALU.add))
            step.link(nc.vector.tensor_copy(c8[:, :, 0:NG], lg[:, :, 0:NG]))
            for tile in range(3):
                step.add(nc.vector.max(out=gmax[:, tile, :], in_=c8[:, tile, :]))
            step.settle()
            for tile in range(3):
                step.add(nc.vector.max_index(out=gidx[:, tile, :], in_max=gmax[:, tile, :], in_values=c8[:, tile, :]))
            TTo(e8, lg[:, :, 0:NG], gmax[:, :, 0:1].broadcast_to([P, 3, NG]), ALU.subtract).then_inc(sm_in, 1)
            step.settle()
            step.link(nc.vector.tensor_copy(grp, gidx[:, :, 0]))
            step.link(TTo(ohg, iota32[:, 0:NG].unsqueeze(1).broadcast_to([P, 3, NG]),
                          grp.unsqueeze(2).broadcast_to([P, 3, NG]), ALU.is_equal))
            for tile in range(3):
                step.add(TTo(pick[:, tile], lg[:, tile, NG:NL].rearrange("p (g j) -> p g j", g=NG),
                             ohg[:, tile, :].unsqueeze(2).broadcast_to([P, NG, EG]), ALU.mult))
            step.settle()
            for tile in range(3):
                step.add(nc.vector.tensor_reduce(f8[:, tile, :], pick[:, tile].rearrange("p g j -> p j g"), AX.X, ALU.add))
            step.settle()
            for tile in range(3):
                step.add(nc.vector.max(out=fmax[:, tile, :], in_=f8[:, tile, :]))
            step.settle()
            for tile in range(3):
                step.add(nc.vector.max_index(out=fidx[:, tile, :], in_max=fmax[:, tile, :], in_values=f8[:, tile, :]))
            step.settle()
            TTo(dv, fmax[:, :, 1], fmax[:, :, 0], ALU.subtract).then_inc(sm_in, 1)
            step.add(nc.vector.tensor_copy(e0, fidx[:, :, 0]))
            step.link(nc.vector.tensor_copy(e1, fidx[:, :, 1]))
            step.add(STT(e0, grp, float(EG), e0, ALU.mult, ALU.add))
            step.add(STT(e1, grp, float(EG), e1, ALU.mult, ALU.add))
            step.link(TS(valid, tid, float(T), None, ALU.is_lt))
            for o_, e_ in ((OH0, e0), (OH1, e1)):
                step.add(TTo(o_, iota32.unsqueeze(1).broadcast_to([P, 3, NE]), e_.unsqueeze(2).broadcast_to([P, 3, NE]), ALU.is_equal))
            step.settle()
            for o_ in (OH0, OH1):
                step.add(TTo(o_, o_, valid.unsqueeze(2).broadcast_to([P, 3, NE]), ALU.mult))
            step.settle()
            TTo(Mr, OH0, OH1, ALU.add).then_inc(route_ready, 1)
            dve.wait_ge(sm_exp, 2)
            step.add(nc.vector.tensor_reduce(pgi, e8, AX.X, ALU.add))
            step.link(TS(w0, dv, 1.0, None, ALU.add))
            step.link(TTo(w0, w0, pgi, ALU.mult))
            step.link(nc.vector.reciprocal(w0, w0))
            step.link(TTo(w1, w0, dv, ALU.mult))
            step.add(nc.vector.memset(PL, 0.0))
            step.add(nc.vector.memset(rankm, -1.0))
            step.settle()
            tidb = tid.unsqueeze(2).broadcast_to([P, 3, NE])
            step.add(TTo(pick.rearrange("p a g j -> p a (g j)"), OH0, w0.unsqueeze(2).broadcast_to([P, 3, NE]), ALU.mult))
            step.add(TTo(PL[:, :, 0:NE, 2], OH1, w1.unsqueeze(2).broadcast_to([P, 3, NE]), ALU.mult))
            step.add(TS(PL[:, :, 0:NE, 0], tidb, -BIG, None, ALU.add))
            step.link(STT(PL[:, :, 0:NE, 1], OH1, float(T), tidb, ALU.mult, ALU.add))
            step.add(TTo(PL[:, :, 0:NE, 2], PL[:, :, 0:NE, 2], pick.rearrange("p a g j -> p a (g j)"), ALU.add))
            step.link(TS(PL[:, :, 0:NE, 1], PL[:, :, 0:NE, 1], -BIG, None, ALU.add))
            dve.wait_ge(rank_done, 1)
            step.add(TTo(rankm[:, :, 0:NE], PB[7][:, 0:3 * NE].rearrange("p (a n) -> p a n", a=3), Mr, ALU.mult))
            step.link(nc.vector.tensor_reduce(maxn, PB[7][:, 3 * NE:4 * NE], AX.X, ALU.max))
            step.add(TTo(rankm[:, :, 0:NE], rankm[:, :, 0:NE], Mr, ALU.add))
            for r in range(1, ROUNDS):
                step.add(TS(ext[:, r - 1:r], maxn, float(CAP * r), None, ALU.is_gt))
            step.settle()
            step.add(TS(rankm[:, :, 0:NE], rankm[:, :, 0:NE], -1.0, None, ALU.add))
            step.link(nc.vector.tensor_reduce(maxn, ext, AX.X, ALU.add))
            nc.vector.tensor_copy(extra_i[:, :], maxn).then_inc(lists_ready, 1)
            nc.vector.engine_nop().then_inc(h_made, 1)
            dve.wait_ge(lists_ready, 1)

            def places(e):
                TTo(oh[:, :, :], rankm[:, :, bass.ds(e, 1)].broadcast_to([P, 3, CAP]),
                    slotid.unsqueeze(1).broadcast_to([P, 3, CAP]), ALU.is_equal).then_inc(oh_ready, 1)

            def indices(g, p):
                dve.wait_ge(list_done, g + 1)
                TS(idx_tok[p][:, :], PB[7][0:CAP, 0:1], BIG, None, ALU.add)
                TS(idx_dst[p][:, :], PB[7][0:CAP, 1:2], BIG, None, ALU.add)
                nc.vector.tensor_copy(gcol[p][:, :], PB[7][0:CAP, 2:3]).then_inc(idx_ready, 1)

            def rows_in(g, p):
                dve.wait_ge(tr_done, g + 2)
                for q in range(2):
                    ins = TTo(xgT[p][:, 8 * q:8 * q + 8, :], PB[4 + q][:, :].rearrange("p (a n) -> p a n", a=8),
                              vecs[:, V_FFN + 8 * q:V_FFN + 8 * q + 8].unsqueeze(2).broadcast_to([P, 8, CAP]), ALU.mult)
                ins.then_inc(xgT_ready, 1)

            def round_dve(R):
                g0 = R * (NE + 1)
                if not is_first(R):
                    dve.wait_ge(list_done, g0)
                    TS(rankm, rankm, -float(CAP), None, ALU.add).then_inc(lists_ready, 1)
                    dve.wait_ge(lists_ready, R + 1)
                    dve.wait_ge(rows_free, R * NE + 2)
                places(0)
                indices(g0, 0)
                rows_in(g0, 0)
                with dve.Fori(0, NE // 2) as i:
                    for b in range(2):
                        x = i * 2 + (R * NE + b)
                        g = i * 2 + (R * (NE + 1) + b + 1)
                        dve.wait_ge(list_done, g)
                        places(i * 2 + (b + 1))
                        dve.wait_ge(rows_free, x + 2)
                        indices(g, 1 - b)
                        dve.wait_ge(act_ready, x + 1)
                        STT(hh[0:CAP, :], sg[0:CAP, :], gcol[b][:, 0:1], up[0:CAP, :], ALU.mult, ALU.mult).then_inc(h_made, 1)
                        dve.wait_ge(hT_done, x + 1)
                        nc.vector.tensor_copy(hT, PB[6][:, 0:KF * CAP].rearrange("p (a n) -> p a n", a=KF)).then_inc(hT_ready, 1)
                        rows_in(g, 1 - b)

            run_rounds(dve, round_dve)
            dve.wait_ge(moe_done, 1)
            dve.wait_ge(gfin_loaded, 16)
            for tile in range(3):
                n = TT[tile]
                dve.wait_ge(yrow_loaded[tile % 2], 32 * (tile // 2 + 1))
                y0, y1 = yrow[2 * (tile % 2)], yrow[2 * (tile % 2) + 1]
                xt = x1[0:n, tile, :]
                step.link(TTo(xt, xt, y0[0:n, :], ALU.add))
                TTo(xt, xt, y1[0:n, :], ALU.add).then_inc(ysum_done, 1)
                dve.wait_ge(f_rms, tile + 1)
                r = token_stats[0:n, 3 + tile:4 + tile]
                step.link(nc.vector.reciprocal(r, token_stats[0:n, tile:tile + 1]))
                STT(xt, xt, r, gfin[0:n, :], ALU.mult, ALU.mult).then_inc(out_ready, 1)


_INS = ['x_prompt', 'x_sample', 'state_s5_re', 'state_s5_im', 'state_hgrn', 'meta_tokens', 'norm_mix', 'w_in',
        's5_A_re', 's5_A_im', 's5_log_step', 's5_B_re', 's5_B_im', 's5_C_re', 's5_C_im', 's5_D', 's5_w_glu',
        's5_b_glu', 's5_out_gain', 'hg_lb_logits', 'hg_out_gain', 'w_out', 'norm_ffn', 'w_coarse', 'b_coarse',
        'w_fine', 'b_fine', 'w_gate', 'w_up', 'w_down', 'norm_final']
_OUTS = ['y_prompt', 'y_sample', 's5_re_prompt', 's5_im_prompt', 'hgrn_prompt', 's5_re_sample', 's5_im_sample',
         'hgrn_sample']


def kernel(**inputs):
    import numpy as _np
    import concourse.bacc as _bacc
    from concourse import mybir as _mybir
    from concourse.bass_utils import run_bass_kernel_spmd as _run

    nc = _bacc.Bacc("TRN2", target_bir_lowering=False, num_devices=1)
    arrays, args = {}, {}
    for name in _INS:
        a = _np.ascontiguousarray(inputs[name])
        arrays[f"in_{name}_dram"] = a
        args[name] = nc.dram_tensor(f"in_{name}_dram", a.shape, _mybir.dt.from_np(a.dtype), kind="ExternalInput").ap()
    g5, p5 = inputs["s5_A_re"].shape[1:]
    nh, dk, dv = inputs["state_hgrn"].shape[2:]
    ns = inputs["x_sample"].shape[0]
    shapes = [inputs["x_prompt"].shape, inputs["x_sample"].shape, (1, 1, g5, p5), (1, 1, g5, p5),
              (1, 1, nh, dk, dv), (1, ns, g5, p5), (1, ns, g5, p5), (1, ns, nh, dk, dv)]
    for name, shape in zip(_OUTS, shapes):
        args[name] = nc.dram_tensor(f"out_{name}_dram", shape, _mybir.dt.float32, kind="ExternalOutput").ap()
    hymba_step(nc, args)
    r = _run(nc, [arrays], core_ids=[0])
    return tuple(r.results[0][f"out_{name}_dram"] for name in _OUTS)
```

```python
import math
from contextlib import ExitStack

import concourse.bass as bass
from concourse import mybir

F32 = mybir.dt.float32
I32 = mybir.dt.int32
U32 = mybir.dt.uint32
U8 = mybir.dt.uint8
ALU = mybir.AluOpType
ACT = mybir.ActivationFunctionType
AX = mybir.AxisListType

P = 128
EPS = 1e-6
MAGIC = 1.5 * 2.0 ** 23
TWO_PI_HI = 6.28125
TWO_PI_LO = 2 * math.pi - TWO_PI_HI
PI_BELOW = 3.1415925
BIG = 1024.0
LOWEST = -3.0e38


class Chain:

    def __init__(self, eng, sem):
        self.eng, self.sem, self.n = eng, sem, 0

    def add(self, ins):
        ins.then_inc(self.sem, 1)
        self.n += 1

    def settle(self):
        self.eng.wait_ge(self.sem, self.n)

    def link(self, ins):
        self.add(ins)
        self.settle()


def hymba_step(nc, t):
    SEQ, D = t["x_prompt"].shape[1:]
    NS = t["x_sample"].shape[0]
    NM = t["meta_tokens"].shape[0]
    TP = NM + SEQ
    T = TP + NS
    TT = [P, P, T - 2 * P]
    TILE_ORDER = (2, 0, 1)
    KD = D // P
    G5, P5, C5 = t["s5_B_re"].shape[1:]
    W5 = G5 * C5
    N5 = W5 // P
    NJ = G5 * P5 // P
    HG = t["hg_out_gain"].shape[1]
    NH = HG // P
    NE, _, FH = t["w_gate"].shape[1:]
    NG = t["w_coarse"].shape[2]
    EG = NE // NG
    KF = FH // P
    CB = 256
    CAP = 64
    ROUNDS = -(-T // CAP)
    LAST = TP - 2 * P
    assert D == 2 * W5 == 2 * HG and NE % 2 == 0 and T <= 3 * P and NS == NH and TT[2] == LAST + NS

    ctx = ExitStack()
    with ctx:
        def sb(name, shape, dt=F32):
            return ctx.enter_context(nc.sbuf_tensor(name, shape, dt))

        def sem(name):
            return ctx.enter_context(nc.semaphore(name))

        SLOT = KD * CB
        ring = sb("ring", [P, 6, SLOT])
        AR_N = 5 * N5 * T + KD * T + 2 * 33 * NJ + 8536
        arena = sb("arena", [P, AR_N])
        ident = sb("ident", [P, P])
        ones = sb("ones", [P, P])
        upper = sb("upper", [P, P])
        vecs = sb("vecs", [P, 80])
        sc5 = sb("sc5", [P, 6, NJ])
        masks = sb("masks", [P, 8, P], U8)
        eps_col = sb("eps_col", [P, 1])
        token_stats = sb("token_stats", [P, 8])
        lb, one_minus_lb, lb_tmp = sb("lb", [P, NH]), sb("one_minus_lb", [P, NH]), sb("lb_tmp", [P, 3, NH])
        parity = sb("parity", [P, 3])
        fs, ks = (sb(n, [P, NH, NS]) for n in ("f_samples", "k_samples"))
        one_of_eight = sb("one_of_eight", [P, 2 * NH - 1])
        chunk_decay = [sb(f"chunk_decay{i}", [P, 2]) for i in range(2)]

        class Carver:
            def __init__(self, base, at):
                self.base, self.at = base, at

            def __call__(self, *shape):
                n = math.prod(shape)
                v = self.base[:, self.at:self.at + n]
                self.at += n
                if len(shape) > 1:
                    names = "abcd"[:len(shape)]
                    v = v.rearrange(f"p ({' '.join(names)}) -> p {' '.join(names)}",
                                    **{n_: s for n_, s in zip(names, shape)})
                return v

        upair = ring[:, 4:6, :].rearrange("p a n -> p (a n)")

        c = Carver(arena, 0)
        uT, gT = c(N5, T), c(NH, T)
        gT_at, x1_at = N5 * T, c.at
        qT, GT, kT = c(NH, T), c(NH, T), c(NH, T)
        xnT_at = c.at
        xnT = c(KD, T)
        tab_at = c.at
        turn_table = c(2, NJ, 33)
        rest_at = c.at
        c = Carver(arena, rest_at)
        turn = [c(2, TP), c(2, TP)]
        turn_tmp = [c(2, TP), c(2, TP)]
        M1, M2, Wt, Gs = c(2, TP), c(2, TP), c(2, TP), c(2, TP)
        NHST = 5
        Hst = [c(2, T) for _ in range(NHST)]
        assert c.at <= rest_at + 7168
        c = Carver(arena, rest_at)
        Braw, BP = [c(NJ, C5), c(NJ, C5)], [c(N5, P), c(N5, P)]
        Craw, CP = [c(N5, P5), c(N5, P5)], [c(N5, 2, P5), c(N5, 2, P5)]
        Btmp = [c(NJ, C5), c(NJ, C5)]
        assert c.at == rest_at + 7168
        Zs, fin = c(2, NS, NJ), c(2, 1 + NS, NJ)
        rms5 = c(T)
        assert c.at <= AR_N
        LV = [64, 32, 16, 8, 4, 2, 1]
        LW = [TP if b <= 8 else 2 * P for b in LV]
        LO = [sum(LW[:i]) for i in range(len(LV))]
        c = Carver(arena, rest_at)
        QK = [c(sum(LW)), c(sum(LW))]
        att, qG, kG = ([c(TP), c(TP)] for _ in range(3))
        kGt, Sst = ([c(3, P), c(3, P)] for _ in range(2))
        assert c.at <= rest_at + 7168
        c = Carver(arena, tab_at)
        S0_last, vk = c(NH, P), c(NH, P)
        assert c.at <= rest_at
        c = Carver(arena, xnT_at)
        fin_rows, o_rows = c(2, 3, P), c(2, P)
        c = Carver(arena, gT_at)
        vrow, h0row, r5 = c(P), c(2, 2, P), c(12, P)
        assert c.at <= x1_at
        xraw = Carver(arena, x1_at)(3, D)
        c = Carver(upair, 0)
        v_tok = c(3, HG)
        mat_at = c.at
        BT, CT = [c(N5, P), c(N5, P)], [c(N5, P), c(N5, P)]
        v_part = c(4, CB)
        assert c.at <= 2 * SLOT
        c = Carver(upair, mat_at)
        sgT = c(N5, T)
        S0 = [c(NH, P), c(NH, P), S0_last]
        q_own = c(NH, NS, NS)
        assert c.at <= 2 * SLOT
        c = Carver(upair, 0)
        xsq = c(D)
        ang_r, ang_n, ang_cos, ang_sin = (c(NJ, 33) for _ in range(4))
        z_tmp = [c(NS, NJ), c(NS, NJ)]
        assert c.at <= 2 * SLOT
        c = Carver(arena, tab_at)
        iI, iJ, iX, iota_i = (c(P).bitcast(I32) for _ in range(4))
        mX, mG, mL = c(P), c(P), c(P)
        c = Carver(arena, x1_at)
        x1, wr = c(3, D), c(KD, NG + NE)
        assert c.at <= xnT_at
        xn2T = Carver(arena, xnT_at)(KD, T)
        oh = Carver(arena, xnT_at)(3, CAP)
        c = Carver(arena, tab_at)
        lgT = Carver(arena, tab_at)(T)
        _, xg0, xg1 = c(D), c(D), c(D)
        xg = [xg0, xg1]
        yout = [c(D), c(D)]
        assert c.at <= AR_N
        c = Carver(arena, 0)
        xgT = [c(KD, CAP), c(KD, CAP)]
        sg, up, hh = c(FH), c(FH), c(FH)
        hT = c(KF, CAP)
        lg, c8, e8, pick, f8 = c(3, NG + NE), c(3, 8), c(3, NG), c(3, NG, EG), c(3, EG)
        OH0, OH1, Mr = c(3, NE), c(3, NE), c(3, NE)
        assert c.at <= x1_at
        yrow = [ring[:, i // 2, (i % 2) * D:(i % 2 + 1) * D] for i in range(6)]
        gfin = Carver(arena, xnT_at + 3 * CAP)(D)
        ynorm = Carver(arena, tab_at)(D)
        V_COLS = D - 640
        route = sb("route", [P, 707])
        c = Carver(route, 0)
        bias36 = c(NG + NE)
        tid, valid, pgi, dv, w0, w1, grp, e0, e1 = (c(3) for _ in range(9))
        ohg = c(3, NG)
        iota32, slotid = c(NE), c(CAP)
        rankm = c(3, NE + 1)
        PL = c(3, NE + 1, 4)
        maxn, ext, mvals = c(1), c(ROUNDS - 1), c(33)
        assert c.at <= 707
        gmax, fmax = sb("gmax", [P, 3, 8]), sb("fmax", [P, 3, 8])
        gidx, fidx = sb("gidx", [P, 3, 8], U32), sb("fidx", [P, 3, 8], U32)
        extra_i = sb("extra_i", [P, 1], I32)
        idx_tok = [sb(f"idx_tok{i}", [CAP, 1], U32) for i in range(2)]
        idx_dst = [sb(f"idx_dst{i}", [CAP, 1], U32) for i in range(2)]
        gcol = [sb(f"gcol{i}", [CAP, 1]) for i in range(2)]
        rcol = [sb(f"rcol{i}", [CAP, 1]) for i in range(2)]
        square_sums = sb("square_sums", [P, 3, D // CB])

        PB = [ctx.enter_context(nc.psum_tensor(f"bank{i}", [P, 512], F32)) for i in range(8)]
        x1_dram = nc.dram_tensor("x1_rows", [T, D], F32, kind="Internal").ap()
        v_dram = nc.dram_tensor("v_samples", [NS, HG], F32, kind="Internal").ap()
        y_dram = nc.dram_tensor("expert_rows", [2 * T, D], F32, kind="Internal").ap()

        V_MIX, V_FFN, V_D, V_BGLU, V_G5, V_LB0, V_LB1, V_GH = 0, KD, 32, 40, 48, 56, 64, 72

        def sems(names):
            return [sem(n) for n in names.split()]

        x_loaded = [sem(f"x_loaded{i}") for i in range(3)]
        vec_loaded, s5_loaded, bc_loaded, wr_loaded = sems("vec_loaded s5_loaded bc_loaded wr_loaded")
        slot_loaded = [sem(f"slot_loaded{i}") for i in range(6)]
        pool_consts, dve_consts, act_step, dve_step, pool_step = sems("pool_consts dve_consts act_step dve_step pool_step")
        x_rms, xn_made, xt_done, xt_copied, vec_t, vec_copied = sems("x_rms xn_made xt_done xt_copied vec_t vec_copied")
        lb_in, lb_exp = sems("lb_in lb_exp")
        s5_exp_in, s5_exp, s5_sin_in, s5_sin, s5r_ready = sems("s5_exp_in s5_exp s5_sin_in s5_sin s5r_ready")
        par_t, par_copied, ang_ready, table_ready = sems("par_t par_copied ang_ready table_ready")
        mat_ready, mat_t, mat_copied = sems("mat_ready mat_t mat_copied")
        proj_done, proj_read, v_summed, g_done, g_read, silu_done = sems(
            "proj_done proj_read v_summed g_done g_read silu_done")
        bu_done, bu_read, turn_ready, turn_used = sems("bu_done bu_read turn_ready turn_used")
        h_ready, h_used, y5_ready, fin_copied = sems("h_ready h_used y5_ready fin_copied")
        gelu_done, k_ready, lnf_done, G_ready = sems("gelu_done k_ready lnf_done G_ready")
        diff_ready, exp_ready, qk_ready, att_done, att_read = sems("diff_ready exp_ready qk_ready att_done att_read")
        kgt_done, kgt_copied, st_done, st_ready, o_done, o_copied = sems("kgt_done kgt_copied st_done st_ready o_done o_copied")
        S0_loaded = [sem(f"S0_loaded{i}") for i in range(3)]
        S0_stored = [sem(f"S0_stored{i}") for i in range(3)]
        st_stored = [sem(f"st_stored{i}") for i in range(2)]
        S0_decayed, v_stored, v_spread, S1_ready, os_done = sems("S0_decayed v_stored v_spread S1_ready os_done")
        os_copied, os_turned, samp_copied = sems("os_copied os_turned samp_copied")
        glu_done, glu_read, y5g_ready, sq_ready, ss_done, rt_ready, yT_ready = sems(
            "glu_done glu_read y5g_ready sq_ready ss_done rt_ready yT_ready")
        banks_clear, rstd_ready, spread_done, spread_read = sems("banks_clear rstd_ready spread_done spread_read")
        fin_t, fin_read, fin_stored = sems("fin_t fin_read fin_stored")
        x_again, out_done, x1_ready = sems("x_again out_done x1_ready")
        squares_ready, r_sum, r_rms, x1_stored, xt2_done, xt2_copied = sems(
            "squares_ready r_sum r_rms x1_stored xt2_done xt2_copied")
        part_logits, logitsT_ready, logit_done, sm_in, sm_exp, route_ready, rank_done, lists_ready = sems(
            "part_logits logitsT_ready logit_done sm_in sm_exp route_ready rank_done lists_ready")
        oh_ready, list_done, idx_ready, dst_ready, tr_done, xgT_ready, wait_carried = sems(
            "oh_ready list_done idx_ready dst_ready tr_done xgT_ready wait_carried")
        gathered, scattered = ([sem(f"{n}{i}") for i in range(2)] for n in ("gathered", "scattered"))
        gate_up_done, act_ready, h_made, hT_done, hT_ready, down_done, rows_ready, rows_free = sems(
            "gate_up_done act_ready h_made hT_done hT_ready down_done rows_ready rows_free")
        moe_done, gfin_loaded, ysum_done, f_rms, out_ready, out_stored = sems(
            "moe_done gfin_loaded ysum_done f_rms out_ready out_stored")
        yrow_loaded = [sem(f"yrow_loaded{i}") for i in range(3)]
        ysum_pool, rstd_last, out_ready_pool = sems("ysum_pool rstd_last out_ready_pool")

        PART_AT = {"u": 0, "q": W5, "f": W5 + HG, "v": W5 + 2 * HG, "g": W5 + 3 * HG}
        NB = W5 // CB
        STEPS = [(part, m) for part in "ufqv" for m in range(NB)]
        NW, NO = len(STEPS), D // CB
        PRE_SLOTS = 4
        HEAD_BLOCKS = [("g", 0, 2), ("glu", 0, 4), ("g", 1, 4), ("g", 2, 6), ("glu", 1, 8), ("g", 3, 8)]
        G_BLOCK = [NW + i for i, blk in enumerate(HEAD_BLOCKS) if blk[0] == "g"]
        GLU_BLOCK = [NW + i for i, blk in enumerate(HEAD_BLOCKS) if blk[0] == "glu"]
        OUT_AT = NW + len(HEAD_BLOCKS)
        NPRE = OUT_AT + NO
        FILLS = [len(range(s, NPRE, PRE_SLOTS)) for s in range(4)] + [0, 0]
        MOE_SLOT = (2, 3, 0, 1)
        EIGHTHS = 8
        S5_TILES = {}
        for j in range(NJ):
            at = EIGHTHS * NB + j * EIGHTHS * (NW - NB) // NJ
            S5_TILES[divmod(at, EIGHTHS)] = j
        STEP_OF = {j: n for (n, _), j in S5_TILES.items()}
        assert len(S5_TILES) == NJ
        PARAMETERS_AT = [(NB - 2, 0), (NB - 1, 0), (NB - 1, 4)]

        PROJ_BANKS = 3
        BU_BANKS = ((4, 5), (7, 3))

        def half_tiles(n, b):
            per_half = EIGHTHS if STEPS[n][0] == "v" else EIGHTHS // 2
            return [S5_TILES[n, q] for q in range(b * per_half, min((b + 1) * per_half, EIGHTHS)) if (n, q) in S5_TILES]
        CHUNKS = ((0, P), (P, P), (2 * P, LAST))
        F_TILE = min(j for j in range(NJ) if STEPS[STEP_OF[j]][0] == "q") + 1
        LN_STEP = STEP_OF[F_TILE + NH - 1] + 1
        G_TILE = NJ - NH
        assert STEP_OF[G_TILE] > LN_STEP

        def token_rows(tile):
            meta, prompt, sample = t["meta_tokens"], t["x_prompt"][0], t["x_sample"][:, 0]
            if tile == 0:
                return [(0, meta), (NM, prompt[0:P - NM])]
            if tile == 1:
                return [(0, prompt[P - NM:2 * P - NM])]
            return [(0, prompt[2 * P - NM:SEQ]), (LAST, sample)]

        def slot(s, k):
            return ring[:, s, :].rearrange("p (k n) -> p k n", k=k)

        def run_rounds(eng, one_round):
            one_round(0)
            eng.wait_ge(lists_ready, 1)
            extra = eng.value_load(extra_i[0:1, 0:1], min_val=0, max_val=ROUNDS - 1)
            with eng.If(extra > 0):
                with eng.Fori(0, extra) as r:
                    one_round(r + 1)

        def is_first(R):
            return isinstance(R, int)

        block = ctx.enter_context(nc.Block())

        @block.sync
        def _(sp):
            def load_gate_up(e, q):
                w = t["w_gate"] if q % 2 == 0 else t["w_up"]
                half = D // 2
                src = w[0][bass.ds(e, 1), (q // 2) * half:(q // 2 + 1) * half, :]
                sp.dma_start(slot(MOE_SLOT[q], KD // 2), src.rearrange("a (k p) n -> p (a k) n", p=P)) \
                    .then_inc(slot_loaded[MOE_SLOT[q]], 16)

            def load_down(e, s):
                half = FH // 2
                src = t["w_down"][0][bass.ds(e, 1), (s - 4) * half:(s - 3) * half, :]
                sp.dma_start(slot(s, KF // 2), src.rearrange("a (k p) n -> p (a k) n", p=P)) \
                    .then_inc(slot_loaded[s], 16)

            def pre_load(n):
                last = n - PRE_SLOTS
                if last >= OUT_AT:
                    sp.wait_ge(out_done, 2 * (last - OUT_AT + 1))
                elif last >= NW:
                    kind, _, used = HEAD_BLOCKS[last - NW]
                    sp.wait_ge(g_done if kind == "g" else glu_done, used)
                elif last >= 0:
                    sp.wait_ge(proj_done, 2 * (last + 1))
                if n < OUT_AT:
                    part, m = STEPS[n] if n < NW else HEAD_BLOCKS[n - NW][:2]
                    if part == "glu":
                        src = t["s5_w_glu"][0, :, m * 2 * CB:(m + 1) * 2 * CB]
                    else:
                        c0 = PART_AT[part] + m * CB
                        src = t["w_in"][0, :, c0:c0 + CB]
                else:
                    o = n - OUT_AT
                    src = t["w_out"][0, :, o * CB:(o + 1) * CB]
                sp.dma_start(slot(n % PRE_SLOTS, src.shape[0] // P), src.rearrange("(k p) n -> p k n", p=P)) \
                    .then_inc(slot_loaded[n % PRE_SLOTS], 16)

            def load_vectors():
                for name, at in (("norm_mix", V_MIX), ("norm_ffn", V_FFN), ("s5_D", V_D), ("s5_b_glu", V_BGLU),
                                 ("s5_out_gain", V_G5), ("hg_lb_logits", V_LB0), ("hg_out_gain", V_GH)):
                    rows = t[name].rearrange("a (k p) -> (a k) p", p=P)
                    sp.dma_start(vrow[at:at + rows.shape[0], :], rows).then_inc(vec_loaded, 16)

            for tile in TILE_ORDER:
                for at, rows in token_rows(tile):
                    sp.dma_start(xraw[at:at + rows.shape[0], tile, :], rows).then_inc(x_loaded[tile], 16)
                if tile == TILE_ORDER[0]:
                    load_vectors()
            for n in range(NW + PRE_SLOTS):
                pre_load(n)

            def load_S0(b):
                if b >= 3:
                    sp.wait_ge(os_done, b - 2)
                    sp.wait_ge(S0_stored[b % 3], 16 * (b // 3))
                else:
                    sp.wait_ge(y5_ready, N5)
                    sp.wait_ge(v_summed, NB)
                sp.dma_start(S0[b % 3], t["state_hgrn"][0, b].rearrange("h k v -> k h v")).then_inc(S0_loaded[b % 3], 16)

            def spread_v(b):
                if b:
                    sp.wait_ge(S1_ready, b)
                sp.dma_start(vk, v_dram[b:b + 1, :].broadcast_to([P, HG])).then_inc(v_spread, 16)

            sp.wait_ge(v_summed, NB)
            sp.dma_start(v_dram, v_tok[LAST:TT[2], 2, :]).then_inc(v_stored, 16)
            load_S0(0)
            sp.wait_ge(v_stored, 16)
            spread_v(0)
            load_S0(1)
            load_S0(2)
            for b in range(NS):
                sp.wait_ge(S1_ready, b + 1)
                if b + 1 < NS:
                    spread_v(b + 1)
                sp.dma_start(t["hgrn_sample"][0, b].rearrange("h k v -> k h v"), S0[b % 3]).then_inc(S0_stored[b % 3], 16)
                sp.wait_ge(st_ready, 3 * (b + 1))
                sp.dma_start(t["hgrn_prompt"][0, 0, b], Sst[b % 2][:, 2, :]).then_inc(st_stored[b % 2], 16)
                if b + 3 < NS:
                    load_S0(b + 3)
                for n in {0: (20,), 2: (22,), 3: (21,), 4: (23,)}.get(b, ()):
                    pre_load(n)

            sp.wait_ge(yT_ready, 2)
            for tile in range(3):
                for at, rows in token_rows(tile):
                    sp.dma_start(x1[at:at + rows.shape[0], tile, :], rows).then_inc(x_again, 16)
            sp.dma_start(wr[:, :, 0:NG], t["w_coarse"][0].rearrange("(k p) n -> p k n", p=P)).then_inc(wr_loaded, 16)
            sp.dma_start(wr[:, :, NG:NG + NE], t["w_fine"][0].rearrange("(k p) n -> p k n", p=P)).then_inc(wr_loaded, 16)
            for n in range(OUT_AT + 2, NPRE):
                pre_load(n)
            for b in range(2):
                sp.wait_ge(S0_stored[b], 16 * len(range(b, NS, 3)))
            for s in (4, 5):
                load_down(0, s)
            for q in range(4):
                sp.wait_ge(out_done, 2 * (NO - 3 + q))
                load_gate_up(0, q)

            def round_loads(R):
                with sp.Fori(1 if is_first(R) else 0, NE) as e:
                    x = e + R * NE
                    for q in range(4):
                        sp.wait_ge(gate_up_done, x * 2 + (q // 2 - 1))
                        load_gate_up(e, q)
                    for s in (4, 5):
                        sp.wait_ge(down_done, x * 2 + (s - 5))
                        load_down(e, s)

            sp.wait_ge(x1_ready, 2 * NO)
            for tile in range(3):
                sp.dma_start(x1_dram[tile * P:tile * P + TT[tile], :], x1[0:TT[tile], tile, :]).then_inc(x1_stored, 16)
            sp.wait_ge(logit_done, 1)
            sp.dma_start(gfin, t["norm_final"].rearrange("(a n) -> a n", a=1).broadcast_to([P, D])).then_inc(gfin_loaded, 16)

            run_rounds(sp, round_loads)

            sp.wait_ge(moe_done, 1)
            for tile in TILE_ORDER:
                for j in range(2):
                    r0 = j * T + tile * P
                    sp.dma_start(yrow[2 * tile + j][0:TT[tile], :], y_dram[r0:r0 + TT[tile], :]).then_inc(yrow_loaded[tile], 16)
            y = t["y_prompt"][0]
            for i, tile in enumerate(TILE_ORDER):
                sp.wait_ge(out_ready, i + 1)
                sp.wait_ge(out_ready_pool, i + 1)
                if tile == 0:
                    sp.dma_start(y[0:P - NM, :], x1[NM:P, 0, :]).then_inc(out_stored, 16)
                elif tile == 1:
                    sp.dma_start(y[P - NM:2 * P - NM, :], x1[:, 1, :]).then_inc(out_stored, 16)
                else:
                    sp.dma_start(y[2 * P - NM:SEQ, :], x1[0:LAST, 2, :]).then_inc(out_stored, 16)
                    sp.dma_start(t["y_sample"][:, 0, :], x1[LAST:LAST + NS, 2, :]).then_inc(out_stored, 16)
            sp.wait_ge(out_stored, 64)
            for b in range(3):
                sp.wait_ge(S0_stored[b], 16 * len(range(b, NS, 3)))
            for b in range(2):
                sp.wait_ge(st_stored[b], 16 * NH // 2)

        @block.scalar
        def _(act):
            act.dma_start(r5[0:NJ, 0, :], t["s5_A_re"].rearrange("a (j g) p -> (a j) (g p)", g=2)).then_inc(s5_loaded, 16)
            act.dma_start(r5[0:NJ, 1, :], t["s5_A_im"].rearrange("a (j g) p -> (a j) (g p)", g=2)).then_inc(s5_loaded, 16)
            act.dma_start(r5[0:NJ, 2, 0:2], t["s5_log_step"].rearrange("a (j g) -> (a j) g", g=2)).then_inc(s5_loaded, 16)
            for z, name in enumerate(("state_s5_re", "state_s5_im")):
                src = t[name][0].rearrange("(h b) (j g) p -> h b j (g p)", g=2, h=2)
                for half in range(2):
                    act.dma_start(h0row[:, z, half, :], src[half].rearrange("b j n -> (b j) n")).then_inc(s5_loaded, 16)
            step = Chain(act, act_step)

            def token_rms(src, scratch, tile, signal):
                n = TT[tile]
                s = token_stats[0:n, tile:tile + 1]
                step.link(nc.scalar.activation(scratch[0:n, :], src[0:n, tile, :], ACT.Square, accum_out=s))
                nc.scalar.activation(s, s, ACT.Sqrt, bias=eps_col[0:n, :], scale=1.0 / D).then_inc(signal, 1)

            act.wait_ge(dve_consts, 1)
            nc.scalar.activation(token_stats[:, 7:8], eps_col[:, :], ACT.Sqrt)
            for tile in TILE_ORDER:
                act.wait_ge(x_loaded[tile], 16 * len(token_rows(tile)))
                token_rms(xraw, xsq, tile, x_rms)
            for z, (bn, cn) in enumerate((("s5_B_re", "s5_C_re"), ("s5_B_im", "s5_C_im"))):
                act.dma_start(Braw[z], t[bn][0].rearrange("(j g) p c -> (g p) j c", g=2)).then_inc(bc_loaded, 16)
                act.dma_start(Craw[z], t[cn][0].rearrange("(i g) c p -> (g c) i p", g=8)).then_inc(bc_loaded, 16)
            act.dma_start(bias36[:, 0:NG], t["b_coarse"].broadcast_to([P, NG])).then_inc(wr_loaded, 16)
            act.dma_start(bias36[:, NG:NG + NE], t["b_fine"].broadcast_to([P, NE])).then_inc(wr_loaded, 16)

            act.wait_ge(s5_loaded, 16 * 7)
            nc.scalar.activation(r5[0:NJ, 2, 2:4], r5[0:NJ, 2, 0:2], ACT.Exp).then_inc(s5_exp, 1)
            act.wait_ge(s5_exp_in, 1)
            nc.scalar.activation(r5[0:NJ, 3, :], r5[0:NJ, 10, :], ACT.Exp).then_inc(s5_exp, 1)
            act.wait_ge(lb_in, 1)
            nc.scalar.activation(lb_tmp[:, 0:2, :], lb_tmp[:, 0:2, :], ACT.Exp).then_inc(lb_exp, 1)
            act.wait_ge(s5_sin_in, 1)
            nc.scalar.activation(r5[0:NJ, 6, :], r5[0:NJ, 4, :], ACT.Sin).then_inc(s5_sin, 1)
            nc.scalar.activation(r5[0:NJ, 7, :], r5[0:NJ, 5, :], ACT.Sin).then_inc(s5_sin, 1)
            def evac(n, b):
                part, m = STEPS[n]
                unit = 2 * n + b
                act.wait_ge(proj_done, unit + 1)
                bank, i = PB[unit % PROJ_BANKS], 2 * m + b
                if part == "u":
                    ins = nc.scalar.activation(uT[:, i, :], bank[:, 0:T], ACT.Copy)
                elif part == "f":
                    ins = nc.scalar.activation(GT[:, i, :], bank[:, 0:T], ACT.Sigmoid)
                elif part == "q":
                    ins = nc.scalar.activation(qT[:, i, :], bank[:, 0:T], ACT.Copy, scale=float(P) ** -0.5)
                elif b == 0:
                    ins = nc.scalar.activation(v_tok[:, 0:2, m * CB:(m + 1) * CB],
                                               bank[:, 0:2 * CB].rearrange("p (a n) -> p a n", a=2), ACT.Copy)
                else:
                    if m:
                        act.wait_ge(v_summed, m)
                    for a in range(4):
                        ins = nc.scalar.activation(v_part[0:TT[2], a, :], bank[32 * a:32 * a + TT[2], 0:CB], ACT.Copy)
                ins.then_inc(proj_read, 1)

            def keep_last(j):
                act.wait_ge(h_ready, j + 1)
                nc.scalar.activation(fin[:, :, :, j], Hst[j % NHST][:, :, TP - 1:T], ACT.Copy).then_inc(fin_copied, 1)

            for n in range(NW):
                if n == PARAMETERS_AT[0][0]:
                    for z, ang in ((1, ang_sin), (0, ang_cos)):
                        act.wait_ge(ang_ready, 2 - z)
                        nc.scalar.activation(turn_table[:, z], ang, ACT.Sin, scale=6.283185).then_inc(table_ready, 1)
                if STEPS[n] == ("f", 0):
                    act.wait_ge(xt_done, 12)
                if STEPS[n] == ("v", 0):
                    act.wait_ge(mat_copied, 8)
                for b in range(2):
                    evac(n, b)
                    for j in half_tiles(n, b):
                        if j >= 1:
                            keep_last(j - 1)
                if n == LN_STEP:
                    act.wait_ge(k_ready, NH)
                    nc.scalar.activation(GT, GT, ACT.Ln).then_inc(lnf_done, 1)
            keep_last(NJ - 1)
            act.wait_ge(y5_ready, N5)
            nc.scalar.activation(uT, uT, ACT.Gelu_apprx_tanh).then_inc(gelu_done, 1)

            def keep_g(i):
                act.wait_ge(g_done, i + 1)
                nc.scalar.activation(gT[:, i, :], PB[2][:, 0:T], ACT.Copy).then_inc(g_read, 1)

            def exponents(h):
                b = h % 2
                act.wait_ge(G_ready, h + 1)
                act.wait_ge(diff_ready, h + 1)
                nc.scalar.activation(QK[b], QK[b], ACT.Exp)
                if h >= 2:
                    act.wait_ge(o_done, h - 1)
                    act.wait_ge(st_ready, 3 * (h - 1))
                nc.scalar.activation(qG[b], GT[:, h, 0:TP], ACT.Exp)
                nc.scalar.activation(chunk_decay[b][:, :], GT[:, h, 2 * P - 1:TP:LAST], ACT.Exp)
                for c0, n in CHUNKS:
                    ins = nc.scalar.activation(kG[b][:, c0:c0 + n], GT[:, h, c0:c0 + n], ACT.Exp,
                                               bias=GT[:, h, c0 + n - 1:c0 + n], scale=-1.0)
                ins.then_inc(exp_ready, 1)

            keep_g(0)
            act.wait_ge(fin_copied, NJ)
            exponents(0)
            for h in range(NH):
                b = h % 2
                act.wait_ge(glu_done, h + 1)
                nc.scalar.activation(sgT[:, h, :], PB[2][:, 0:T], ACT.Sigmoid,
                                     bias=vecs[:, V_BGLU + h:V_BGLU + h + 1]).then_inc(glu_read, 1)
                act.wait_ge(kgt_done, h + 1)
                nc.scalar.activation(kGt[b][:, 0:2, :], PB[7][:, 0:2 * P].rearrange("p (a n) -> p a n", a=2), ACT.Copy)
                nc.scalar.activation(kGt[b][0:LAST, 2, :], PB[7][0:LAST, 2 * P:3 * P], ACT.Copy).then_inc(kgt_copied, 1)
                if h + 1 < NH:
                    exponents(h + 1)
                    keep_g(h + 1)
                else:
                    act.wait_ge(g_read, NH)
                    nc.scalar.activation(gT, gT, ACT.Silu).then_inc(silu_done, 1)
                    for i in range(N5):
                        act.wait_ge(y5g_ready, i + 1)
                        nc.scalar.activation(sgT[:, i, :], uT[:, i, :], ACT.Square).then_inc(sq_ready, 1)
                    act.wait_ge(ss_done, 1)
                    nc.scalar.activation(rms5, PB[2][:, 0:T], ACT.Sqrt, bias=eps_col[:, :], scale=1.0 / W5).then_inc(rt_ready, 1)
                act.wait_ge(o_done, h + 1)
                nc.scalar.activation(kT[:, h, 0:TP], PB[6][:, 0:TP], ACT.Copy)
                nc.scalar.activation(qT[:, h, 0:TP], PB[6][:, 0:TP], ACT.Square).then_inc(o_copied, 1)
            act.wait_ge(samp_copied, 4)
            nc.scalar.activation(qT[:, :, TP:T], kT[:, :, TP:T], ACT.Square).then_inc(sq_ready, 1)
            for at, bank, n, count in ((0, PB[7], TP, 2), (TP, PB[3], NS, 3)):
                act.wait_ge(ss_done, count)
                nc.scalar.activation(GT[0:NH, 0, at:at + n], bank[0:NH, 0:n], ACT.Sqrt, bias=eps_col[0:NH, :],
                                     scale=1.0 / P).then_inc(rt_ready, 1)
            for z in range(2):
                act.wait_ge(fin_t, z + 1)
                nc.scalar.activation(fin_rows[0:3 * NJ, z, :, :], PB[z][0:3 * NJ, 0:3 * P].rearrange("p (a n) -> p a n", a=3),
                                     ACT.Copy).then_inc(fin_read, 1)
            act.wait_ge(fin_read, 2)
            for z, (pn, sn) in enumerate((("s5_re_prompt", "s5_re_sample"), ("s5_im_prompt", "s5_im_sample"))):
                act.dma_start(t[pn][0, 0].rearrange("(j g) p -> j (g p)", g=2), fin_rows[0:NJ, z, 0, :]).then_inc(fin_stored, 16)
                rows = t[sn][0].rearrange("b (j g) p -> (b j) (g p)", g=2)
                act.dma_start(rows[0:2 * NJ], fin_rows[NJ:3 * NJ, z, 0, :]).then_inc(fin_stored, 16)
                act.dma_start(rows[2 * NJ:5 * NJ], fin_rows[0:3 * NJ, z, 1, :]).then_inc(fin_stored, 16)
                act.dma_start(rows[5 * NJ:8 * NJ], fin_rows[0:3 * NJ, z, 2, :]).then_inc(fin_stored, 16)
            act.wait_ge(S0_stored[2], 16 * len(range(2, NS, 3)))
            for o in range(NO):
                step.settle()
                for tile in range(3):
                    n = TT[tile]
                    act.wait_ge(x1_ready, 2 * o + 1 + tile // 2)
                    ins = nc.scalar.activation(yout[0][0:n, tile * CB:(tile + 1) * CB], x1[0:n, tile, o * CB:(o + 1) * CB], ACT.Square,
                                               accum_out=square_sums[0:n, tile, o:o + 1])
                    if o == NO - 1 and tile == 2:
                        ins.then_inc(squares_ready, 1)
                    else:
                        step.add(ins)
            act.wait_ge(r_sum, 1)
            nc.scalar.activation(token_stats[:, 0:3], token_stats[:, 0:3], ACT.Sqrt, bias=eps_col[:, :], scale=1.0 / D) \
                .then_inc(r_rms, 1)
            act.wait_ge(sm_in, 1)
            nc.scalar.activation(e8, e8, ACT.Exp).then_inc(sm_exp, 1)
            act.wait_ge(sm_in, 2)
            nc.scalar.activation(dv, dv, ACT.Exp).then_inc(sm_exp, 1)
            nc.scalar.activation(chunk_decay[0][:, :], chunk_decay[0][:, :], ACT.Copy).then_inc(rows_ready, 1)

            def round_act(R):
                with act.Fori(0, NE // 2) as i:
                    for b in range(2):
                        x = i * 2 + (R * NE + b)
                        act.wait_ge(gate_up_done, x * 2 + 2)
                        act.wait_ge(h_made, x + 1)
                        nc.scalar.activation(sg[0:CAP, :], PB[b][0:CAP, :], ACT.Silu, scale=rcol[b][:, 0:1])
                        nc.scalar.activation(up[0:CAP, :], PB[b][CAP:P, :], ACT.Copy).then_inc(act_ready, 1)
                        act.wait_ge(down_done, x * 2 + 2)
                        act.wait_ge(rows_free, x + 1)
                        for cc in range(4):
                            ins = nc.scalar.activation(yout[b][0:CAP, cc * 512:(cc + 1) * 512],
                                                       PB[2 + cc // 2][(cc % 2) * CAP:(cc % 2 + 1) * CAP, :], ACT.Copy)
                        ins.then_inc(rows_ready, 1)

            run_rounds(act, round_act)
            for i, tile in enumerate(TILE_ORDER):
                n = TT[tile]
                act.wait_ge(ysum_done, i + 1)
                act.wait_ge(ysum_pool, i + 1)
                s = token_stats[0:n, tile:tile + 1]
                step.link(nc.scalar.activation(ynorm[0:n, :], x1[0:n, tile, :], ACT.Square, accum_out=s))
                nc.scalar.activation(s, s, ACT.Sqrt, bias=eps_col[0:n, :], scale=1.0 / D).then_inc(f_rms, 1)

        @block.gpsimd
        def _(pool):
            def made(ins):
                ins.then_inc(pool_consts, 1)

            made(pool.memset(ident[:, :], 0.0))
            made(pool.memset(upper[:, :], 0.0))
            pool.wait_ge(pool_consts, 2)
            made(pool.affine_select(out=ident[:, :], in_=ident[:, :], compare_op=ALU.not_equal, fill=1.0, base=0,
                                    pattern=[[-1, P]], channel_multiplier=1))
            made(pool.affine_select(out=upper[:, :], in_=upper[:, :], compare_op=ALU.is_ge, fill=1.0, base=0,
                                    pattern=[[-1, P]], channel_multiplier=1))
            made(pool.iota(iI, pattern=[[1, P]], base=0, channel_multiplier=0))
            made(pool.iota(iJ, pattern=[[0, P]], base=0, channel_multiplier=1))
            made(pool.iota(iota_i[:, 0:64], pattern=[[1, 64]], base=0, channel_multiplier=0))
            made(pool.iota(iota_i[:, 64:81], pattern=[[16, 17]], base=0, channel_multiplier=0))
            made(pool.iota(iota_i[:, 81:84], pattern=[[P, 3]], base=0, channel_multiplier=1))

            step = Chain(pool, pool_step)
            pool.wait_ge(table_ready, 2)
            pool.wait_ge(mat_t, 8)
            for j in range(NJ):
                b = j % 2
                if j >= 2:
                    pool.wait_ge(turn_used, j - 1)
                A = [turn_table[:, z, j, 16:33].unsqueeze(2).broadcast_to([P, 17, 16]) for z in range(2)]
                B = [turn_table[:, z, j, 0:16].unsqueeze(1).broadcast_to([P, 17, 16]) for z in range(2)]

                def out(x, z):
                    return x[:, z].rearrange("p (a b) -> p a b", b=16)

                t1, t2 = turn_tmp
                step.add(pool.tensor_tensor(out(t1, 0), A[0], B[0], ALU.mult))
                step.add(pool.tensor_tensor(out(t1, 1), A[1], B[0], ALU.mult))
                step.add(pool.tensor_tensor(out(t2, 0), A[1], B[1], ALU.mult))
                step.add(pool.tensor_tensor(out(t2, 1), A[0], B[1], ALU.mult))
                step.settle()
                step.add(pool.tensor_tensor(turn[b][:, 0], t1[:, 0], t2[:, 0], ALU.subtract))
                step.add(pool.tensor_tensor(turn[b][:, 1], t1[:, 1], t2[:, 1], ALU.add))
                step.settle()
                pool.engine_nop().then_inc(turn_ready, 1)
            pool.wait_ge(turn_used, NJ)
            for h in range(NH):
                b = h % 2
                if h == 1:
                    pool.wait_ge(h_ready, NJ)
                pool.wait_ge(G_ready, h + 1)
                if h >= 2:
                    pool.wait_ge(att_done, 8 * (h - 1))
                for l, B in enumerate(LV):
                    g = GT[:, h, 0:LW[l]].rearrange("p (n two b) -> p n two b", two=2, b=B)
                    o = QK[b][:, LO[l]:LO[l] + LW[l]].rearrange("p (n two b) -> p n two b", two=2, b=B)
                    mid = g[:, :, 0, B - 1:B].broadcast_to([P, LW[l] // (2 * B), B])
                    pool.tensor_tensor(o[:, :, 0, :], mid, g[:, :, 0, :], ALU.subtract)
                    ins = pool.tensor_tensor(o[:, :, 1, :], g[:, :, 1, :], mid, ALU.subtract)
                ins.then_inc(diff_ready, 1)
                pool.wait_ge(S0_loaded[h % 3], 16 * (h // 3 + 1))
                pool.tensor_tensor(S0[h % 3], S0[h % 3], fs[:, :, h:h + 1].broadcast_to([P, NH, P]), ALU.mult) \
                    .then_inc(S0_decayed, 1)
            pool.engine_nop().then_inc(rows_free, 1)
            pool.engine_nop().then_inc(rows_free, 1)
            pool.wait_ge(x1_stored, 48)
            last_token, last_row = pool.to_reg(T - 1), pool.to_reg(2 * T - 1)

            def gather(g, p):
                pool.wait_ge(idx_ready, g + 1)
                pool.sem_inc(wait_carried, 1)
                pool.indirect_dma_start(out=xg[p][0:CAP, :], out_offset=None, in_=x1_dram,
                                        in_offset=bass.IndirectOffsetOnAxis(ap=idx_tok[p][:, 0:1], axis=0),
                                        bounds_check=last_token, oob_is_err=False).then_inc(gathered[p], 16)

            def round_rows(R):
                if not is_first(R):
                    pool.wait_ge(tr_done, R * (NE + 1) + 1)
                gather(R * (NE + 1), 0)
                with pool.Fori(0, NE // 2) as i:
                    for b in range(2):
                        x = i * 2 + (R * NE + b)
                        g = i * 2 + (R * (NE + 1) + b + 1)
                        pool.wait_ge(tr_done, g)
                        gather(g, 1 - b)
                        pool.wait_ge(rows_ready, x + 2)
                        pool.sem_inc(wait_carried, 1)
                        pool.indirect_dma_start(out=y_dram, out_offset=bass.IndirectOffsetOnAxis(ap=idx_dst[b][:, 0:1], axis=0),
                                                in_=yout[b][0:CAP, :], in_offset=None, bounds_check=last_row,
                                                oob_is_err=False).then_inc(scattered[b], 16)
                        pool.wait_ge(scattered[b], i * 16 + (R * (NE // 2) + 1) * 16)
                        pool.sem_inc(rows_free, 1)

            run_rounds(pool, round_rows)
            pool.engine_nop().then_inc(moe_done, 1)
            cols = slice(V_COLS, D)

            def add_rows(tile):
                n = TT[tile]
                pool.wait_ge(yrow_loaded[tile], 32)
                xt = x1[0:n, tile, cols]
                step.link(pool.tensor_tensor(xt, xt, yrow[2 * tile][0:n, cols], ALU.add))
                pool.tensor_tensor(xt, xt, yrow[2 * tile + 1][0:n, cols], ALU.add).then_inc(ysum_pool, 1)

            def norm_rows(i, tile):
                n = TT[tile]
                pool.wait_ge(rstd_last, i + 1)
                xt = x1[0:n, tile, cols]
                step.link(pool.tensor_tensor(xt, xt, gfin[0:n, cols], ALU.mult))
                pool.tensor_tensor(xt, xt, token_stats[0:n, 3 + tile:4 + tile].broadcast_to([n, D - V_COLS]), ALU.mult) \
                    .then_inc(out_ready_pool, 1)

            pool.wait_ge(gfin_loaded, 16)
            add_rows(TILE_ORDER[0])
            add_rows(TILE_ORDER[1])
            norm_rows(0, TILE_ORDER[0])
            add_rows(TILE_ORDER[2])
            norm_rows(1, TILE_ORDER[1])
            norm_rows(2, TILE_ORDER[2])

        @block.tensor
        def _(pe):
            pe.wait_ge(pool_consts, 4)
            pe.wait_ge(vec_loaded, 16 * 7)
            pe.transpose(PB[7][:, 0:80], vrow[0:80, :], ident[0:80, 0:80]).then_inc(vec_t, 1)

            for i, tile in enumerate(TILE_ORDER):
                n = TT[tile]
                pe.wait_ge(xn_made, i + 1)
                for q in range(KD // 4):
                    unit = i * (KD // 4) + q
                    if unit >= 4:
                        pe.wait_ge(xt_copied, unit - 3)
                    for a in range(4):
                        k = 4 * q + a
                        ins = pe.transpose(PB[unit % 4][:, a * P:a * P + n], xraw[0:n, tile, k * P:(k + 1) * P], ident[0:n, 0:n])
                    ins.then_inc(xt_done, 1)

            def last_tile(bank, lhs, w):
                for k in range(KD):
                    at = 32 * (k % 4)
                    ins = pe.matmul(bank[at:at + TT[2], 0:CB], lhs[k][:, 2 * P:T], w[:, k, :], start=(k < 4), stop=(k >= KD - 4),
                                    tile_position=(0, at))
                return ins

            def project(n, eighth_work):
                part, _ = STEPS[n]
                s = n % PRE_SLOTS
                w = slot(s, KD)
                pe.wait_ge(slot_loaded[s], 16 * (n // PRE_SLOTS + 1))
                if n == 0:
                    pe.wait_ge(xt_copied, 12)
                for b in range(2):
                    unit = 2 * n + b
                    if unit >= PROJ_BANKS:
                        pe.wait_ge(proj_read, unit - PROJ_BANKS + 1)
                    bank = PB[unit % PROJ_BANKS]
                    if part == "v" and b == 0:
                        for tile in range(2):
                            for k in range(KD):
                                if k % 4 == 0:
                                    eighth_work(tile * 4 + k // 4)
                                ins = pe.matmul(bank[:, tile * CB:(tile + 1) * CB], xnT[:, k, tile * P:(tile + 1) * P],
                                                w[:, k, :], start=(k == 0), stop=(k == KD - 1))
                    elif part == "v":
                        ins = last_tile(bank, [xnT[:, k] for k in range(KD)], w)
                    else:
                        for k in range(KD):
                            if k % 4 == 0:
                                eighth_work(b * 4 + k // 4)
                            ins = pe.matmul(bank[:, 0:T], w[:, k, b * P:(b + 1) * P], xnT[:, k, :],
                                            start=(k == 0), stop=(k == KD - 1))
                    ins.then_inc(proj_done, 1)

            def bu_pair(j):
                i = j // 4
                if j % 4 == 0:
                    pe.wait_ge(proj_read, i + 1)
                if j >= 2:
                    pe.wait_ge(bu_read, j)
                else:
                    pe.wait_ge(mat_copied, 8)
                for z in range(2):
                    for jj in (j, j + 1):
                        rows = slice(32 * (jj % 4), 32 * (jj % 4) + 32)
                        ins = pe.matmul(PB[BU_BANKS[jj % 2][z]][:, 0:T], BT[z][rows, i, :], uT[rows, i, :], start=True, stop=True)
                        if z == 1:
                            ins.then_inc(bu_done, 1)

            def y_of(i):
                pe.wait_ge(h_ready, 4 * i + 4)
                if i >= 1:
                    pe.wait_ge(y5_ready, i)
                for z in range(2):
                    for a in range(4):
                        ins = pe.matmul(PB[6][32 * a:32 * a + 32, 0:T], CT[z][:, i, 32 * a:32 * a + 32], Hst[(4 * i + a) % NHST][:, z, :],
                                        start=(z == 0), stop=(z == 1), tile_position=(0, 32 * a))
                ins.then_inc(h_used, 1)

            def parameters(n):
                if n == 0:
                    pe.wait_ge(s5r_ready, 1)
                    pe.wait_ge(vec_copied, 1)
                    for q, row in enumerate((3, 5, 8, 9, 6, 7)):
                        ins = pe.transpose(PB[7][:, P + q * NJ:P + (q + 1) * NJ], r5[0:NJ, row, :], ident[0:NJ, 0:NJ])
                    ins.then_inc(par_t, 1)
                    for z in range(2):
                        for half in range(2):
                            at = z * 2 * P + half * P
                            ins = pe.transpose(PB[6][:, at:at + P], h0row[:, z, half, :], ident[:, :])
                    ins.then_inc(par_t, 1)
                else:
                    pe.wait_ge(mat_ready, n)
                    pe.wait_ge(par_copied, 2)
                    for z in range(2):
                        for q in range(2):
                            bank = PB[4 + 2 * z + q]
                            if n == 2:
                                pe.wait_ge(mat_copied, 2 * z + q + 1)
                            for a in range(4):
                                i = 4 * q + a
                                src = BP[z][:, i, :] if n == 1 else CP[z][:, i].rearrange("p a b -> p (a b)")
                                ins = pe.transpose(bank[:, a * P:(a + 1) * P], src, ident[:, :])
                            ins.then_inc(mat_t, 1)

            for n in range(NW):
                def between(q):
                    if (n, q) in PARAMETERS_AT:
                        parameters(PARAMETERS_AT.index((n, q)))
                    if (n, q) in S5_TILES:
                        j = S5_TILES[n, q]
                        if j % 2 == 0:
                            bu_pair(j)
                        if j % 4 == 1 and j > 1:
                            y_of(j // 4 - 1)

                project(n, between)
            def project_g(i, ks):
                n = G_BLOCK[i // 2]
                s = n % PRE_SLOTS
                if ks[0] == 0:
                    pe.wait_ge(slot_loaded[s], 16 * (n // PRE_SLOTS + 1))
                    if i >= 1:
                        pe.wait_ge(glu_read, i)
                for k in ks:
                    ins = pe.matmul(PB[2][:, 0:T], slot(s, KD)[:, k, (i % 2) * P:(i % 2 + 1) * P], xnT[:, k, :],
                                    start=(k == 0), stop=(k == KD - 1))
                if ks[-1] == KD - 1:
                    ins.then_inc(g_done, 1)

            def sum_y5(i):
                pe.wait_ge(sq_ready, i + 1)
                ins = pe.matmul(PB[2][:, 0:T], ones[:, :], sgT[:, i, :], start=(i == 0), stop=(i == N5 - 1))
                if i == N5 - 1:
                    ins.then_inc(ss_done, 1)

            def sum_head(h):
                pe.wait_ge(o_copied, h + 1)
                pe.wait_ge(kgt_copied, NH)
                ins = pe.matmul(PB[7][0:NH, 0:TP], one_of_eight[:, NH - 1 - h:2 * NH - 1 - h], qT[:, h, 0:TP],
                                start=(h == 0), stop=(h == NH - 1))
                if h == NH - 1:
                    ins.then_inc(ss_done, 1)

            pe.wait_ge(proj_read, 2 * NW - 2)
            project_g(0, range(4))
            y_of(N5 - 1)
            project_g(0, range(4, KD))
            pe.wait_ge(proj_read, 2 * NW)
            pe.wait_ge(y5_ready, N5)
            pe.wait_ge(v_summed, NB)
            for h in range(NH):
                b = h % 2
                cols = slice(h * P, (h + 1) * P)
                pe.wait_ge(gelu_done, 1)
                pe.wait_ge(g_read, h + 1)
                n = GLU_BLOCK[h // 4]
                s = n % PRE_SLOTS
                pe.wait_ge(slot_loaded[s], 16 * (n // PRE_SLOTS + 1))
                for k in range(N5):
                    ins = pe.matmul(PB[2][:, 0:T], slot(s, N5)[:, k, (h % 4) * P:(h % 4 + 1) * P], uT[:, k, :],
                                    start=(k == 0), stop=(k == N5 - 1))
                ins.then_inc(glu_done, 1)
                pe.wait_ge(qk_ready, h + 1)
                if h >= 1:
                    pe.wait_ge(kgt_copied, h)
                for q, (c0, n_) in enumerate(CHUNKS):
                    ins = pe.transpose(PB[7][0:n_, q * P:(q + 1) * P], kG[b][:, c0:c0 + n_], ident[:, :])
                ins.then_inc(kgt_done, 1)
                for l in range(8):
                    u = 8 * h + l
                    if u >= 2:
                        pe.wait_ge(att_read, u - 1)
                    bank = PB[4 + l % 2]
                    for c0, n_ in (CHUNKS if l >= 3 else CHUNKS[:2]):
                        if l < 7:
                            k_ = q_ = QK[b][:, LO[l] + c0:LO[l] + c0 + n_]
                        else:
                            k_, q_ = kT[:, h, c0:c0 + n_], qT[:, h, c0:c0 + n_]
                        ins = pe.matmul(bank[0:n_, c0:c0 + n_], k_, q_, start=True, stop=True)
                    ins.then_inc(att_done, 1)
                    if h + 1 < NH:
                        project_g(h + 1, (2 * l, 2 * l + 1))
                    else:
                        if l >= 1:
                            sum_y5(l - 1)
                        if l < NH - 1:
                            sum_head(l)
                if h == NH - 1:
                    sum_y5(N5 - 1)
                pe.wait_ge(kgt_copied, h + 1)
                if h >= 1:
                    pe.wait_ge(st_ready, 3 * h)
                for q, (c0, n_) in enumerate(CHUNKS):
                    ins = pe.matmul(PB[3][:, q * P:(q + 1) * P], kGt[b][0:n_, q, :], v_tok[0:n_, q, cols], start=True, stop=True)
                ins.then_inc(st_done, 1)
                pe.wait_ge(att_read, 8 * (h + 1))
                pe.wait_ge(st_ready, 3 * h + 2)
                if h >= 1:
                    pe.wait_ge(o_copied, h)
                for q, (c0, n_) in enumerate(CHUNKS):
                    if q:
                        pe.matmul(PB[6][:, c0:c0 + n_], Sst[b][:, q - 1, :], qG[b][:, c0:c0 + n_], start=True, stop=False)
                    ins = pe.matmul(PB[6][:, c0:c0 + n_], v_tok[0:n_, q, cols], att[b][0:n_, c0:c0 + n_],
                                    start=(q == 0), stop=True)
                ins.then_inc(o_done, 1)
                pe.wait_ge(S1_ready, h + 1)
                pe.wait_ge(banks_clear, 1)
                for half in range(2):
                    for a in range(4):
                        ins = pe.matmul(PB[half][32 * a:32 * a + NS, 0:P], q_own[:, 4 * half + a, h, :],
                                        S0[h % 3][:, 4 * half + a, :], start=(h == 0), stop=(h == NS - 1),
                                        tile_position=(0, 32 * a))
                ins.then_inc(os_done, 1)

            sum_head(NH - 1)
            pe.wait_ge(os_copied, 1)
            pe.wait_ge(o_copied, NH)
            for hd in range(NH):
                half, a = hd // 4, hd % 4
                rows = slice(32 * a, 32 * a + NS)
                at = half * NS if a < 3 else 3 * P + half * NS
                ins = pe.transpose(PB[4 + a][:, at:at + NS], o_rows[rows, half, :], ident[rows, rows])
            ins.then_inc(os_turned, 1)

            for z in range(2):
                flat = fin[:, z].rearrange("p a b -> p (a b)")
                for a in range(3):
                    ins = pe.transpose(PB[z][0:3 * NJ, a * P:(a + 1) * P], flat[:, a * 3 * NJ:(a + 1) * 3 * NJ], ident[:, :])
                ins.then_inc(fin_t, 1)
            pe.wait_ge(sq_ready, N5 + 1)
            pe.wait_ge(st_ready, 3 * NH)
            for h in range(NH):
                ins = pe.matmul(PB[3][0:NH, 0:NS], one_of_eight[:, NH - 1 - h:2 * NH - 1 - h], qT[:, h, TP:T],
                                start=(h == 0), stop=(h == NH - 1))
            ins.then_inc(ss_done, 1)
            pe.wait_ge(rstd_ready, 1)
            for h in range(NH):
                if h >= 4:
                    pe.wait_ge(spread_read, h - 3)
                pe.matmul(PB[4 + h % 4][:, 0:T], ident[0:NH, h:h + 1].broadcast_to([NH, P]), GT[0:NH, 0, :],
                          start=True, stop=True).then_inc(spread_done, 1)

            yT = [uT[:, k] for k in range(N5)] + [gT[:, k] for k in range(NH)]
            pe.wait_ge(yT_ready, 1)
            pe.wait_ge(fin_read, 2)

            def turn_block(o):
                pe.wait_ge(x1_ready, 2 * o + 2)
                for kk in range(2):
                    k = 2 * o + kk
                    if k >= 2:
                        pe.wait_ge(xt2_copied, k - 1)
                    for tile in range(3):
                        n = TT[tile]
                        ins = pe.transpose(PB[4 + kk][:, tile * P:tile * P + n], x1[0:n, tile, k * P:(k + 1) * P], ident[0:n, 0:n])
                    ins.then_inc(xt2_done, 1)

            def logits_of(o):
                for kk in range(2):
                    k = 2 * o + kk
                    pe.wait_ge(xt2_copied, k + 1)
                    if k == 0:
                        pe.wait_ge(wr_loaded, 64)
                    ins = pe.matmul(PB[6][64 * kk:64 * kk + NG + NE, 0:T], wr[:, k, :], xn2T[:, k, :], start=(k < 2), stop=(k >= KD - 2),
                                    tile_position=(0, 64 * kk))
                if o == NO - 1:
                    ins.then_inc(part_logits, 1)

            for o in range(NO):
                n = OUT_AT + o
                s = n % PRE_SLOTS
                pe.wait_ge(slot_loaded[s], 16 * (n // PRE_SLOTS + 1))
                for b in range(2):
                    unit = 2 * o + b
                    if b == 1 and o >= 2:
                        logits_of(o - 2)
                    if b == 1 and o >= 1:
                        turn_block(o - 1)
                    if unit >= 4:
                        pe.wait_ge(x1_ready, unit - 3)
                    if b == 0:
                        for tile in range(2):
                            for k in range(KD):
                                if unit == tile == 0 and k == N5:
                                    pe.wait_ge(yT_ready, 2)
                                ins = pe.matmul(PB[unit % 4][:, tile * CB:(tile + 1) * CB], yT[k][:, tile * P:(tile + 1) * P],
                                                slot(s, KD)[:, k, :], start=(k == 0), stop=(k == KD - 1))
                    else:
                        ins = last_tile(PB[unit % 4], yT, slot(s, KD))
                    ins.then_inc(out_done, 1)

            logits_of(NO - 2)
            turn_block(NO - 1)
            logits_of(NO - 1)
            pe.wait_ge(logitsT_ready, 1)
            for tile in range(3):
                n, at = TT[tile], tile * (NG + NE)
                ins = pe.transpose(PB[7][0:n, at:at + NG + NE], lgT[0:NG + NE, tile * P:tile * P + n], ident[0:NG + NE, 0:NG + NE])
            ins.then_inc(logit_done, 1)
            pe.wait_ge(route_ready, 1)
            for q in range(4):
                for tile in range(min(q + 1, 3)):
                    last = tile == min(q, 2)
                    ins = pe.matmul(PB[7][:, q * NE:(q + 1) * NE], (upper if tile == q else ones)[:, :], Mr[:, tile, :],
                                    start=(tile == 0), stop=last)
            ins.then_inc(rank_done, 1)
            pe.nop().then_inc(tr_done, 1)

            def list_of(g, e):
                pe.wait_ge(oh_ready, g + 1)
                for tile in range(3):
                    ins = pe.matmul(PB[7][0:CAP, 0:4], oh[:, tile, :], PL[:, tile, bass.ds(e, 1), :].rearrange("p a b -> p (a b)"),
                                    start=(tile == 0), stop=(tile == 2))
                ins.then_inc(list_done, 1)

            def turn_64(out, rows, waits):
                eye = ident[0:CAP, 0:CAP]
                return pe.matmul(out, rows, eye, start=True, stop=True) if waits else pe.transpose(out, rows, eye)

            def transpose_rows(p):
                for k in range(KD):
                    ins = turn_64(PB[4 + k // 8][:, (k % 8) * CAP:(k % 8 + 1) * CAP], xg[p][0:CAP, k * P:(k + 1) * P], k == 0)
                ins.then_inc(tr_done, 1)

            def round_pe(R):
                if is_first(R):
                    pe.wait_ge(lists_ready, 1)
                else:
                    pe.wait_ge(dst_ready, R * (NE + 1))
                    pe.wait_ge(xgT_ready, R * (NE + 1))
                list_of(R * (NE + 1), 0)
                pe.wait_ge(gathered[0], R * (16 * 17) + 16)
                transpose_rows(0)
                with pe.Fori(0, NE // 2) as i:
                    for b in range(2):
                        x = i * 2 + (R * NE + b)
                        g = i * 2 + (R * (NE + 1) + b + 1)
                        pe.wait_ge(dst_ready, g)
                        list_of(g, i * 2 + (b + 1))
                        pe.wait_ge(xgT_ready, g)
                        for half in range(2):
                            sg_, su_ = MOE_SLOT[2 * half], MOE_SLOT[2 * half + 1]
                            pe.wait_ge(slot_loaded[sg_], x * 16 + 16 * (FILLS[sg_] + 1))
                            pe.wait_ge(slot_loaded[su_], x * 16 + 16 * (FILLS[su_] + 1))
                            for k in range(KD // 2):
                                kk = half * (KD // 2) + k
                                for at, s in ((0, sg_), (CAP, su_)):
                                    ins = pe.matmul(PB[b][at:at + CAP, :], xgT[b][:, kk, :], slot(s, KD // 2)[:, k, :],
                                                    start=(kk == 0), stop=(kk == KD - 1))
                            ins.then_inc(gate_up_done, 1)
                        if b == 0:
                            pe.wait_ge(gathered[1], i * 16 + (R * 16 + 1) * 16)
                        else:
                            pe.wait_ge(gathered[0], i * 16 + (R * 17 + 2) * 16)
                        transpose_rows(1 - b)
                        pe.wait_ge(h_made, x + 2)
                        for f in range(KF):
                            ins = turn_64(PB[6][:, f * CAP:(f + 1) * CAP], hh[0:CAP, f * P:(f + 1) * P], f == 0)
                        ins.then_inc(hT_done, 1)
                        pe.wait_ge(hT_ready, x + 1)
                        pe.wait_ge(rows_ready, x + 1)
                        for half in range(2):
                            pe.wait_ge(slot_loaded[4 + half], x * 16 + 16)
                            for k in range(KF // 2):
                                f = half * (KF // 2) + k
                                for cc in range(4):
                                    at = (cc % 2) * CAP
                                    ins = pe.matmul(PB[2 + cc // 2][at:at + CAP, :], hT[:, f, :],
                                                    slot(4 + half, KF // 2)[:, k, cc * 512:(cc + 1) * 512],
                                                    start=(f == 0), stop=(f == KF - 1))
                            ins.then_inc(down_done, 1)

            run_rounds(pe, round_pe)

        @block.vector
        def _(dve):
            step = Chain(dve, dve_step)
            TS, TTo, STT = nc.vector.tensor_scalar, nc.vector.tensor_tensor, nc.vector.scalar_tensor_tensor
            nc.vector.memset(ones[:, :], 1.0)
            nc.vector.memset(one_of_eight[:, :], 0.0)
            nc.vector.memset(square_sums[:, :, :], 0.0)
            nc.vector.memset(eps_col[:, :], EPS).then_inc(dve_consts, 1)

            for i, tile in enumerate(TILE_ORDER):
                n = TT[tile]
                dve.wait_ge(x_rms, i + 1)
                r = token_stats[0:n, 3 + tile:4 + tile]
                step.link(nc.vector.reciprocal(r, token_stats[0:n, tile:tile + 1]))
                TS(xraw[0:n, tile, :], xraw[0:n, tile, :], r, None, ALU.mult).then_inc(xn_made, 1)
            dve.wait_ge(vec_t, 1)
            nc.vector.tensor_copy(vecs[:, :], PB[7][:, 0:80]).then_inc(vec_copied, 1)
            dve.wait_ge(vec_copied, 1)

            for i, tile in enumerate(TILE_ORDER):
                n = TT[tile]
                for q in range(KD // 4):
                    unit = i * (KD // 4) + q
                    dve.wait_ge(xt_done, unit + 1)
                    TTo(xnT[:, 4 * q:4 * q + 4, tile * P:tile * P + n],
                        PB[unit % 4][:, :].rearrange("p (a n) -> p a n", a=4)[:, :, 0:n],
                        vecs[:, V_MIX + 4 * q:V_MIX + 4 * q + 4].unsqueeze(2).broadcast_to([P, 4, n]), ALU.mult) \
                        .then_inc(xt_copied, 1)

            nc.vector.memset(one_of_eight[:, NH - 1:NH], 1.0)
            step.link(TTo(lb_tmp[:, 2, :], vecs[:, V_LB0:V_LB0 + 8], vecs[:, V_LB1:V_LB1 + 8], ALU.max))
            TTo(lb_tmp[:, 0, :], vecs[:, V_LB0:V_LB0 + 8], lb_tmp[:, 2, :], ALU.subtract)
            TTo(lb_tmp[:, 1, :], vecs[:, V_LB1:V_LB1 + 8], lb_tmp[:, 2, :], ALU.subtract).then_inc(lb_in, 1)

            R = [r5[0:NJ, q, :] for q in range(12)]
            two = [r.rearrange("p (a b) -> p a b", a=2) for r in R]
            stepc = R[2][:, 2:4].unsqueeze(2).broadcast_to([NJ, 2, P5])
            dve.wait_ge(s5_loaded, 16 * 7)
            dve.wait_ge(s5_exp, 1)
            TTo(two[10], two[0], stepc, ALU.mult).then_inc(s5_exp_in, 1)
            step.link(TTo(two[11], two[1], stepc, ALU.mult))
            step.link(TS(R[4], R[11], 1 / (2 * math.pi), MAGIC, ALU.mult, ALU.add))
            step.link(TS(R[4], R[4], MAGIC, None, ALU.subtract))
            step.link(STT(R[11], R[4], -TWO_PI_HI, R[11], ALU.mult, ALU.add))
            step.link(STT(R[4], R[4], -TWO_PI_LO, R[11], ALU.mult, ALU.add))
            step.link(TS(R[4], R[4], PI_BELOW, -PI_BELOW, ALU.min, ALU.max))
            step.link(TS(R[5], R[4], math.pi / 2, None, ALU.add))
            step.link(TS(R[11], R[5], PI_BELOW, -2 * math.pi, ALU.is_gt, ALU.mult))
            step.link(TTo(R[5], R[5], R[11], ALU.add))
            TS(R[5], R[5], PI_BELOW, -PI_BELOW, ALU.min, ALU.max).then_inc(s5_sin_in, 1)
            dve.wait_ge(lb_exp, 1)
            step.link(TTo(lb_tmp[:, 1, :], lb_tmp[:, 0, :], lb_tmp[:, 1, :], ALU.add))
            step.link(nc.vector.reciprocal(lb_tmp[:, 1, :], lb_tmp[:, 1, :]))
            step.link(TTo(lb[:, :], lb_tmp[:, 0, :], lb_tmp[:, 1, :], ALU.mult))
            step.link(TS(one_minus_lb[:, :], lb[:, :], -1.0, 1.0, ALU.mult, ALU.add))
            dve.wait_ge(s5_exp, 2)
            dve.wait_ge(s5_sin, 2)
            step.add(TS(R[5], R[4], 1 / (2 * math.pi), None, ALU.mult))
            step.add(TTo(R[8], R[3], R[7], ALU.mult))
            step.add(TTo(R[9], R[3], R[6], ALU.mult))
            step.add(TTo(R[10], R[0], R[0], ALU.mult))
            step.add(TTo(R[11], R[1], R[1], ALU.mult))
            step.settle()
            step.link(TTo(R[10], R[10], R[11], ALU.add))
            step.add(nc.vector.reciprocal(R[10], R[10]))
            step.link(TS(R[11], R[8], -1.0, None, ALU.add))
            step.add(TTo(R[6], R[11], R[0], ALU.mult))
            step.link(TTo(R[7], R[9], R[1], ALU.mult))
            step.link(TTo(R[6], R[6], R[7], ALU.add))
            step.add(TTo(R[6], R[6], R[10], ALU.mult))
            step.add(TTo(R[7], R[9], R[0], ALU.mult))
            step.link(TTo(R[11], R[11], R[1], ALU.mult))
            step.link(TTo(R[7], R[7], R[11], ALU.subtract))
            TTo(R[7], R[7], R[10], ALU.mult).then_inc(s5r_ready, 1)

            dve.wait_ge(pool_consts, 9)
            nc.vector.tensor_copy(mvals[:, 0:16], iota_i[:, 0:16])
            nc.vector.tensor_copy(mvals[:, 16:33], iota_i[:, 64:81])
            nc.vector.tensor_copy(iota32, iota_i[:, 0:NE])
            nc.vector.tensor_copy(slotid, iota_i[:, 0:CAP])
            nc.vector.tensor_copy(tid, iota_i[:, 81:84])
            step.add(TTo(iX, iI, iJ, ALU.bitwise_xor))
            step.add(TTo(mG, iI, iJ, ALU.is_gt))
            step.add(TTo(masks[:, 7, :], iI, iJ, ALU.is_equal))
            step.link(TS(parity[:, 2:3].bitcast(I32), iJ[:, 0:1], 16, None, ALU.bitwise_and))
            step.link(nc.vector.tensor_copy(mX, iX))
            step.link(STT(mX, mX, 1.0, mG, ALU.add, ALU.mult))
            step.add(TS(mX, mX, -1.0, None, ALU.add))
            step.link(nc.vector.tensor_copy(parity[:, 1:2], parity[:, 2:3].bitcast(I32)))
            step.link(TS(parity[:, 1:2], parity[:, 1:2], 1.0 / 16, None, ALU.mult))
            step.link(TS(parity[:, 0:1], parity[:, 1:2], -1.0, 1.0, ALU.mult, ALU.add))
            for l, B in enumerate(LV):
                step.link(TS(mL, mX, 2.0 * B, None, ALU.is_lt))
                step.link(STT(masks[:, l, :], mX, float(B), mL, ALU.is_ge, ALU.mult))

            dve.wait_ge(bc_loaded, 16 * 4)
            for z in range(2):
                for half in range(2):
                    TS(CP[z][:, :, half, :], Craw[z], parity[:, half:half + 1], 1.0 if z == 0 else -1.0, ALU.mult, ALU.mult)
            for z in range(2):
                step.add(nc.vector.memset(BP[z], 0.0))

            dve.wait_ge(par_t, 2)
            step.link(nc.vector.tensor_copy(sc5[:, :, :], PB[7][:, P:P + 6 * NJ].rearrange("p (a n) -> p a n", a=6)))
            dec = [sc5[:, q, :].unsqueeze(1).broadcast_to([P, NS, NJ]) for q in (2, 3)]
            h0 = [PB[6][:, z * 2 * P:(z + 1) * 2 * P].rearrange("p (a n) -> p a n", a=NS) for z in range(2)]
            step.add(TTo(Zs[:, 0], h0[0], dec[0], ALU.mult))
            step.add(TTo(z_tmp[0], h0[1], dec[1], ALU.mult))
            step.add(TTo(Zs[:, 1], h0[1], dec[0], ALU.mult))
            step.add(TTo(z_tmp[1], h0[0], dec[1], ALU.mult))
            step.link(TTo(ang_r, sc5[:, 1, :].unsqueeze(2).broadcast_to([P, NJ, 33]),
                          mvals.unsqueeze(1).broadcast_to([P, NJ, 33]), ALU.mult))
            nc.vector.tensor_copy(parity[:, 2:3], parity[:, 1:2]).then_inc(par_copied, 2)
            step.add(TTo(Zs[:, 0], Zs[:, 0], z_tmp[0], ALU.subtract))
            step.add(TTo(Zs[:, 1], Zs[:, 1], z_tmp[1], ALU.add))
            step.link(TS(ang_n, ang_r, MAGIC, MAGIC, ALU.add, ALU.subtract))
            step.link(TTo(ang_sin, ang_r, ang_n, ALU.subtract))
            TS(ang_sin, ang_sin, 0.5, -0.5, ALU.min, ALU.max).then_inc(ang_ready, 1)
            step.link(TS(ang_r, ang_r, 0.25, None, ALU.add))
            step.link(TS(ang_n, ang_r, MAGIC, MAGIC, ALU.add, ALU.subtract))
            step.link(TTo(ang_cos, ang_r, ang_n, ALU.subtract))
            TS(ang_cos, ang_cos, 0.5, -0.5, ALU.min, ALU.max).then_inc(ang_ready, 1)
            fr, fi = (sc5[:, q, :].unsqueeze(2).broadcast_to([P, NJ, C5]) for q in (4, 5))
            for z in range(2):
                step.add(TTo(Btmp[0], fr, Braw[z], ALU.mult))
                step.link(TTo(Btmp[1], fi, Braw[1 - z], ALU.mult))
                op = ALU.subtract if z == 0 else ALU.add
                pad = BP[z].rearrange("p i (a g c) -> p (i a) g c", a=4, g=2)
                for g in range(2):
                    rows = slice(64 * g, 64 * g + 64)
                    ins = TTo(pad[rows, :, g, :], Btmp[0][rows], Btmp[1][rows], op)
                    if z == 1 and g == 1:
                        ins.then_inc(mat_ready, 1)
                    else:
                        step.add(ins)
                step.settle()
            nc.vector.tensor_copy(parity[:, 2:3], parity[:, 1:2]).then_inc(mat_ready, 1)
            dve.wait_ge(table_ready, 2)
            for n in range(2):
                for z in range(2):
                    for q in range(2):
                        dve.wait_ge(mat_t, 4 * n + 2 * z + q + 1)
                        nc.vector.tensor_copy((BT, CT)[n][z][:, 4 * q:4 * q + 4, :],
                                              PB[4 + 2 * z + q][:, :].rearrange("p (a n) -> p a n", a=4)).then_inc(mat_copied, 1)

            def make_k(h):
                dve.wait_ge(proj_read, 4 * NB)
                step.link(TS(GT[:, h, :], GT[:, h, :], one_minus_lb[:, h:h + 1], lb[:, h:h + 1], ALU.mult, ALU.add))
                step.add(nc.vector.tensor_copy(fs[:, h, :], GT[:, h, TP:T]))
                TS(kT[:, h, :], GT[:, h, :], -1.0, 1.0, ALU.mult, ALU.add).then_inc(k_ready, 1)

            def sum_ln_f(h):
                dve.wait_ge(lnf_done, 1)
                for c0, n in CHUNKS:
                    ins = nc.vector.tensor_tensor_scan(GT[:, h, c0:c0 + n], ones[:, 0:1].broadcast_to([P, n]),
                                                       GT[:, h, c0:c0 + n], 0.0, ALU.mult, ALU.add)
                ins.then_inc(G_ready, 1)

            def add_v_parts(n):
                m = STEPS[n][1]
                dve.wait_ge(proj_read, 2 * n + 2)
                v = v_part[0:TT[2]]
                step.link(TTo(v[:, 0:2, :], v[:, 0:2, :], v[:, 2:4, :], ALU.add))
                TTo(v_tok[0:TT[2], 2, m * CB:(m + 1) * CB], v[:, 0, :], v[:, 1, :], ALU.add).then_inc(v_summed, 1)

            for j in range(NJ):
                b = j % 2
                hst = Hst[j % NHST]
                re, im = (PB[q] for q in BU_BANKS[b])
                cos, sin = turn[b][:, 0], turn[b][:, 1]
                dve.wait_ge(bu_done, j + 1)
                dve.wait_ge(turn_ready, j + 1)
                if j >= NHST:
                    dve.wait_ge(h_used, (j - NHST) // 4 + 1)
                    dve.wait_ge(fin_copied, j - NHST + 1)
                if j >= 1:
                    dve.wait_ge(h_ready, j)
                step.add(TTo(M1[:, 0], re[:, 0:TP], cos, ALU.mult))
                step.add(TTo(M1[:, 1], im[:, 0:TP], cos, ALU.mult))
                step.add(TTo(M2[:, 0], im[:, 0:TP], sin, ALU.mult))
                step.add(TTo(M2[:, 1], re[:, 0:TP], sin, ALU.mult))
                step.add(TTo(hst[:, 0, TP:T], re[:, TP:T], Zs[:, 0, :, j], ALU.add))
                TTo(hst[:, 1, TP:T], im[:, TP:T], Zs[:, 1, :, j], ALU.add).then_inc(bu_read, 1)
                step.settle()
                step.add(TTo(Wt[:, 0], M1[:, 0], M2[:, 0], ALU.add))
                step.link(TTo(Wt[:, 1], M1[:, 1], M2[:, 1], ALU.subtract))
                for z in range(2):
                    step.add(nc.vector.tensor_tensor_scan(Gs[:, z], sc5[:, 0, j:j + 1].broadcast_to([P, TP]), Wt[:, z], 0.0,
                                                          ALU.mult, ALU.add))
                step.settle()
                step.add(TTo(M1[:, 0], Gs[:, 0], cos, ALU.mult))
                step.add(TTo(M1[:, 1], Gs[:, 1], cos, ALU.mult))
                step.add(TTo(M2[:, 0], Gs[:, 1], sin, ALU.mult))
                step.add(TTo(M2[:, 1], Gs[:, 0], sin, ALU.mult))
                step.settle()
                TTo(hst[:, 0, 0:TP], M1[:, 0], M2[:, 0], ALU.subtract).then_inc(turn_used, 1)
                TTo(hst[:, 1, 0:TP], M1[:, 1], M2[:, 1], ALU.add).then_inc(h_ready, 1)
                for i in ((j - 5) // 4,) if j % 4 == 1 and j > 1 else (N5 - 1,) if j == NJ - 1 else ():
                    dve.wait_ge(h_used, i + 1)
                    STT(uT[:, i, :], uT[:, i, :], vecs[:, V_D + i:V_D + i + 1], PB[6][:, 0:T], ALU.mult, ALU.add) \
                        .then_inc(y5_ready, 1)
                if F_TILE <= j < F_TILE + NH:
                    make_k(j - F_TILE)
                if j >= G_TILE:
                    sum_ln_f(j - G_TILE)
                n = STEP_OF[j] - 1
                if STEPS[n][0] == "v" and STEP_OF[j - 1] == n:
                    add_v_parts(n)
            add_v_parts(NW - 1)

            dve.wait_ge(proj_read, 2 * NW)
            step.add(nc.vector.memset(PB[0][:, 0:P], 0.0))
            nc.vector.memset(PB[1][:, 0:P], 0.0).then_inc(banks_clear, 1)
            step.add(nc.vector.tensor_copy(ks[:, :, :], kT[:, :, TP:T]))
            dve.wait_ge(y5_ready, N5)
            dve.wait_ge(v_summed, NB)
            step.link(nc.vector.memset(q_own, 0.0))
            for b in range(NS):
                step.add(nc.vector.tensor_copy(q_own[:, :, b, b:b + 1], qT[:, :, TP + b:TP + b + 1]))
            dve.wait_ge(fin_copied, NJ)
            for b in range(2):
                step.add(nc.vector.memset(att[b], 0.0))
            step.settle()
            def gate_o(h):
                dve.wait_ge(o_copied, h + 1)
                step.add(STT(gT[:, h, 0:TP], kT[:, h, 0:TP], vecs[:, V_GH + h:V_GH + h + 1], gT[:, h, 0:TP], ALU.mult, ALU.mult))

            for h in range(NH):
                b = h % 2
                dve.wait_ge(exp_ready, h + 1)
                for l, B in enumerate(LV):
                    o = QK[b][:, LO[l]:LO[l] + LW[l]].rearrange("p (n two b) -> p n two b", two=2, b=B)
                    for side, src in ((0, kT), (1, qT)):
                        s = src[:, h, 0:LW[l]].rearrange("p (n two b) -> p n two b", two=2, b=B)
                        TTo(o[:, :, side, :], o[:, :, side, :], s[:, :, side, :], ALU.mult)
                TTo(qG[b], qG[b], qT[:, h, 0:TP], ALU.mult)
                TTo(kG[b], kG[b], kT[:, h, 0:TP], ALU.mult).then_inc(qk_ready, 1)
                dve.wait_ge(v_spread, 16 * (h + 1))
                step.add(TTo(vk, vk, ks[:, :, h:h + 1].broadcast_to([P, NH, P]), ALU.mult))
                step.settle()
                dve.wait_ge(S0_decayed, h + 1)
                TTo(S0[h % 3], S0[h % 3], vk, ALU.add).then_inc(S1_ready, 1)
                for l in range(8):
                    u = 8 * h + l
                    dve.wait_ge(att_done, u + 1)
                    if u:
                        dve.wait_ge(att_read, u)
                    bank = PB[4 + l % 2]
                    ins = nc.vector.copy_predicated(att[b][:, 0:2 * P].rearrange("p (a n) -> p a n", a=2),
                                                    masks[:, l, :].unsqueeze(1).broadcast_to([P, 2, P]),
                                                    bank[:, 0:2 * P].rearrange("p (a n) -> p a n", a=2))
                    if l >= 3:
                        ins = nc.vector.copy_predicated(att[b][0:LAST, 2 * P:TP], masks[0:LAST, l, 0:LAST],
                                                        bank[0:LAST, 2 * P:TP])
                    ins.then_inc(att_read, 1)
                    if h == NH - 1:
                        dve.wait_ge(glu_read, NH)
                        TTo(uT[:, l, :], uT[:, l, :], sgT[:, l, :], ALU.mult).then_inc(y5g_ready, 1)
                        dve.wait_ge(silu_done, 1)
                        if l < NH - 1:
                            gate_o(l)
                dve.wait_ge(st_done, h + 1)
                if h >= 2:
                    dve.wait_ge(st_stored[b], 16 * (h // 2))
                for q in range(3):
                    part = PB[3][:, q * P:(q + 1) * P]
                    if q == 0:
                        ins = nc.vector.tensor_copy(Sst[b][:, 0, :], part)
                    else:
                        dve.wait_ge(st_ready, 3 * h + q)
                        ins = STT(Sst[b][:, q, :], Sst[b][:, q - 1, :], chunk_decay[b][:, q - 1:q], part, ALU.mult, ALU.add)
                    ins.then_inc(st_ready, 1)

            dve.wait_ge(os_done, NS)
            step.add(nc.vector.tensor_copy(o_rows[:, 0, :], PB[0][:, 0:P]))
            nc.vector.tensor_copy(o_rows[:, 1, :], PB[1][:, 0:P]).then_inc(os_copied, 1)
            gate_o(NH - 1)
            dve.wait_ge(os_turned, 1)
            for a in range(4):
                at = 0 if a < 3 else 3 * P
                nc.vector.tensor_copy(kT[:, a::4, TP:T], PB[4 + a][:, at:at + 2 * NS].rearrange("p (h b) -> p h b", h=2)) \
                    .then_inc(samp_copied, 1)
            step.add(TTo(gT[:, :, TP:T], gT[:, :, TP:T], vecs[:, V_GH:V_GH + NH].unsqueeze(2).broadcast_to([P, NH, NS]), ALU.mult))
            dve.wait_ge(samp_copied, 4)
            step.settle()
            step.add(TTo(gT[:, :, TP:T], gT[:, :, TP:T], kT[:, :, TP:T], ALU.mult))
            dve.wait_ge(rt_ready, 1)
            step.add(nc.vector.reciprocal(rms5, rms5))
            dve.wait_ge(rt_ready, 3)
            nc.vector.reciprocal(GT[0:NH, 0, :], GT[0:NH, 0, :]).then_inc(rstd_ready, 1)
            step.settle()

            def norm_head(h):
                dve.wait_ge(spread_done, h + 1)
                return TTo(gT[:, h, :], gT[:, h, :], PB[4 + h % 4][:, 0:T], ALU.mult)

            for i in range(N5):
                ins = STT(uT[:, i, :], uT[:, i, :], vecs[:, V_G5 + i:V_G5 + i + 1], rms5, ALU.mult, ALU.mult)
            ins.then_inc(yT_ready, 1)
            for h in range(4):
                norm_head(h).then_inc(spread_read, 1)
            for h in range(4, NH):
                ins = norm_head(h)
            ins.then_inc(yT_ready, 1)

            dve.wait_ge(x_again, 16 * 5)
            dve.wait_ge(fin_stored, 16 * 8)

            def copy_block(o):
                for kk in range(2):
                    k = 2 * o + kk
                    dve.wait_ge(xt2_done, k + 1)
                    TS(xn2T[:, k, :], PB[4 + kk][:, 0:T], vecs[:, V_FFN + k:V_FFN + k + 1], None, ALU.mult).then_inc(xt2_copied, 1)

            for o in range(NO):
                for b in range(2):
                    unit = 2 * o + b
                    if b == 1 and o >= 1:
                        copy_block(o - 1)
                    dve.wait_ge(out_done, unit + 1)
                    cols = slice(o * CB, (o + 1) * CB)
                    if b == 0:
                        x_, p_ = x1[:, 0:2, cols], PB[unit % 4][:, 0:2 * CB].rearrange("p (a n) -> p a n", a=2)
                    else:
                        x_ = x1[0:TT[2], 2, cols]
                        for a in range(3):
                            step.link(TTo(x_, x_, PB[unit % 4][32 * a:32 * a + TT[2], 0:CB], ALU.add))
                        p_ = PB[unit % 4][96:96 + TT[2], 0:CB]
                    TTo(x_, x_, p_, ALU.add).then_inc(x1_ready, 1)
            copy_block(NO - 1)
            dve.wait_ge(squares_ready, 1)
            nc.vector.tensor_reduce(token_stats[:, 0:3], square_sums[:, :, :], AX.X, ALU.add).then_inc(r_sum, 1)

            step.add(nc.vector.memset(lg, 0.0))
            step.add(nc.vector.memset(c8, LOWEST))
            NL = NG + NE
            dve.wait_ge(part_logits, 1)
            dve.wait_ge(S0_stored[2], 16 * len(range(2, NS, 3)))
            step.link(nc.vector.tensor_copy(lgT[0:NL, :], PB[6][0:NL, 0:T]))
            TTo(lgT[0:NL, :], lgT[0:NL, :], PB[6][64:64 + NL, 0:T], ALU.add).then_inc(logitsT_ready, 1)
            dve.wait_ge(r_rms, 1)
            rstd = token_stats[:, 3:6]
            step.link(nc.vector.reciprocal(rstd, token_stats[:, 0:3]))
            dve.wait_ge(logit_done, 1)
            for tile in range(3):
                n = TT[tile]
                step.add(STT(lg[0:n, tile, :], PB[7][0:n, tile * NL:(tile + 1) * NL], token_stats[0:n, 3 + tile:4 + tile],
                             bias36[0:n, :], ALU.mult, ALU.add))
            step.settle()
            step.link(nc.vector.tensor_copy(c8[:, :, 0:NG], lg[:, :, 0:NG]))
            for tile in range(3):
                step.add(nc.vector.max(out=gmax[:, tile, :], in_=c8[:, tile, :]))
            step.settle()
            for tile in range(3):
                step.add(nc.vector.max_index(out=gidx[:, tile, :], in_max=gmax[:, tile, :], in_values=c8[:, tile, :]))
            TTo(e8, lg[:, :, 0:NG], gmax[:, :, 0:1].broadcast_to([P, 3, NG]), ALU.subtract).then_inc(sm_in, 1)
            step.settle()
            step.link(nc.vector.tensor_copy(grp, gidx[:, :, 0]))
            step.link(TTo(ohg, iota32[:, 0:NG].unsqueeze(1).broadcast_to([P, 3, NG]),
                          grp.unsqueeze(2).broadcast_to([P, 3, NG]), ALU.is_equal))
            for tile in range(3):
                step.add(TTo(pick[:, tile], lg[:, tile, NG:NL].rearrange("p (g j) -> p g j", g=NG),
                             ohg[:, tile, :].unsqueeze(2).broadcast_to([P, NG, EG]), ALU.mult))
            step.settle()
            for tile in range(3):
                step.add(nc.vector.tensor_reduce(f8[:, tile, :], pick[:, tile].rearrange("p g j -> p j g"), AX.X, ALU.add))
            step.settle()
            for tile in range(3):
                step.add(nc.vector.max(out=fmax[:, tile, :], in_=f8[:, tile, :]))
            step.settle()
            for tile in range(3):
                step.add(nc.vector.max_index(out=fidx[:, tile, :], in_max=fmax[:, tile, :], in_values=f8[:, tile, :]))
            step.settle()
            TTo(dv, fmax[:, :, 1], fmax[:, :, 0], ALU.subtract).then_inc(sm_in, 1)
            step.add(nc.vector.tensor_copy(e0, fidx[:, :, 0]))
            step.link(nc.vector.tensor_copy(e1, fidx[:, :, 1]))
            step.add(STT(e0, grp, float(EG), e0, ALU.mult, ALU.add))
            step.add(STT(e1, grp, float(EG), e1, ALU.mult, ALU.add))
            step.link(TS(valid, tid, float(T), None, ALU.is_lt))
            for o_, e_ in ((OH0, e0), (OH1, e1)):
                step.add(TTo(o_, iota32.unsqueeze(1).broadcast_to([P, 3, NE]), e_.unsqueeze(2).broadcast_to([P, 3, NE]), ALU.is_equal))
            step.settle()
            for o_ in (OH0, OH1):
                step.add(TTo(o_, o_, valid.unsqueeze(2).broadcast_to([P, 3, NE]), ALU.mult))
            step.settle()
            TTo(Mr, OH0, OH1, ALU.add).then_inc(route_ready, 1)
            dve.wait_ge(sm_exp, 2)
            step.add(nc.vector.tensor_reduce(pgi, e8, AX.X, ALU.add))
            step.link(TS(w0, dv, 1.0, None, ALU.add))
            step.link(TTo(w0, w0, pgi, ALU.mult))
            step.link(nc.vector.reciprocal(w0, w0))
            step.link(TTo(w0, w0, rstd, ALU.mult))
            step.link(TTo(w1, w0, dv, ALU.mult))
            step.add(nc.vector.memset(PL, 0.0))
            step.add(nc.vector.memset(rankm, -1.0))
            step.settle()
            tidb = tid.unsqueeze(2).broadcast_to([P, 3, NE])
            step.add(TTo(pick.rearrange("p a g j -> p a (g j)"), OH0, w0.unsqueeze(2).broadcast_to([P, 3, NE]), ALU.mult))
            step.add(TTo(PL[:, :, 0:NE, 2], OH1, w1.unsqueeze(2).broadcast_to([P, 3, NE]), ALU.mult))
            step.add(nc.vector.tensor_copy(PL[:, :, 0:NE, 3], rstd.unsqueeze(2).broadcast_to([P, 3, NE])))
            step.add(TS(PL[:, :, 0:NE, 0], tidb, -BIG, None, ALU.add))
            step.link(STT(PL[:, :, 0:NE, 1], OH1, float(T), tidb, ALU.mult, ALU.add))
            step.add(TTo(PL[:, :, 0:NE, 2], PL[:, :, 0:NE, 2], pick.rearrange("p a g j -> p a (g j)"), ALU.add))
            step.link(TS(PL[:, :, 0:NE, 1], PL[:, :, 0:NE, 1], -BIG, None, ALU.add))
            dve.wait_ge(rank_done, 1)
            step.add(TTo(rankm[:, :, 0:NE], PB[7][:, 0:3 * NE].rearrange("p (a n) -> p a n", a=3), Mr, ALU.mult))
            step.link(nc.vector.tensor_reduce(maxn, PB[7][:, 3 * NE:4 * NE], AX.X, ALU.max))
            step.add(TTo(rankm[:, :, 0:NE], rankm[:, :, 0:NE], Mr, ALU.add))
            for r in range(1, ROUNDS):
                step.add(TS(ext[:, r - 1:r], maxn, float(CAP * r), None, ALU.is_gt))
            step.settle()
            step.add(TS(rankm[:, :, 0:NE], rankm[:, :, 0:NE], -1.0, None, ALU.add))
            step.link(nc.vector.tensor_reduce(maxn, ext, AX.X, ALU.add))
            nc.vector.tensor_copy(extra_i[:, :], maxn).then_inc(lists_ready, 1)
            nc.vector.engine_nop().then_inc(h_made, 1)
            dve.wait_ge(lists_ready, 1)

            def places(e):
                TTo(oh[:, :, :], rankm[:, :, bass.ds(e, 1)].broadcast_to([P, 3, CAP]),
                    slotid.unsqueeze(1).broadcast_to([P, 3, CAP]), ALU.is_equal).then_inc(oh_ready, 1)

            def indices(g, p):
                dve.wait_ge(list_done, g + 1)
                TS(idx_tok[p][:, :], PB[7][0:CAP, 0:1], BIG, None, ALU.add)
                nc.vector.tensor_copy(rcol[p][:, :], PB[7][0:CAP, 3:4])
                nc.vector.tensor_copy(gcol[p][:, :], PB[7][0:CAP, 2:3]).then_inc(idx_ready, 1)

            def destinations(p):
                TS(idx_dst[p][:, :], PB[7][0:CAP, 1:2], BIG, None, ALU.add).then_inc(dst_ready, 1)

            def rows_in(g, p):
                dve.wait_ge(tr_done, g + 2)
                for q in range(2):
                    ins = TTo(xgT[p][:, 8 * q:8 * q + 8, :], PB[4 + q][:, :].rearrange("p (a n) -> p a n", a=8),
                              vecs[:, V_FFN + 8 * q:V_FFN + 8 * q + 8].unsqueeze(2).broadcast_to([P, 8, CAP]), ALU.mult)
                ins.then_inc(xgT_ready, 1)

            def round_dve(R):
                g0 = R * (NE + 1)
                if not is_first(R):
                    dve.wait_ge(list_done, g0)
                    TS(rankm, rankm, -float(CAP), None, ALU.add).then_inc(lists_ready, 1)
                    dve.wait_ge(lists_ready, R + 1)
                    dve.wait_ge(rows_free, R * NE + 2)
                places(0)
                indices(g0, 0)
                destinations(0)
                rows_in(g0, 0)
                with dve.Fori(0, NE // 2) as i:
                    for b in range(2):
                        x = i * 2 + (R * NE + b)
                        g = i * 2 + (R * (NE + 1) + b + 1)
                        dve.wait_ge(list_done, g)
                        places(i * 2 + (b + 1))
                        indices(g, 1 - b)
                        dve.wait_ge(act_ready, x + 1)
                        STT(hh[0:CAP, :], sg[0:CAP, :], gcol[b][:, 0:1], up[0:CAP, :], ALU.mult, ALU.mult).then_inc(h_made, 1)
                        dve.wait_ge(rows_free, x + 2)
                        destinations(1 - b)
                        dve.wait_ge(hT_done, x + 1)
                        nc.vector.tensor_copy(hT, PB[6][:, 0:KF * CAP].rearrange("p (a n) -> p a n", a=KF)).then_inc(hT_ready, 1)
                        rows_in(g, 1 - b)

            run_rounds(dve, round_dve)
            dve.wait_ge(moe_done, 1)
            dve.wait_ge(gfin_loaded, 16)
            cols = slice(0, V_COLS)

            def add_rows(tile):
                n = TT[tile]
                dve.wait_ge(yrow_loaded[tile], 32)
                xt = x1[0:n, tile, cols]
                step.link(TTo(xt, xt, yrow[2 * tile][0:n, cols], ALU.add))
                TTo(xt, xt, yrow[2 * tile + 1][0:n, cols], ALU.add).then_inc(ysum_done, 1)

            def norm_rows(i, tile):
                n = TT[tile]
                dve.wait_ge(f_rms, i + 1)
                r = token_stats[0:n, 3 + tile:4 + tile]
                nc.vector.reciprocal(r, token_stats[0:n, tile:tile + 1]).then_inc(rstd_last, 1)
                dve.wait_ge(rstd_last, i + 1)
                xt = x1[0:n, tile, cols]
                STT(xt, xt, r, gfin[0:n, cols], ALU.mult, ALU.mult).then_inc(out_ready, 1)

            add_rows(TILE_ORDER[0])
            add_rows(TILE_ORDER[1])
            norm_rows(0, TILE_ORDER[0])
            add_rows(TILE_ORDER[2])
            norm_rows(1, TILE_ORDER[1])
            norm_rows(2, TILE_ORDER[2])


_INS = ['x_prompt', 'x_sample', 'state_s5_re', 'state_s5_im', 'state_hgrn', 'meta_tokens', 'norm_mix', 'w_in',
        's5_A_re', 's5_A_im', 's5_log_step', 's5_B_re', 's5_B_im', 's5_C_re', 's5_C_im', 's5_D', 's5_w_glu',
        's5_b_glu', 's5_out_gain', 'hg_lb_logits', 'hg_out_gain', 'w_out', 'norm_ffn', 'w_coarse', 'b_coarse',
        'w_fine', 'b_fine', 'w_gate', 'w_up', 'w_down', 'norm_final']
_OUTS = ['y_prompt', 'y_sample', 's5_re_prompt', 's5_im_prompt', 'hgrn_prompt', 's5_re_sample', 's5_im_sample',
         'hgrn_sample']


def kernel(**inputs):
    import numpy as _np
    import concourse.bacc as _bacc
    from concourse import mybir as _mybir
    from concourse.bass_utils import run_bass_kernel_spmd as _run

    nc = _bacc.Bacc("TRN2", target_bir_lowering=False, num_devices=1)
    arrays, args = {}, {}
    for name in _INS:
        a = _np.ascontiguousarray(inputs[name])
        arrays[f"in_{name}_dram"] = a
        args[name] = nc.dram_tensor(f"in_{name}_dram", a.shape, _mybir.dt.from_np(a.dtype), kind="ExternalInput").ap()
    g5, p5 = inputs["s5_A_re"].shape[1:]
    nh, dk, dv = inputs["state_hgrn"].shape[2:]
    ns = inputs["x_sample"].shape[0]
    shapes = [inputs["x_prompt"].shape, inputs["x_sample"].shape, (1, 1, g5, p5), (1, 1, g5, p5),
              (1, 1, nh, dk, dv), (1, ns, g5, p5), (1, ns, g5, p5), (1, ns, nh, dk, dv)]
    for name, shape in zip(_OUTS, shapes):
        args[name] = nc.dram_tensor(f"out_{name}_dram", shape, _mybir.dt.float32, kind="ExternalOutput").ap()
    hymba_step(nc, args)
    r = _run(nc, [arrays], core_ids=[0])
    return tuple(r.results[0][f"out_{name}_dram"] for name in _OUTS)
```
